# Optimizing a Trainium2 kernel written in Bass

```python
import math
import jax
import jax.numpy as jnp
from jax import lax
import numpy as np
import jax, jax.numpy as jnp

D_MODEL = 2048
BATCH = 1
SEQ = 256
DEPTH = 2

N_A_LAYERS = DEPTH // 2
N_B_LAYERS = DEPTH - N_A_LAYERS
SSM_GROUP = 16
SSM_GROUPS = D_MODEL // SSM_GROUP
SSM_STATE = 64
SCAN_CHUNK = 128
HEAD_DIM = 128
N_HEADS = D_MODEL // HEAD_DIM
DILATION_CFG = ((128, 1), (512, 4), (2048, 16))
N_GROUPS = len(DILATION_CFG)
ATTN_BLOCK = 128
D_FF = -(-8 * D_MODEL // (3 * 256)) * 256
EPS = 1e-6


def rmsnorm(x, g):
    xf = x.astype(jnp.float32)
    y = xf * lax.rsqrt(jnp.mean(xf * xf, axis=-1, keepdims=True) + EPS) * g.astype(jnp.float32)
    return y.astype(x.dtype)

def swiglu_ffn(h, w_gate_up, w_down):
    gate, up = jnp.split(h @ w_gate_up, 2, axis=-1)
    return (jax.nn.silu(gate) * up) @ w_down

def _complex_scan_combine(e1, e2):
    a1r, a1i, b1r, b1i = e1
    a2r, a2i, b2r, b2i = e2
    ar = a2r * a1r - a2i * a1i
    ai = a2r * a1i + a2i * a1r
    br = a2r * b1r - a2i * b1i + b2r
    bi = a2r * b1i + a2i * b1r + b2i
    return (ar, ai, br, bi)

def s5_mixer(u, a_re, a_im, log_dt, b_re, b_im, c_re, c_im, d_skip, w_glu):
    bsz, seqlen, _ = u.shape
    f32 = jnp.float32
    lam_re = jnp.minimum(a_re.astype(f32), -1e-4)
    lam_im = a_im.astype(f32)
    dt = jnp.exp(log_dt.astype(f32))[:, None]
    mag = jnp.exp(lam_re * dt)
    ang = lam_im * dt
    lb_re = mag * jnp.cos(ang)
    lb_im = mag * jnp.sin(ang)
    den = lam_re * lam_re + lam_im * lam_im
    nr = lb_re - 1.0
    ni = lb_im
    coef_re = (nr * lam_re + ni * lam_im) / den
    coef_im = (ni * lam_re - nr * lam_im) / den
    br = b_re.astype(f32)
    bi = b_im.astype(f32)
    bb_re = coef_re[..., None] * br - coef_im[..., None] * bi
    bb_im = coef_re[..., None] * bi + coef_im[..., None] * br
    cr = c_re.astype(f32)
    ci = c_im.astype(f32)
    a_shape = (bsz, SCAN_CHUNK, SSM_GROUPS, SSM_STATE)
    a_el_re = jnp.broadcast_to(lb_re, a_shape)
    a_el_im = jnp.broadcast_to(lb_im, a_shape)

    uf = u.astype(f32)
    n_chunks = seqlen // SCAN_CHUNK
    u_chunks = uf.reshape(bsz, n_chunks, SCAN_CHUNK, SSM_GROUPS, SSM_GROUP).transpose(1, 0, 2, 3, 4)

    def step(carry, u_c):
        h_re, h_im = carry
        bu_re = jnp.einsum('blgh,gph->blgp', u_c, bb_re)
        bu_im = jnp.einsum('blgh,gph->blgp', u_c, bb_im)
        ar, ai, sr, si = lax.associative_scan(_complex_scan_combine, (a_el_re, a_el_im, bu_re, bu_im), axis=1)
        st_re = ar * h_re[:, None] - ai * h_im[:, None] + sr
        st_im = ar * h_im[:, None] + ai * h_re[:, None] + si
        y = jnp.einsum('blgp,ghp->blgh', st_re, cr) - jnp.einsum('blgp,ghp->blgh', st_im, ci)
        return (st_re[:, -1], st_im[:, -1]), y

    h0 = (jnp.zeros((bsz, SSM_GROUPS, SSM_STATE), f32), jnp.zeros((bsz, SSM_GROUPS, SSM_STATE), f32))
    _, y = lax.scan(step, h0, u_chunks)
    y = y.transpose(1, 0, 2, 3, 4).reshape(bsz, seqlen, D_MODEL) + d_skip.astype(f32) * uf
    g = jax.nn.gelu(y).astype(u.dtype)
    val, gate = jnp.split(g @ w_glu, 2, axis=-1)
    return (val.astype(f32) * jax.nn.sigmoid(gate.astype(f32))).astype(u.dtype)

def alibi_slopes():
    n = N_GROUPS * N_HEADS
    i = jnp.arange(1, n + 1, dtype=jnp.float32)
    s = jnp.exp2(-8.0 * i / n)
    return s.reshape(N_HEADS, N_GROUPS).T

def head_rmsnorm(t, g):
    tf = t.astype(jnp.float32)
    y = tf * lax.rsqrt(jnp.mean(tf * tf, axis=-1, keepdims=True) + EPS) * g.astype(jnp.float32)
    return y.astype(t.dtype)

def shared_kv(x, kv_norm, w_kv, k_norm):
    bsz, seqlen, _ = x.shape
    kv = (rmsnorm(x, kv_norm) @ w_kv).reshape(bsz, seqlen, 2, N_HEADS, HEAD_DIM)
    k = head_rmsnorm(kv[:, :, 0], k_norm)
    v = kv[:, :, 1]
    return k, v

def dilated_window_group(q, k, v, window, dilation, slopes):
    bsz, seqlen, nh, dh = q.shape
    span = dilation * ATTN_BLOCK
    lp = -(-seqlen // span) * span
    pad = lp - seqlen
    n_sub = lp // dilation
    nb = n_sub // ATTN_BLOCK
    w_sub = window // dilation

    def to_blocks(t):
        t = jnp.pad(t, ((0, 0), (0, pad), (0, 0), (0, 0)))
        t = t.reshape(bsz, n_sub, dilation, nh, dh).transpose(0, 2, 1, 3, 4)
        return t.reshape(bsz, dilation, nb, ATTN_BLOCK, nh, dh)

    def with_prev(t):
        prev = jnp.pad(t[:, :, :-1], ((0, 0), (0, 0), (1, 0), (0, 0), (0, 0), (0, 0)))
        return jnp.concatenate([prev, t], axis=3)

    qb = to_blocks(q)
    kk = with_prev(to_blocks(k))
    vv = with_prev(to_blocks(v))
    s = jnp.einsum('bdnqhe,bdnkhe->bdnhqk', qb, kk, preferred_element_type=jnp.float32) * (dh ** -0.5)
    qi = jnp.arange(ATTN_BLOCK)[:, None] + ATTN_BLOCK
    kj = jnp.arange(2 * ATTN_BLOCK)[None, :]
    dist = qi - kj
    valid = (dist >= 0) & (dist <= w_sub)
    valid = valid[None] & ((jnp.arange(nb)[:, None, None] > 0) | (kj >= ATTN_BLOCK)[None])
    bias = -slopes[:, None, None] * (dilation * dist).astype(jnp.float32)[None]
    s = jnp.where(valid[:, None], s + bias, -jnp.inf)
    lse = jax.nn.logsumexp(s, axis=-1)
    p = jnp.exp(s - lse[..., None])
    o = jnp.einsum('bdnhqk,bdnkhe->bdnqhe', p.astype(v.dtype), vv, preferred_element_type=jnp.float32)
    o = o.reshape(bsz, dilation, n_sub, nh, dh).transpose(0, 2, 1, 3, 4).reshape(bsz, lp, nh, dh)[:, :seqlen]
    lse = lse.transpose(0, 1, 2, 4, 3).reshape(bsz, dilation, n_sub, nh)
    lse = lse.transpose(0, 2, 1, 3).reshape(bsz, lp, nh)[:, :seqlen]
    return o, lse

def dilated_attention(h, k, v, q_norm_l, w_q_l, w_o_l):
    bsz, seqlen, _ = h.shape
    q = (h @ w_q_l).reshape(bsz, seqlen, N_GROUPS, N_HEADS, HEAD_DIM)
    q = head_rmsnorm(q, q_norm_l[:, None, :])
    slopes = alibi_slopes()
    outs = []
    lses = []
    for g, (win, dil) in enumerate(DILATION_CFG):
        o, lse = dilated_window_group(q[:, :, g], k, v, win, dil, slopes[g])
        outs.append(o)
        lses.append(lse)
    wts = jax.nn.softmax(jnp.stack(lses, axis=0), axis=0)
    merged = jnp.sum(wts[..., None] * jnp.stack(outs, axis=0), axis=0)
    return merged.reshape(bsz, seqlen, N_HEADS * HEAD_DIM).astype(h.dtype) @ w_o_l

def first_inputs(seed: int = 0) -> dict:
    key = jax.random.key(seed)
    ks = jax.random.split(key, 24)
    f32 = jnp.float32
    d = D_MODEL
    qkv_w = N_HEADS * HEAD_DIM
    nrm = lambda k, shape, scale: jax.random.normal(k, shape, f32) * scale
    n_idx = jnp.arange(SSM_STATE, dtype=f32)
    x = jax.random.normal(ks[0], (BATCH, SEQ, d), f32)
    mix_norm = 1.0 + nrm(ks[1], (DEPTH, d), 0.02)
    ffn_norm = 1.0 + nrm(ks[2], (DEPTH, d), 0.02)
    ssm_a_re = -0.5 + nrm(ks[3], (N_A_LAYERS, SSM_GROUPS, SSM_STATE), 0.01)
    ssm_a_im = math.pi * n_idx + nrm(ks[4], (N_A_LAYERS, SSM_GROUPS, SSM_STATE), 0.01)
    ssm_log_dt = jax.random.uniform(ks[5], (N_A_LAYERS, SSM_GROUPS), f32, math.log(1e-3), math.log(1e-1))
    ssm_b_re = nrm(ks[6], (N_A_LAYERS, SSM_GROUPS, SSM_STATE, SSM_GROUP), SSM_GROUP ** -0.5)
    ssm_b_im = nrm(ks[7], (N_A_LAYERS, SSM_GROUPS, SSM_STATE, SSM_GROUP), SSM_GROUP ** -0.5)
    ssm_c_re = nrm(ks[8], (N_A_LAYERS, SSM_GROUPS, SSM_GROUP, SSM_STATE), SSM_STATE ** -0.5)
    ssm_c_im = nrm(ks[9], (N_A_LAYERS, SSM_GROUPS, SSM_GROUP, SSM_STATE), SSM_STATE ** -0.5)
    ssm_d = nrm(ks[10], (N_A_LAYERS, d), 1.0)
    w_glu = nrm(ks[11], (N_A_LAYERS, d, 2 * d), d ** -0.5)
    kv_norm = 1.0 + nrm(ks[12], (d,), 0.02)
    w_kv = nrm(ks[13], (d, 2 * qkv_w), d ** -0.5)
    k_norm = 1.0 + nrm(ks[14], (HEAD_DIM,), 0.02)
    w_q = nrm(ks[15], (N_B_LAYERS, d, N_GROUPS * qkv_w), d ** -0.5)
    q_norm = 1.0 + nrm(ks[16], (N_B_LAYERS, N_GROUPS, HEAD_DIM), 0.02)
    w_o = nrm(ks[17], (N_B_LAYERS, qkv_w, d), qkv_w ** -0.5)
    w_gate_up = nrm(ks[18], (DEPTH, d, 2 * D_FF), d ** -0.5)
    w_down = nrm(ks[19], (DEPTH, D_FF, d), D_FF ** -0.5)
    return {'x': x, 'mix_norm': mix_norm, 'ffn_norm': ffn_norm,
            'ssm_a_re': ssm_a_re, 'ssm_a_im': ssm_a_im, 'ssm_log_dt': ssm_log_dt,
            'ssm_b_re': ssm_b_re, 'ssm_b_im': ssm_b_im, 'ssm_c_re': ssm_c_re, 'ssm_c_im': ssm_c_im,
            'ssm_d': ssm_d, 'w_glu': w_glu, 'kv_norm': kv_norm, 'w_kv': w_kv, 'k_norm': k_norm,
            'w_q': w_q, 'q_norm': q_norm, 'w_o': w_o, 'w_gate_up': w_gate_up, 'w_down': w_down}

def first_block(x, mix_norm, ffn_norm, ssm_a_re, ssm_a_im, ssm_log_dt, ssm_b_re, ssm_b_im, ssm_c_re, ssm_c_im,
              ssm_d, w_glu, kv_norm, w_kv, k_norm, w_q, q_norm, w_o, w_gate_up, w_down):
    k = None
    v = None
    for layer in range(DEPTH):
        h = rmsnorm(x, mix_norm[layer])
        if layer < N_A_LAYERS:
            i = layer
            x = x + s5_mixer(h, ssm_a_re[i], ssm_a_im[i], ssm_log_dt[i], ssm_b_re[i], ssm_b_im[i],
                             ssm_c_re[i], ssm_c_im[i], ssm_d[i], w_glu[i])
        else:
            if layer == N_A_LAYERS:
                k, v = shared_kv(x, kv_norm, w_kv, k_norm)
            j = layer - N_A_LAYERS
            x = x + dilated_attention(h, k, v, q_norm[j], w_q[j], w_o[j])
        x = x + swiglu_ffn(rmsnorm(x, ffn_norm[layer]), w_gate_up[layer], w_down[layer])
    return x


RET_HEADS = 6
RET_W = RET_HEADS * HEAD_DIM
RET_CHUNK = 128
DIFF_HEADS = 4
DIFF_QK = HEAD_DIM // 2
DIFF_W = DIFF_HEADS * HEAD_DIM
Q_BLOCK = 128
LRU_W = 768
LRU_BLOCKS = 8
LRU_BW = LRU_W // LRU_BLOCKS
CONV_W = 4
LRU_C = 8.0
D_MIX = RET_W + DIFF_W + LRU_W
SPLIT_SIZES = (RET_W, RET_W, RET_W, RET_W,
               DIFF_W, DIFF_W, DIFF_W, DIFF_W,
               LRU_W, LRU_W)
D_IN = sum(SPLIT_SIZES)
ROPE_THETA = 10000.0


def rms_norm(x, g=None):
    x32 = x.astype(jnp.float32)
    y = x32 * lax.rsqrt(jnp.mean(x32 * x32, axis=-1, keepdims=True) + EPS)
    if g is not None:
        y = y * g.astype(jnp.float32)
    return y.astype(x.dtype)

def rope(x, positions, inv_freq):
    ang = positions.astype(jnp.float32)[..., None] * inv_freq
    cos = jnp.cos(ang)[:, :, None, :].astype(x.dtype)
    sin = jnp.sin(ang)[:, :, None, :].astype(x.dtype)
    x1, x2 = jnp.split(x, 2, axis=-1)
    return jnp.concatenate([x1 * cos - x2 * sin, x2 * cos + x1 * sin], axis=-1)

def retention(q, k, v, positions):
    B, S, H, D = q.shape
    dt = q.dtype
    inv = 1.0 / (ROPE_THETA ** jnp.linspace(0.0, 1.0, D // 2, dtype=jnp.float32))
    q = rope(q, positions, inv)
    k = rope(k, positions, inv) * (D ** -0.5)
    log_g = jnp.log1p(-jnp.power(2.0, -5.0 - jnp.arange(H, dtype=jnp.float32)))
    C = RET_CHUNK
    N = S // C
    idx = jnp.arange(C, dtype=jnp.float32)
    rel = idx[:, None] - idx[None, :]
    intra_decay = jnp.where(rel[None] >= 0,
                            jnp.exp(jnp.maximum(rel, 0.0)[None] * log_g[:, None, None]),
                            0.0).astype(dt)
    qc = q.reshape(B, N, C, H, D)
    kc = k.reshape(B, N, C, H, D)
    vc = v.reshape(B, N, C, H, D)
    scores = jnp.einsum('bnihd,bnjhd->bnhij', qc, kc) * intra_decay
    o_intra = jnp.einsum('bnhij,bnjhe->bnihe', scores, vc)
    k_w = jnp.exp((C - 1.0 - idx)[:, None] * log_g[None, :]).astype(dt)
    kv = jnp.einsum('bnjhd,bnjhe->nbhde', kc * k_w[:, :, None], vc)
    chunk_decay = jnp.exp(C * log_g)[None, :, None, None].astype(kv.dtype)

    def step(state, kv_n):
        return state * chunk_decay + kv_n, state

    _, s_prev = lax.scan(step, jnp.zeros_like(kv[0]), kv)
    q_w = jnp.exp((idx + 1.0)[:, None] * log_g[None, :]).astype(dt)
    o_cross = jnp.einsum('bnihd,nbhde->bnihe', qc * q_w[:, :, None], s_prev)
    return (o_intra + o_cross).reshape(B, S, H, D)

def diff_attention(q, k, v, positions, lam):
    B, S, H, _, DQ = q.shape
    inv = 1.0 / (ROPE_THETA ** (jnp.arange(0, DQ, 2, dtype=jnp.float32) / DQ))
    q = rope(q.reshape(B, S, H * 2, DQ), positions, inv).reshape(B, S, H, 2, DQ) * (DQ ** -0.5)
    k = rope(k.reshape(B, S, H * 2, DQ), positions, inv).reshape(B, S, H, 2, DQ)
    kpos = jnp.arange(S)

    def block(i):
        qb = lax.dynamic_slice_in_dim(q, i * Q_BLOCK, Q_BLOCK, axis=1)
        s = jnp.einsum('bqhcd,bkhcd->bhcqk', qb, k).astype(jnp.float32)
        qpos = i * Q_BLOCK + jnp.arange(Q_BLOCK)
        s = jnp.where(kpos[None, :] <= qpos[:, None], s, -jnp.inf)
        p = jax.nn.softmax(s, axis=-1)
        w = p[:, :, 0] - lam * p[:, :, 1]
        return jnp.einsum('bhqk,bkhe->bqhe', w.astype(v.dtype), v)

    o = lax.map(block, jnp.arange(S // Q_BLOCK))
    return jnp.transpose(o, (1, 0, 2, 3, 4)).reshape(B, S, H, v.shape[-1])

def rg_lru(x, conv_w, conv_b, wa, ba, wx, bx, lam):
    B, S, W = x.shape
    xp = jnp.pad(x, ((0, 0), (CONV_W - 1, 0), (0, 0)))
    xc = conv_b + xp[:, 0:S] * conv_w[0]
    for j in range(1, CONV_W):
        xc = xc + xp[:, j:j + S] * conv_w[j]
    xb = xc.reshape(B, S, LRU_BLOCKS, LRU_BW)
    r = jax.nn.sigmoid(jnp.einsum('bsnk,nkj->bsnj', xb, wa).reshape(B, S, W) + ba)
    i = jax.nn.sigmoid(jnp.einsum('bsnk,nkj->bsnj', xb, wx).reshape(B, S, W) + bx)
    log_a = (LRU_C * r.astype(jnp.float32)) * jax.nn.log_sigmoid(lam.astype(jnp.float32))
    a = jnp.exp(log_a)
    mult = jnp.sqrt(-jnp.expm1(2.0 * log_a))
    b = mult * (i * xc).astype(jnp.float32)

    def combine(left, right):
        a1, b1 = left
        a2, b2 = right
        return a1 * a2, a2 * b1 + b2

    _, h = lax.associative_scan(combine, (a, b), axis=1)
    return h.astype(x.dtype)

def second_inputs(seed: int = 0) -> dict:
    key = jax.random.key(seed)
    ks = jax.random.split(key, 20)
    f32 = jnp.float32
    x = jax.random.normal(ks[0], (BATCH, SEQ, D_MODEL), f32)
    positions = jnp.broadcast_to(jnp.arange(SEQ, dtype=jnp.int32), (BATCH, SEQ))
    pre_norm_g = 1.0 + 0.05 * jax.random.normal(ks[1], (DEPTH, D_MODEL), f32)
    w_in = jax.random.normal(ks[2], (DEPTH, D_MODEL, D_IN), f32) * (D_MODEL ** -0.5)
    diff_lambda_q1 = 0.1 * jax.random.normal(ks[3], (DEPTH, DIFF_QK), f32)
    diff_lambda_k1 = 0.1 * jax.random.normal(ks[4], (DEPTH, DIFF_QK), f32)
    diff_lambda_q2 = 0.1 * jax.random.normal(ks[5], (DEPTH, DIFF_QK), f32)
    diff_lambda_k2 = 0.1 * jax.random.normal(ks[6], (DEPTH, DIFF_QK), f32)
    diff_subln_g = 1.0 + 0.05 * jax.random.normal(ks[7], (DEPTH, HEAD_DIM), f32)
    lru_conv_w = jax.random.normal(ks[8], (DEPTH, CONV_W, LRU_W), f32) * (CONV_W ** -0.5)
    lru_conv_b = 0.01 * jax.random.normal(ks[9], (DEPTH, LRU_W), f32)
    lru_wa = jax.random.normal(ks[10], (DEPTH, LRU_BLOCKS, LRU_BW, LRU_BW), f32) * (LRU_BW ** -0.5)
    lru_ba = 0.01 * jax.random.normal(ks[11], (DEPTH, LRU_W), f32)
    lru_wx = jax.random.normal(ks[12], (DEPTH, LRU_BLOCKS, LRU_BW, LRU_BW), f32) * (LRU_BW ** -0.5)
    lru_bx = 0.01 * jax.random.normal(ks[13], (DEPTH, LRU_W), f32)
    u = jax.random.uniform(ks[14], (DEPTH, LRU_W), f32, minval=0.9, maxval=0.999)
    s = u ** (1.0 / LRU_C)
    lru_lambda = jnp.log(s) - jnp.log1p(-s)
    w_out = jax.random.normal(ks[15], (DEPTH, D_MIX, D_MODEL), f32) * (D_MIX ** -0.5)
    post_norm_g = 1.0 + 0.05 * jax.random.normal(ks[16], (DEPTH, D_MODEL), f32)
    return {"x": x, "positions": positions, "pre_norm_g": pre_norm_g, "w_in": w_in,
            "diff_lambda_q1": diff_lambda_q1, "diff_lambda_k1": diff_lambda_k1,
            "diff_lambda_q2": diff_lambda_q2, "diff_lambda_k2": diff_lambda_k2,
            "diff_subln_g": diff_subln_g, "lru_conv_w": lru_conv_w, "lru_conv_b": lru_conv_b,
            "lru_wa": lru_wa, "lru_ba": lru_ba, "lru_wx": lru_wx, "lru_bx": lru_bx,
            "lru_lambda": lru_lambda, "w_out": w_out, "post_norm_g": post_norm_g}

def second_block(x, positions, pre_norm_g, w_in, diff_lambda_q1, diff_lambda_k1,
              diff_lambda_q2, diff_lambda_k2, diff_subln_g, lru_conv_w, lru_conv_b,
              lru_wa, lru_ba, lru_wx, lru_bx, lru_lambda, w_out, post_norm_g):
    B, S, _ = x.shape
    split_idx = [int(v) for v in np.cumsum(SPLIT_SIZES)[:-1]]
    for l in range(DEPTH):
        h = rms_norm(x, pre_norm_g[l])
        proj = jnp.einsum('bsd,de->bse', h, w_in[l])
        (rq, rk, rv, rg, dq, dk, dv, dg, lx, lg) = jnp.split(proj, split_idx, axis=-1)

        ro = retention(rq.reshape(B, S, RET_HEADS, HEAD_DIM),
                       rk.reshape(B, S, RET_HEADS, HEAD_DIM),
                       rv.reshape(B, S, RET_HEADS, HEAD_DIM), positions)
        ret_out = rms_norm(ro).reshape(B, S, RET_W) * jax.nn.silu(rg)

        lam_init = 0.8 - 0.6 * math.exp(-0.3 * l)
        lam = (jnp.exp(jnp.sum(diff_lambda_q1[l] * diff_lambda_k1[l]).astype(jnp.float32))
               - jnp.exp(jnp.sum(diff_lambda_q2[l] * diff_lambda_k2[l]).astype(jnp.float32))
               + lam_init)
        do = diff_attention(dq.reshape(B, S, DIFF_HEADS, 2, DIFF_QK),
                            dk.reshape(B, S, DIFF_HEADS, 2, DIFF_QK),
                            dv.reshape(B, S, DIFF_HEADS, HEAD_DIM), positions, lam)
        diff_out = (rms_norm(do, diff_subln_g[l]) * (1.0 - lam_init)).reshape(B, S, DIFF_W) * jax.nn.silu(dg)

        lru_out = rg_lru(lx, lru_conv_w[l], lru_conv_b[l], lru_wa[l], lru_ba[l],
                         lru_wx[l], lru_bx[l], lru_lambda[l]) * jax.nn.silu(lg)

        mixed = jnp.concatenate([ret_out, diff_out, lru_out], axis=-1)
        y = jnp.einsum('bse,ed->bsd', mixed, w_out[l])
        x = x + rms_norm(y, post_norm_g[l])
    return x


def setup_inputs(seed=0):
    out = dict(first_inputs(seed))
    for name, value in second_inputs(seed + 1).items():
        if name != "x":
            out[name + "_2"] = value
    return out


def reference(
    x, mix_norm, ffn_norm, ssm_a_re, ssm_a_im, ssm_log_dt, ssm_b_re, ssm_b_im, ssm_c_re,
    ssm_c_im, ssm_d, w_glu, kv_norm, w_kv, k_norm, w_q, q_norm, w_o, w_gate_up, w_down,
    positions_2, pre_norm_g_2, w_in_2, diff_lambda_q1_2, diff_lambda_k1_2, diff_lambda_q2_2,
    diff_lambda_k2_2, diff_subln_g_2, lru_conv_w_2, lru_conv_b_2, lru_wa_2, lru_ba_2, lru_wx_2,
    lru_bx_2, lru_lambda_2, w_out_2, post_norm_g_2,
):
    x = first_block(
        x, mix_norm, ffn_norm, ssm_a_re, ssm_a_im, ssm_log_dt, ssm_b_re, ssm_b_im, ssm_c_re,
        ssm_c_im, ssm_d, w_glu, kv_norm, w_kv, k_norm, w_q, q_norm, w_o, w_gate_up, w_down,
    )
    return second_block(
        x, positions_2, pre_norm_g_2, w_in_2, diff_lambda_q1_2, diff_lambda_k1_2,
        diff_lambda_q2_2, diff_lambda_k2_2, diff_subln_g_2, lru_conv_w_2, lru_conv_b_2,
        lru_wa_2, lru_ba_2, lru_wx_2, lru_bx_2, lru_lambda_2, w_out_2, post_norm_g_2,
    )


_drawn_inputs = setup_inputs


def setup_inputs(seed=0):
    import zlib

    import numpy as np

    out = dict(_drawn_inputs(seed))
    spreads = {}
    factors = {'mix_norm': 2.716,
     'ssm_a_re': 200.0,
     'kv_norm': 3.837,
     'k_norm': 8.0,
     'q_norm': 8.0,
     'diff_lambda_k1_2': 3.469,
     'diff_subln_g_2': 15.852,
     'lru_ba_2': 200.0,
     'lru_bx_2': 64.0,
     'lru_conv_b_2': 8.0,
     'lru_wa_2': 2.698,
     'post_norm_g_2': 3.33}
    for name, (base, spread) in spreads.items():
        noise = np.random.default_rng([zlib.crc32(name.encode()), seed]).standard_normal(out[name].shape)
        drawn = base * np.exp(spread * noise) if base else spread * noise
        out[name] = jnp.asarray(drawn.astype(out[name].dtype))
    for name, factor in factors.items():
        out[name] = (out[name] * factor).astype(out[name].dtype)
    return out
```

```python
import math
from contextlib import ExitStack

import numpy as np

import concourse.bass as bass
from concourse import mybir

F32 = mybir.dt.float32
F32R = mybir.dt.float32r
BF16 = mybir.dt.bfloat16
I32 = mybir.dt.int32
ALU = mybir.AluOpType
ACT = mybir.ActivationFunctionType
AX = mybir.AxisListType

P = 128
T = 256
TB = T // P
D = 2048
KT = D // P
DFF = 5632
EPS = 1e-6
PANEL = 512
CK = 2
RAW = 8
AHEAD = 6
SPLIT = 2
HEADS, DH = 16, 128
NG = 3
RH, DIFH = 6, 4
RW, DW, LW = RH * DH, DIFH * DH, 768
LB, LBW = 8, 96
DIN = 4 * RW + 4 * DW + 2 * LW
C_RQ, C_RK, C_RV, C_RG = 0, RW, 2 * RW, 3 * RW
C_DQ, C_DK, C_DV, C_DG = 4 * RW, 4 * RW + DW, 4 * RW + 2 * DW, 4 * RW + 3 * DW
C_LX, C_LG = 4 * RW + 4 * DW, 4 * RW + 4 * DW + LW
NLAYER2 = 2
BIG = 1.0e30
MAGIC = 12582912.0
TWO_PI_BELOW = 6.2831850
C1 = 6.28125
C2 = float(np.float32(round((2 * math.pi - C1) * 2**21) / 2**21))
C3 = 2 * math.pi - C1 - C2
KB = 1024


class Gemm:

    def __init__(self, name, w, chunks, panels, cols, chunk0, panel0, slot_uses):
        self.name, self.w, self.chunks, self.panels, self.cols = name, w, chunks, panels, cols
        self.chunk0, self.panel0, self.slot_uses = chunk0, panel0, list(slot_uses)
        self.first = int(name == "glu")
        self.per = [chunks // RAW + (s < chunks % RAW) for s in range(RAW)]

    def chunk(self, q, k):
        return q * self.chunks + (self.chunk0 + k)

    def raw_count(self, q, k):
        s = k % RAW
        return q * (16 * self.per[s]) + 16 * (self.slot_uses[s] + k // RAW + 1)

    def done(self, q):
        return (q + 1) * self.chunks + (self.chunk0 + SPLIT)

    def evacuated(self, q):
        return q + (self.panel0 + 3)

    @property
    def all_evacuated(self):
        return self.panel0 + self.panels + 2


def plan(w):
    plain = lambda i, j: i * (2 * PANEL) + j * PANEL
    table = [
        ("glu", w["w_glu"][0], D, 8, lambda i, j: i * PANEL + ((1 - j) * D - PANEL)),
        ("gu0", w["w_gate_up"][0], D, 22, lambda i, j: i * PANEL + j * DFF),
        ("dn0", w["w_down"][0], DFF, 4, plain),
        ("k", w["w_kv"], D, 4, plain),
        ("v", w["w_kv"], D, 4, lambda i, j: i * (2 * PANEL) + (j * PANEL + D)),
        ("q", w["w_q"][0], D, 12, plain),
        ("o", w["w_o"][0], D, 4, plain),
        ("gu1", w["w_gate_up"][1], D, 22, lambda i, j: i * PANEL + j * DFF),
        ("dn1", w["w_down"][1], DFF, 4, plain),
    ]
    for l in range(NLAYER2):
        table += [(f"in{l}", w["w_in_2"][l], D, 13, plain), (f"out{l}", w["w_out_2"][l], D, 4, plain)]
    gemms, chunk0, panel0, uses = {}, 0, 0, [0] * RAW
    for name, ap, k, panels, cols in table:
        g = Gemm(name, ap, k // (P * CK), panels, cols, chunk0, panel0, uses)
        gemms[name] = g
        chunk0 += g.chunks * panels
        panel0 += panels
        uses = [u + n * panels for u, n in zip(uses, g.per)]
    return gemms


def heads_in_turn(eng, a, b, last=None):
    last = last or (lambda h, j: None)
    a(0, 0)
    a(1, 1)
    b(0, 0)
    with eng.Fori(0, HEADS // 2 - 1) as n:
        for j in range(2):
            a(n * 2 + (j + 2), j)
            b(n * 2 + (j + 1), 1 - j)
            last(n * 2 + j, j)
    b(HEADS - 1, 1)
    last(HEADS - 2, 0)
    last(HEADS - 1, 1)


class Links:

    def __init__(self, eng, sem):
        self.eng, self.sem, self.n = eng, sem, 0

    def link(self, instruction):
        self.n += 1
        instruction.then_inc(self.sem, 1)
        self.eng.wait_ge(self.sem, self.n)


GAINS = ["mix0", "ffn0", "kv", "mix1", "ffn1", "pre0", "pre1", "skip"]
TURNS = ["mix0", "ffn0", "kv", "mix1", "ffn1", "pre0", None, "pre1", None]
T_MIX0, T_FFN0, T_KV, T_MIX1, T_FFN1 = range(5)
T_PRE, T_OUT = (5, 7), (6, 8)
N_MIX0, N_FFN0, N_KV, N_FFN1 = range(4)
N_PRE = (4, 5)


def program(nc, w, c, out):
    G = plan(w)
    with ExitStack() as ctx:
        def sb(name, shape, dt=F32):
            return ctx.enter_context(nc.sbuf_tensor(name, shape, dt))

        def sem(name):
            return ctx.enter_context(nc.semaphore(name))

        x = sb("x_res", [P, TB, D])
        raw = sb("raw", [P, RAW, CK, PANEL])
        whi = sb("w_hi", [P, SPLIT, CK, PANEL], F32R)
        wlo = sb("w_lo", [P, SPLIT, CK, PANEL], F32R)
        ident = sb("ident", [P, P])
        gains = sb("gains", [P, len(GAINS), KT])
        half_pi = sb("half_pi", [P, 1])
        ssq = sb("ssq", [P, TB])
        msq = sb("msq", [P, TB])
        sdev = sb("sdev", [P, TB])
        rstd = sb("rstd", [P, TB])
        ps = ctx.enter_context(nc.psum_tensor("ps", [P, 8, 512], F32))

        def at(kb, name, shape, dt=F32):
            with ExitStack() as scope:
                if kb:
                    scope.enter_context(nc.sbuf_tensor(f"before_{name}", [P, int(kb * KB // 4)], F32))
                return scope.enter_context(nc.sbuf_tensor(name, shape, dt))

        xh = at(0, "x_hi", [P, KT, T], F32R)
        xl = at(16, "x_lo", [P, KT, T], F32R)
        gbuf = at(32, "gbuf", [P, TB, PANEL])
        hbuf = at(36, "hbuf", [P, TB, PANEL])
        junk = at(32, "junk", [P, D], BF16)
        tok = at(40, "tok", [P, TB, D])
        hh = at(40, "h_hi", [P, DFF // P, T], F32R)
        hl = at(84, "h_lo", [P, DFF // P, T], F32R)

        raw_ready = [sem(f"raw_ready{s}") for s in range(RAW)]
        hi_done = sem("hi_done")
        lo_done = sem("lo_done")
        chunk_used = sem("chunk_used")
        evac_done = sem("evac_done")
        glu_added = sem("glu_added")
        x_tr = sem("x_tr")
        x_hi_done = sem("x_hi_done")
        x_done = sem("x_done")
        head_norm = sem("head_norm")
        hd_ms = sem("hd_ms")
        hd_sd = sem("hd_sd")
        nrm_ssq, nrm_ms, nrm_sd, xn_ready = sem("nrm_ssq"), sem("nrm_ms"), sem("nrm_sd"), sem("xn_ready")
        tr_ready, tr_hi, tr_lo = sem("tr_ready"), sem("tr_hi"), sem("tr_lo")
        head_link, s5_link = sem("head_link"), sem("s5_link")
        x_in, ident_in, par_in, out_done = sem("x_in"), sem("ident_in"), sem("par_in"), sem("out_done")
        gain_tr, gain_ready, const_ready = sem("gain_tr"), sem("gain_ready"), sem("const_ready")
        dve_link, act_link, pool_link, pe_link = sem("dve_link"), sem("act_link"), sem("pool_link"), sem("pe_link")

        q4 = at(0, "s5_q4", [P, 4, 4, T])
        r_re = at(16, "s5_r_re", [P, 4, T])
        r_im = at(20, "s5_r_im", [P, 4, T])
        cs = at(24, "s5_cs", [P, 2, 2, 4, T])
        p4 = at(40, "s5_p4", [P, 4, 4, T])
        uT = at(56, "s5_uT", [P, KT, T])
        bb_re = at(72, "s5_bb_re", [P, 64, 16])
        bb_im = at(76, "s5_bb_im", [P, 64, 16])
        c_re = at(80, "s5_c_re", [P, KT, 64])
        c_im = at(84, "s5_c_im", [P, KT, 64])
        turn = at(88, "s5_turn", [P, 2, 4, T])
        whole = at(96, "s5_whole", [P, 4, T])
        tval = at(100, "s5_tval", [P, T])
        us = at(101, "s5_us", [P, T])
        bx = at(102, "s5_bx", [P, 2, 4, 2, 16])
        cx = at(103, "s5_cx", [P, 2, 2, 64])
        bt = at(104, "s5_bt", [P, 2, P])
        ct3 = at(105, "s5_ct3", [P, 3, P])
        b_re = at(107, "s5_b_re", [P, 64, 16])
        b_im = at(111, "s5_b_im", [P, 64, 16])
        par = at(115, "s5_par", [P, 20, 64])
        a_rows = at(121, "s5_a_rows", [P, P])
        dt_rows = at(121.5, "s5_dt_rows", [64, 2])
        dt_wide = at(122, "s5_dt_wide", [64, 2, 64])
        parity = at(122.5, "s5_parity", [P, 4])
        gain_rows = at(123, "gain_rows", [P, P])
        absf = at(124, "s5_absf", [P, 4, T])
        s5_in = sem("s5_in")
        s5_a_tr, s5_dt_wide, s5_dt_tr = sem("s5_a_tr"), sem("s5_dt_wide"), sem("s5_dt_tr")
        s5_log, s5_exp = sem("s5_log"), sem("s5_exp")
        s5_par = sem("s5_par")
        s5_stage = sem("s5_stage")
        s5_tr = sem("s5_tr")
        s5_bt, s5_ct = sem("s5_bt"), sem("s5_ct")
        s5_b = sem("s5_b")
        s5_rot = sem("s5_rot")
        s5_turn, s5_whole, s5_frac = sem("s5_turn"), sem("s5_whole"), sem("s5_frac")
        s5_cs = sem("s5_cs")
        s5_q = sem("s5_q")
        s5_y = sem("s5_y")
        s5_z = sem("s5_z")
        s5_g, s5_gh, s5_gl = sem("s5_g"), sem("s5_gh"), sem("s5_gl")

        qT = at(40, "qT", [P, NG * HEADS, T])
        kT = at(88, "kT", [P, HEADS, T])
        vt = at(104, "v_tok", [P, TB, HEADS * DH])
        dist = at(120, "dist", [P, NG * 128 + NG * 256])
        qst = at(124.5, "q_stage", [P, 2, NG, T])
        score = at(130.5, "score", [P, 2, 1152])
        wsum = at(32, "wsum", [P, 2, 384])
        wT = at(35, "wT", [P, 384])
        vst = at(36.5, "v_stage", [P, 2, TB, DH])
        slope = at(139.5, "slope", [P, HEADS, NG])
        at_small = at(139.75, "at_small", [P, 16])
        negm, den, rden = at_small[:, 0:4], at_small[:, 4:8], at_small[:, 8:12]
        qkg = at(140.25, "qk_gain", [P, 4])
        gqk = at(140.5, "gqk", [P, NG])
        hssq = at(139.875, "hssq", [P, 3, TB, 4])
        at_in, gqk_ready = sem("at_in"), sem("gqk_ready")
        at_stage, at_sc, at_bias, at_max = sem("at_stage"), sem("at_sc"), sem("at_bias"), sem("at_max")
        at_exp, at_w, at_pt, at_wt = sem("at_exp"), sem("at_w"), sem("at_pt"), sem("at_wt")
        at_pv, at_oh, at_o = sem("at_pv"), sem("at_oh"), sem("at_o")

        rope_a = at(0, "rope_a", [P, 4, 768])
        rT = at(12, "ret_T", [P, 2 * RH, T])
        dT = at(24, "dif_T", [P, 2 * DIFH, T])
        sq2 = at(0, "sq2", [P, TB, RW + DW])
        dw = at(32, "dif_w", [P, 384])
        dwT = at(33.5, "dif_wT", [P, 384])
        sub_g = at(141, "sub_g", [P, DH])
        lam_v = at(141.5, "lam_v", [P, 4, 64])
        lam_p = at(140, "lam_p", [P, 2, 64])
        proj = at(56, "proj", [P, TB, DIN])
        post_g = at(56, "post_g", [P, D])
        decay = at(108, "decay", [P, RH, 384])
        rope_cs = at(117, "rope_cs", [P, 2, TB, 96])
        rope_t = at(118.5, "rope_t", [P, 4, TB, 96])
        pos_i = at(121.5, "pos_i", [P, TB], I32)
        inv = at(121.75, "inv_freq", [P, 96])
        causal = at(122.25, "causal", [P, 384])
        m2 = at(123.75, "m2_small", [P, 64])
        ra = at(124, "ret_a", [P, 2, 384])
        ds = at(127, "dif_s", [P, 2, 2, 384])
        lru_x = at(0, "lru_x", [LBW, LB, T + 3])
        lru_c = at(8.25, "lru_c", [LBW, LB, T])
        lru_i = at(16.25, "lru_i", [LBW, LB, T])
        lru_y = at(24.25, "lru_y", [LBW, LB, T])
        lru_r = at(124, "lru_r", [LBW, LB, T])
        lru_wa = at(133, "lru_wa", [LBW, LB, LBW])
        lru_wx = at(136, "lru_wx", [LBW, LB, LBW])
        lru_rows = at(139, "lru_rows", [64, LBW])
        lru_p = at(139.5, "lru_p", [LBW, 8, LB])
        lru_t = at(139.75, "lru_t", [LBW, 6, LB])
        pos_f, lam_e, lam_col = m2[:, 0:2], m2[:, 2:4], m2[:, 4:5]
        hs2, hs2_sd = m2[:, 5:25], m2[:, 25:45]
        dnegm, dden, drden, dlr = m2[:, 45:49], m2[:, 49:53], m2[:, 53:57], m2[:, 57:59]
        b2_in, b2l_in, lru_in, pg_in = sem("b2_in"), sem("b2l_in"), sem("lru_in"), sem("pg_in")
        rope_ang, rope_ready, rope_done = sem("rope_ang"), sem("rope_ready"), sem("rope_done")
        lam_dot, lam_exp = sem("lam_dot"), sem("lam_exp")
        gates_done = sem("gates_done")
        a_tr, a_ev = sem("a_tr"), sem("a_ev")
        r_s, r_a, r_o, r_ev = sem("r_s"), sem("r_a"), sem("r_o"), sem("r_ev")
        d_s, d_m, d_max, d_exp, d_w = sem("d_s"), sem("d_m"), sem("d_max"), sem("d_exp"), sem("d_w")
        d_pt, d_wt, d_o, d_ev = sem("d_pt"), sem("d_wt"), sem("d_o"), sem("d_ev")
        h_ms, h_sd, h_done = sem("h_ms"), sem("h_sd"), sem("h_done")
        l_row, l_par, l_e, l_e2, l_l8 = sem("l_row"), sem("l_par"), sem("l_e"), sem("l_e2"), sem("l_l8")
        l_xt, l_x, l_conv, l_g, l_sig = sem("l_xt"), sem("l_x"), sem("l_conv"), sem("l_g"), sem("l_sig")
        l_la, l_a, l_m, l_mq, l_h = sem("l_la"), sem("l_a"), sem("l_m"), sem("l_mq"), sem("l_h")
        l_ht, mix_done = sem("l_ht"), sem("mix_done")
        y_ssq, y_ms, y_sd, res_added = sem("y_ssq"), sem("y_ms"), sem("y_sd"), sem("res_added")

        block = ctx.enter_context(nc.Block())

        def panel_ps(j):
            return ps[:, 2 * j:2 * j + 2, :]

        def x_written(v):
            return [(x_in, 16), (glu_added, 4), (evac_done, G["dn0"].all_evacuated),
                    (evac_done, G["o"].all_evacuated), (evac_done, G["dn1"].all_evacuated),
                    (res_added, 2)][v]

        @block.sync
        def _(sp):
            sp.dma_start(x[:], w["x"][0].rearrange("(b p) d -> p b d", p=P)).then_inc(x_in, 16)
            sp.dma_start(ident[:], c["ident"]).then_inc(ident_in, 16)
            rows = [w["mix_norm"][0], w["ffn_norm"][0], w["kv_norm"], w["mix_norm"][1], w["ffn_norm"][1],
                    w["pre_norm_g_2"][0], w["pre_norm_g_2"][1], w["ssm_d"][0]]
            for n, row in enumerate(rows):
                sp.dma_start(gain_rows[KT * n:KT * n + KT, :], row.rearrange("(k p) -> k p", p=P)).then_inc(par_in, 16)

            def load(g, q, col):
                for k in range(g.chunks):
                    sp.wait_ge(lo_done, g.chunk(q, k) + 1)
                    sp.dma_start(raw[:, k % RAW], g.w[k * CK * P:(k + 1) * CK * P, bass.ds(col, PANEL)]
                                 .rearrange("(t p) n -> p t n", p=P)).then_inc(raw_ready[k % RAW], 16)

            for g in G.values():
                with sp.Fori(g.first, g.panels // 2 + g.first) as i:
                    for j in range(2):
                        load(g, i * 2 + (j - 2 * g.first), g.cols(i, j))
                if g.panels % 2:
                    load(g, g.panels - 1, g.cols(g.panels // 2, 0))
            sp.wait_ge(res_added, 2 * NLAYER2)
            sp.dma_start(out[0].rearrange("(b p) d -> p b d", p=P), x[:]).then_inc(out_done, 16)
            sp.wait_ge(out_done, 16)

        @block.gpsimd
        def _(pool):
            pl = Links(pool, pool_link)
            pool.nop().then_inc(s5_frac, 1)
            pl.link(pool.memset(half_pi[:], math.pi / 2))
            pool.nop().then_inc(const_ready, 1)
            state_major = lambda a: a[0].rearrange("(j g) p h -> (g p) j h", g=2)
            pool.dma_start(a_rows[0:64, :], w["ssm_a_re"][0].rearrange("(j g) p -> j (g p)", g=2)).then_inc(s5_in, 16)
            pool.dma_start(a_rows[64:128, :], w["ssm_a_im"][0].rearrange("(j g) p -> j (g p)", g=2)).then_inc(s5_in, 16)
            pool.dma_start(dt_rows[:], w["ssm_log_dt"][0].rearrange("(j g) -> j g", g=2)).then_inc(s5_in, 16)
            pool.dma_start(tval[:], c["tval"]).then_inc(s5_in, 16)
            pool.dma_start(parity[:], c["parity"]).then_inc(s5_in, 16)
            pool.dma_start(b_re[:], state_major(w["ssm_b_re"])).then_inc(s5_in, 16)
            pool.dma_start(b_im[:], state_major(w["ssm_b_im"])).then_inc(s5_in, 16)
            pool.dma_start(c_re[:], w["ssm_c_re"][0].rearrange("g h p -> (g h) p")
                           .rearrange("(k q) p -> q k p", q=P)).then_inc(s5_in, 16)
            pool.dma_start(c_im[:], w["ssm_c_im"][0].rearrange("g h p -> (g h) p")
                           .rearrange("(k q) p -> q k p", q=P)).then_inc(s5_in, 16)
            pool.wait_ge(s5_in, 16 * 9)
            pool.wait_ge(s5_par, 2)
            pool.wait_ge(tr_hi, 8)

            def s5_stages(i, par_i):
                pool.wait_ge(s5_cs, i + 1)
                pool.tensor_tensor(turn[:, par_i], par[:, 8, bass.ds(i * 4, 4)].unsqueeze(2).to_broadcast([P, 4, T]),
                                   tval[:].unsqueeze(1).to_broadcast([P, 4, T]), ALU.mult).then_inc(s5_turn, 1)
                pool.wait_ge(s5_tr, i + 1)
                for n, b in enumerate((bb_re, bb_im)):
                    pool.tensor_tensor(bx[:, n], b[:, bass.ds(i * 4, 4), :].unsqueeze(2).to_broadcast([P, 4, 2, 16]),
                                       parity[:, 2:4].unsqueeze(1).unsqueeze(3).to_broadcast([P, 4, 2, 16]), ALU.mult)
                for n, cc in enumerate((c_re, c_im)):
                    pool.tensor_tensor(cx[:, n], cc[:, bass.ds(i, 1), :].to_broadcast([P, 2, 64]),
                                       parity[:, 0:2].unsqueeze(2).to_broadcast([P, 2, 64]), ALU.mult)
                pool.wait_ge(s5_b, i + 1)
                pool.tensor_copy(us[:], uT[:, bass.ds(i, 1), :].rearrange("p a t -> p (a t)")).then_inc(s5_stage, 1)
                pool.wait_ge(s5_whole, i + 1)
                pool.tensor_tensor(turn[:, par_i], turn[:, par_i], whole[:], ALU.subtract).then_inc(s5_frac, 1)

            with pool.Fori(0, KT // 2) as n:
                for j in range(2):
                    s5_stages(n * 2 + j, j)

            pool.wait_ge(x_done, 2 * 11 + 2)
            pool.wait_ge(evac_done, G["dn0"].all_evacuated)
            pool.dma_start(dist[:], c["dist"]).then_inc(at_in, 16)
            pool.dma_start(slope[:], c["slope"]).then_inc(at_in, 16)
            pool.dma_start(qkg[:, 0:NG], w["q_norm"][0].rearrange("g e -> e g"),
                           ).then_inc(at_in, 16)
            pool.dma_start(qkg[:, NG:NG + 1], w["k_norm"].rearrange("(e a) -> e a", a=1)).then_inc(at_in, 16)
            pool.wait_ge(gqk_ready, 1)
            pool.wait_ge(x_done, 2 * 27 + 2)
            pool.wait_ge(evac_done, G["q"].all_evacuated)

            def at_stages(h, j):
                pool.wait_ge(at_pv, h + 1)
                pool.tensor_tensor(qst[:, j], qT[:].rearrange("p (g h) t -> p g h t", g=NG)[:, :, bass.ds(h, 1), :]
                                   .rearrange("p g a t -> p g (a t)"),
                                   gqk[:].unsqueeze(2).to_broadcast([P, NG, T]), ALU.mult)
                pool.tensor_copy(vst[:, j], vt[:, :, bass.ds(h * DH, DH)]).then_inc(at_stage, 1)

            with pool.Fori(0, HEADS // 2) as n:
                for j in range(2):
                    at_stages(n * 2 + j, j)

            pool.wait_ge(evac_done, G["dn1"].all_evacuated)
            for dst, src in ((decay, c["decay"]), (inv, c["inv"]), (causal, c["causal"])):
                pool.dma_start(dst[:], src).then_inc(b2_in, 16)
            pool.dma_start(pos_i[:], w["positions_2"][0].rearrange("(b p) -> p b", p=P)).then_inc(b2_in, 16)
            for l in range(NLAYER2):
                if l:
                    pool.wait_ge(mix_done, 4 * l)
                for n, name in enumerate(("q1", "k1", "q2", "k2")):
                    pool.dma_start(lam_v[:, n, :], w[f"diff_lambda_{name}_2"][l].partition_broadcast(P)).then_inc(b2l_in, 16)
                pool.dma_start(sub_g[:], w["diff_subln_g_2"][l].partition_broadcast(P)).then_inc(b2l_in, 16)
                pool.dma_start(lru_rows[0:32, :], w["lru_conv_w_2"][l].rearrange("a (n p) -> (a n) p", p=LBW)).then_inc(lru_in, 16)
                for n, name in enumerate(("conv_b", "ba", "bx", "lambda")):
                    pool.dma_start(lru_rows[32 + 8 * n:40 + 8 * n, :], w[f"lru_{name}_2"][l]
                                   .rearrange("(n p) -> n p", p=LBW)).then_inc(lru_in, 16)
                pool.dma_start(lru_wa[:], w["lru_wa_2"][l].rearrange("n k j -> k n j")).then_inc(lru_in, 16)
                pool.dma_start(lru_wx[:], w["lru_wx_2"][l].rearrange("n k j -> k n j")).then_inc(lru_in, 16)
                pool.wait_ge(tr_ready, 8 * T_OUT[l] + 8)
                pool.wait_ge(mix_done, 4 * l + 4)
                pool.dma_start(post_g[:], w["post_norm_g_2"][l].partition_broadcast(P)).then_inc(pg_in, 16)

        @block.scalar
        def _(act):
            al = Links(act, act_link)

            def split(g, q, ks):
                for k in ks:
                    act.wait_ge(raw_ready[k % RAW], g.raw_count(q, k))
                    act.wait_ge(chunk_used, g.chunk(q, k) + 1)
                    act.activation(whi[:, k % SPLIT], raw[:, k % RAW], ACT.Copy).then_inc(hi_done, 1)

            def whole_panel(g, q):
                act.wait_ge(chunk_used, g.done(q))

            def gate(g, q, j, func):
                whole_panel(g, q)
                act.wait_ge(evac_done, g.evacuated(q) - 1)
                act.activation(gbuf[:], panel_ps(j), func).then_inc(evac_done, 1)

            def store(g, q, j, dst):
                whole_panel(g, q)
                act.activation(dst, panel_ps(j), ACT.Copy).then_inc(evac_done, 1)

            def raw_heads(g, q, j, n):
                whole_panel(g, q)
                act.wait_ge(head_norm, n + 1)
                act.activation(gbuf[:], panel_ps(j), ACT.Copy).then_inc(evac_done, 1)

            def head_sd(n):
                act.wait_ge(hd_ms, n + 1)
                act.activation(hssq[:, 1], hssq[:, 0], ACT.Sqrt).then_inc(hd_sd, 1)

            def hidden_hi(xi, i):
                for u in range(2):
                    act.wait_ge(x_tr, xi * 2 + (u + 3))
                    act.activation(hh[:, bass.ds(i * 4 + 2 * u, 2), :],
                                   ps[:, 4 + u, :].rearrange("p (a t) -> p a t", a=2), ACT.Copy).then_inc(x_hi_done, 1)

            def heads_T(xi, dst, h0):
                for u in range(2):
                    act.wait_ge(x_tr, xi * 2 + (u + 3))
                    act.activation(dst[:, bass.ds(h0 + 2 * u, 2), :],
                                   ps[:, 4 + u, :].rearrange("p (a t) -> p a t", a=2), ACT.Copy).then_inc(x_done, 1)

            def panels(g, evac, after=None):
                def one(q, j, first=False):
                    split(g, q, range(2))
                    if not first:
                        evac(q - 1, 1 - j)
                    split(g, q, range(2, g.chunks))
                    if after and not first:
                        after(q - 1, 1 - j)
                one(0, 0, True)
                one(1, 1)
                pairs = g.panels // 2
                if pairs > 2:
                    with act.Fori(1, pairs) as i:
                        for j in range(2):
                            one(i * 2 + j, j)
                elif pairs == 2:
                    for j in range(2):
                        one(2 + j, j)
                last = 2 * pairs - 1
                if g.panels % 2:
                    one(g.panels - 1, 0)
                    last = g.panels - 1
                evac(last, last % 2)
                if after:
                    after(last, last % 2)

            def norm(v):
                act.wait_ge(*x_written(v))
                for b in range(TB):
                    if b:
                        act.wait_ge(nrm_ssq, 2 * v + b)
                    act.activation(junk[:], x[:, b, :], ACT.Square, accum_out=ssq[:, b:b + 1]).then_inc(nrm_ssq, 1)
                act.wait_ge(nrm_ms, v + 1)
                act.activation(sdev[:], msq[:], ACT.Sqrt).then_inc(nrm_sd, 1)

            def turn_hi(v):
                gain = TURNS[v]
                for u in range(8):
                    act.wait_ge(tr_ready, 8 * v + u + 1)
                    for kk in range(2):
                        kt = 2 * u + kk
                        src = ps[:, 4 + u % 4, kk * T:(kk + 1) * T]
                        dst = uT[:, kt, :] if v == T_MIX0 else xh[:, kt, :]
                        scale = 1.0 if gain is None else gains[:, GAINS.index(gain), kt:kt + 1]
                        last = act.activation(dst, src, ACT.Copy, scale=scale)
                    last.then_inc(tr_hi, 1)

            act.nop().then_inc(s5_cs, 2)
            act.nop().then_inc(s5_ct, 1)
            act.nop().then_inc(at_wt, 1)
            act.wait_ge(const_ready, 1)
            act.wait_ge(gain_tr, 1)
            act.activation(gains[:].rearrange("p a k -> p (a k)"), ps[:, 0, 0:P], ACT.Copy).then_inc(gain_ready, 1)
            norm(N_MIX0)
            turn_hi(T_MIX0)
            act.wait_ge(s5_par, 1)
            act.activation(par[:, 10, :], par[:, 8, :], ACT.Sin, scale=TWO_PI_BELOW).then_inc(s5_exp, 1)
            al.link(act.activation(par[:, 9, :], par[:, 8, :], ACT.Abs))
            act.activation(par[:, 11, :], par[:, 9, :], ACT.Sin, bias=half_pi[:], scale=-TWO_PI_BELOW).then_inc(s5_exp, 1)

            def s5_trig(i, j):
                act.wait_ge(s5_frac, i + 2)
                act.wait_ge(s5_q, i + 1)
                act.activation(cs[:, j, 1], turn[:, j], ACT.Sin, scale=TWO_PI_BELOW)
                act.activation(absf[:], turn[:, j], ACT.Abs).then_inc(act_link, 1)
                act.wait_ge(act_link, i + 2)
                act.activation(cs[:, j, 0], absf[:], ACT.Sin, bias=half_pi[:], scale=-TWO_PI_BELOW).then_inc(s5_cs, 1)

            def s5_mats(i):
                act.wait_ge(s5_tr, i + 2)
                act.wait_ge(s5_b, i + 1)
                act.activation(bt[:], ps[:, 4, 0:2 * P].rearrange("p (a t) -> p a t", a=2), ACT.Copy).then_inc(s5_bt, 1)
                act.wait_ge(s5_y, i + 1)
                act.activation(ct3[:, 0, :], ps[:, 4, 2 * P:3 * P], ACT.Copy)
                act.activation(ct3[:, 1:3, :], ps[:, 4, 2 * P:4 * P].rearrange("p (a t) -> p a t", a=2),
                               ACT.Copy, scale=-1.0).then_inc(s5_ct, 1)

            assert al.n == 1
            with act.Fori(0, KT // 2) as n:
                for j in range(2):
                    s5_trig(n * 2 + j, j)
                    s5_mats(n * 2 + j)
            al.n += KT
            act.wait_ge(s5_z, KT + 1)
            for n in range(4):
                act.activation(uT[:, 4 * n:4 * n + 4, :], uT[:, 4 * n:4 * n + 4, :], ACT.Gelu_apprx_tanh).then_inc(s5_g, 1)
            for n in range(4):
                act.wait_ge(s5_g, n + 1)
                act.activation(xh[:, 4 * n:4 * n + 4, :], uT[:, 4 * n:4 * n + 4, :], ACT.Copy).then_inc(s5_gh, 1)

            panels(G["glu"], lambda q, j: gate(G["glu"], q, j, ACT.Sigmoid) if j == 0 else None)

            def ffn(layer):
                g, x0 = G[f"gu{layer}"], (0, 27)[layer]
                def one(i, j, first=False):
                    q = i * 2 + j
                    split(g, q, range(2))
                    if j == 1:
                        gate(g, q - 1, 0, ACT.Silu)
                    split(g, q, range(2, g.chunks))
                    if j == 0 and not first:
                        hidden_hi(i + (x0 - 1), i - 1)
                one(0, 0, True)
                one(0, 1)
                with act.Fori(1, g.panels // 2) as i:
                    for j in range(2):
                        one(i, j)
                hidden_hi(g.panels // 2 + x0 - 1, g.panels // 2 - 1)
                panels(G[f"dn{layer}"], lambda q, j: None)

            norm(N_FFN0)
            turn_hi(T_FFN0)
            ffn(0)
            norm(N_KV)
            turn_hi(T_KV)

            def head_panels(g, n0, dst):
                def evac(q, j):
                    raw_heads(g, q, j, q + n0)
                    head_sd(q + n0)
                panels(g, evac, lambda q, j: heads_T(q + (n0 + 11), dst, q * 4))

            head_panels(G["k"], 0, kT)
            panels(G["v"], lambda q, j: store(G["v"], q, j, vt[:, :, bass.ds(q * PANEL, PANEL)]))
            turn_hi(T_MIX1)
            head_panels(G["q"], 4, qT)

            def at_a(h, j):
                act.wait_ge(at_max, h + 1)
                for b, (lo, hi) in enumerate(((0, 384), (384, 1152))):
                    last = act.activation(score[:, j, lo:hi], score[:, j, lo:hi], ACT.Exp,
                                          bias=negm[:, 2 * j + b:2 * j + b + 1],
                                          accum_out=den[:, 2 * j + b:2 * j + b + 1])
                last.then_inc(at_exp, 1)

            def at_b(h, j):
                act.wait_ge(at_pt, h + 1)
                act.activation(wT[:], ps[:, 6, 0:384], ACT.Copy).then_inc(at_wt, 1)
                act.wait_ge(at_pv, h + 3)
                act.activation(xh[:, bass.ds(h, 1), :].rearrange("p a t -> p (a t)"), ps[:, 7, 0:T],
                               ACT.Copy).then_inc(at_oh, 1)

            heads_in_turn(act, at_a, at_b, None)
            panels(G["o"], lambda q, j: None)
            norm(N_FFN1)
            turn_hi(T_FFN1)
            ffn(1)

            act.wait_ge(rope_ang, 1)
            act.activation(rope_cs[:, 1], rope_t[:, 0], ACT.Sin, scale=TWO_PI_BELOW)
            al.link(act.activation(rope_t[:, 1], rope_t[:, 0], ACT.Abs))
            act.activation(rope_cs[:, 0], rope_t[:, 1], ACT.Sin, bias=half_pi[:], scale=-TWO_PI_BELOW).then_inc(rope_ready, 1)

            for l in range(NLAYER2):
                act.wait_ge(lam_dot, l + 1)
                act.activation(lam_e, lam_e, ACT.Exp).then_inc(lam_exp, 1)
                norm(N_PRE[l])
                turn_hi(T_PRE[l])
                g = G[f"in{l}"]
                panels(g, lambda q, j: store(g, q, j, proj[:, :, bass.ds(q * PANEL, PANEL)]))
                for col, width in ((C_RG, RW), (C_DG, DW), (C_LG, LW)):
                    act.wait_ge(evac_done, g.all_evacuated)
                    act.activation(proj[:, :, col:col + width], proj[:, :, col:col + width],
                                   ACT.Silu).then_inc(gates_done, 1)
                for u in range(10):
                    act.wait_ge(a_tr, 10 * l + u + 1)
                    dst = rT[:, 2 * u:2 * u + 2, :] if u < 6 else dT[:, 2 * u - 12:2 * u - 10, :]
                    act.activation(dst, ps[:, 4 + u % 4, :].rearrange("p (a t) -> p a t", a=2),
                                   ACT.Copy).then_inc(a_ev, 1)
                for h in range(RH):
                    act.wait_ge(r_o, RH * l + h + 1)
                    act.activation(tok[:, :, DH * h:DH * h + DH], ps[:, 2 + h % 2, 0:TB * DH]
                                   .rearrange("p (b e) -> p b e", b=TB), ACT.Copy).then_inc(r_ev, 1)

                def d_a(h):
                    act.wait_ge(d_max, DIFH * l + h + 1)
                    for m in range(2):
                        for b, (lo, hi) in enumerate(((0, 128), (128, 384))):
                            n = 2 * m + b
                            last = act.activation(ds[:, h % 2, m, lo:hi], ds[:, h % 2, m, lo:hi], ACT.Exp,
                                                  bias=dnegm[:, n:n + 1], accum_out=dden[:, n:n + 1])
                    last.then_inc(d_exp, 1)

                def d_b(h):
                    act.wait_ge(d_pt, DIFH * l + h + 1)
                    act.activation(dwT[:], ps[:, 0, 0:384], ACT.Copy).then_inc(d_wt, 1)
                    act.wait_ge(d_o, DIFH * l + h + 1)
                    act.activation(tok[:, :, RW + DH * h:RW + DH * h + DH], ps[:, 2 + h % 2, 0:TB * DH]
                                   .rearrange("p (b e) -> p b e", b=TB), ACT.Copy).then_inc(d_ev, 1)

                for h in range(DIFH):
                    d_a(h)
                    d_b(h)
                act.wait_ge(h_ms, l + 1)
                act.activation(hs2_sd, hs2, ACT.Sqrt).then_inc(h_sd, 1)

                act.wait_ge(l_row, l + 1)
                act.activation(lru_p[:].rearrange("p a n -> p (a n)"), ps[0:LBW, 3, 0:64], ACT.Copy).then_inc(l_par, 1)
                act.wait_ge(l_e, l + 1)
                act.activation(lru_t[:, 1, :], lru_t[:, 0, :], ACT.Exp, scale=-1.0).then_inc(l_e2, 1)
                act.wait_ge(h_done, 5 * l + 1)
                for u in range(4):
                    act.wait_ge(l_xt, 4 * l + u + 1)
                    act.activation(lru_x[:, 2 * u:2 * u + 2, 3:T + 3], ps[0:LBW, 4 + u, :]
                                   .rearrange("p (a t) -> p a t", a=2), ACT.Copy).then_inc(l_x, 1)
                for n in range(LB):
                    act.wait_ge(l_g, LB * l + n + 1)
                    act.activation(lru_r[:, n, :], ps[0:LBW, n, 0:T], ACT.Sigmoid, bias=lru_p[:, 5, n:n + 1])
                    act.activation(lru_i[:, n, :], ps[0:LBW, n, T:2 * T], ACT.Sigmoid,
                                   bias=lru_p[:, 6, n:n + 1]).then_inc(l_sig, 1)
                act.wait_ge(l_la, l + 1)
                act.activation(lru_x[:, :, 0:T], lru_r[:], ACT.Exp).then_inc(l_a, 1)
                act.activation(lru_y[:], lru_r[:], ACT.Tanh, scale=-1.0).then_inc(l_a, 1)
                act.wait_ge(l_a, 3 * l + 2)
                act.activation(lru_r[:], lru_x[:, :, 0:T], ACT.Square).then_inc(l_a, 1)
                act.wait_ge(l_m, l + 1)
                act.activation(lru_y[:], lru_r[:], ACT.Sqrt).then_inc(l_mq, 1)
                turn_hi(T_OUT[l])
                g = G[f"out{l}"]
                panels(g, lambda q, j: store(g, q, j, tok[:, :, bass.ds(q * PANEL, PANEL)]))
                act.wait_ge(evac_done, g.all_evacuated)
                for b in range(TB):
                    if b:
                        act.wait_ge(y_ssq, 2 * l + b)
                    act.activation(junk[:], tok[:, b, :], ACT.Square, accum_out=ssq[:, b:b + 1]).then_inc(y_ssq, 1)
                act.wait_ge(y_ms, l + 1)
                act.activation(sdev[:], msq[:], ACT.Sqrt).then_inc(y_sd, 1)

        @block.tensor
        def _(pe):
            pe.nop().then_inc(chunk_used, SPLIT)
            for start in (s5_tr, s5_b, s5_y):
                pe.nop().then_inc(start, 1)
            for start in (x_tr, at_pv):
                pe.nop().then_inc(start, 2)

            def chunk(g, q, j, k, hi, lo):
                pe.wait_ge(lo_done, g.chunk(q, k) + (AHEAD + 1))
                for t in range(CK):
                    kt = CK * k + t
                    for b in range(TB):
                        tokens = slice(b * P, b * P + P)
                        for n, (xs, ws) in enumerate(((hi, whi), (hi, wlo), (lo, whi))):
                            last = pe.matmul(ps[:, 2 * j + b, :], xs[:, kt, tokens], ws[:, k % SPLIT, t, :],
                                             start=kt == 0 and n == 0,
                                             stop=kt == CK * g.chunks - 1 and n == 2)
                last.then_inc(chunk_used, 1)

            def panel(g, q, j, hi=xh, lo=xl, between=None):
                pe.wait_ge(evac_done, g.evacuated(q) - 2)
                for k in range(g.chunks):
                    chunk(g, q, j, k, hi, lo)
                    if between and k == 5:
                        between()

            def panels(g, hi=xh, lo=xl, after=None):
                def one(q, j, first=False):
                    panel(g, q, j, hi, lo, (lambda: after(q - 1, 1 - j)) if after and not first else None)
                one(0, 0, True)
                one(1, 1)
                pairs = g.panels // 2
                if pairs > 2:
                    with pe.Fori(1, pairs) as i:
                        for j in range(2):
                            one(i * 2 + j, j)
                elif pairs == 2:
                    for j in range(2):
                        one(2 + j, j)
                if g.panels % 2:
                    one(g.panels - 1, 0)
                if after:
                    after(g.panels - 1, 1)

            def turn_hbuf(xi, ready, count):
                pe.wait_ge(ready, count)
                for u in range(2):
                    pe.wait_ge(x_done, xi * 2 + (u + 1))
                    for f in range(2):
                        for b in range(TB):
                            last = pe.transpose(ps[:, 4 + u, f * T + b * P:f * T + b * P + P],
                                                hbuf[:, b, (2 * u + f) * P:(2 * u + f + 1) * P], ident[:])
                    last.then_inc(x_tr, 1)

            def turn(v):
                if v == T_OUT[0] or v == T_OUT[1]:
                    pe.wait_ge(mix_done, 4 * T_OUT.index(v) + 4)
                elif v != T_MIX1:
                    pe.wait_ge(xn_ready, 2 * [T_MIX0, T_FFN0, T_KV, T_FFN1, *T_PRE].index(v) + 2)
                for u in range(8):
                    if u >= 4 and v == T_MIX0:
                        pe.wait_ge(tr_hi, u - 3)
                    elif u >= 4:
                        pe.wait_ge(tr_lo, 8 * (v - 1) + u - 3)
                    for kk in range(2):
                        for b in range(TB):
                            last = pe.transpose(ps[:, 4 + u % 4, kk * T + b * P:kk * T + b * P + P],
                                                tok[:, b, (2 * u + kk) * P:(2 * u + kk + 1) * P], ident[:])
                    last.then_inc(tr_ready, 1)
                if v != T_MIX0:
                    pe.wait_ge(tr_lo, 8 * v)

            pe.wait_ge(ident_in, 16)
            pe.wait_ge(par_in, 16 * len(GAINS))
            pe.transpose(ps[:, 0, 0:P], gain_rows[:], ident[:]).then_inc(gain_tr, 1)
            pe.wait_ge(s5_in, 16 * 9)
            pe.transpose(ps[:, 1, 0:P], a_rows[:], ident[:]).then_inc(s5_a_tr, 1)
            pe.wait_ge(s5_dt_wide, 1)
            pe.transpose(ps[:, 2, 0:64], dt_wide[:].rearrange("p a b -> p (a b)"), ident[0:64, 0:64]).then_inc(s5_dt_tr, 1)
            turn(T_MIX0)

            def s5_in_products(i):
                pe.wait_ge(s5_stage, i + 1)
                pe.wait_ge(s5_ct, i + 1)
                mats = [bx[:, 0].rearrange("p a g h -> p (a g h)"), bx[:, 1].rearrange("p a g h -> p (a g h)"),
                        cx[:, 0].rearrange("p g h -> p (g h)"), cx[:, 1].rearrange("p g h -> p (g h)")]
                for n, m in enumerate(mats):
                    last = pe.transpose(ps[:, 4, n * P:n * P + P], m, ident[:])
                last.then_inc(s5_tr, 1)
                pe.wait_ge(s5_bt, i + 1)
                pe.wait_ge(s5_rot, i + 1)
                for s in range(4):
                    rows = slice(32 * s, 32 * s + 32)
                    for m in range(2):
                        last = pe.matmul(ps[:, s, m * T:m * T + T], bt[rows, m, :], us[rows, :], start=True, stop=True)
                last.then_inc(s5_b, 1)

            def s5_outputs(i):
                pe.wait_ge(s5_q, i + 3)
                pe.wait_ge(s5_ct, i + 2)
                pe.wait_ge(s5_z, i + 1)
                for s in range(4):
                    rows = slice(32 * s, 32 * s + 32)
                    for n, m in enumerate((0, 1, 2, 2)):
                        last = pe.matmul(ps[rows, 5, 0:T], ct3[:, m, rows], q4[:, n, s, :], start=n == 0, stop=n == 3)
                last.then_inc(s5_y, 1)

            s5_in_products(0)
            with pe.Fori(0, KT // 2 - 1) as n:
                for j in range(2):
                    s5_in_products(n * 2 + (j + 1))
                    s5_outputs(n * 2 + j)
            s5_in_products(KT - 1)
            s5_outputs(KT - 2)
            s5_outputs(KT - 1)
            pe.wait_ge(s5_gl, 4)
            panels(G["glu"])

            def ffn(layer):
                g, x0 = G[f"gu{layer}"], (0, 27)[layer]
                def hidden(i):
                    turn_hbuf(i + x0, evac_done, g.evacuated(i * 2 + 1))
                panel(g, 0, 0)
                panel(g, 1, 1)
                with pe.Fori(1, g.panels // 2) as i:
                    panel(g, i * 2, 0, between=lambda: hidden(i - 1))
                    panel(g, i * 2 + 1, 1)
                hidden(g.panels // 2 - 1)
                pe.wait_ge(x_done, 2 * (x0 + g.panels // 2) + 2)
                panels(G[f"dn{layer}"], hh, hl)

            turn(T_FFN0)
            ffn(0)
            turn(T_KV)
            panels(G["k"], after=lambda q, j: turn_hbuf(q + 11, head_norm, q + 2))
            panels(G["v"])
            turn(T_MIX1)
            panels(G["q"], after=lambda q, j: turn_hbuf(q + 15, head_norm, q + 6))

            def at_scores(h, j):
                pe.wait_ge(at_stage, h + 1)
                pe.wait_ge(at_bias, h + 1)
                for g in range(NG):
                    pe.matmul(ps[:, 3 * j, g * P:g * P + P], qst[:, j, g, 0:P],
                              kT[:, bass.ds(h, 1), 0:P].rearrange("p a t -> p (a t)"), start=True, stop=True)
                for g in range(NG):
                    last = pe.matmul(ps[:, 3 * j + 1 + g // 2, (g % 2) * T:(g % 2) * T + T], qst[:, j, g, P:T],
                                     kT[:, bass.ds(h, 1), :].rearrange("p a t -> p (a t)"), start=True, stop=True)
                last.then_inc(at_sc, 1)

            def at_values(h, j):
                pe.wait_ge(at_w, h + 1)
                pe.wait_ge(at_wt, h + 1)
                for n in range(3):
                    last = pe.transpose(ps[:, 6, n * P:n * P + P], wsum[:, j, n * P:n * P + P], ident[:])
                last.then_inc(at_pt, 1)
                pe.wait_ge(at_wt, h + 2)
                pe.wait_ge(at_o, h + 1)
                pe.matmul(ps[:, 7, 0:T], vst[:, j, 0, :], wT[:, 0:T], start=True, stop=False)
                pe.matmul(ps[:, 7, P:T], vst[:, j, 1, :], wT[:, T:T + P], start=False, stop=True).then_inc(at_pv, 1)

            heads_in_turn(pe, at_scores, at_values)
            pe.wait_ge(at_o, HEADS + 1)
            panels(G["o"])
            turn(T_FFN1)
            ffn(1)

            for l in range(NLAYER2):
                turn(T_PRE[l])
                panels(G[f"in{l}"])
                pe.wait_ge(rope_done, l + 1)
                for u in range(10):
                    if u >= 4:
                        pe.wait_ge(a_ev, 10 * l + u - 3)
                    for f in range(2):
                        i = 2 * u + f
                        col = C_RQ + P * i if u < 6 else C_DQ + P * (i - 12)
                        for b in range(TB):
                            last = pe.transpose(ps[:, 4 + u % 4, f * T + b * P:f * T + b * P + P],
                                                proj[:, b, col:col + P], ident[:])
                    last.then_inc(a_tr, 1)
                pe.wait_ge(a_ev, 10 * l + 10)

                def r_scores(h):
                    if h >= 2:
                        pe.wait_ge(r_a, RH * l + h - 1)
                    q, k = rT[:, h, :], rT[:, RH + h, :]
                    pe.matmul(ps[:, h % 2, 0:T], k[:, 0:P], q, start=True, stop=True)
                    pe.matmul(ps[:, h % 2, T:T + P], k[:, P:T], q[:, P:T], start=True, stop=True).then_inc(r_s, 1)

                def r_values(h):
                    pe.wait_ge(r_a, RH * l + h + 1)
                    if h >= 2:
                        pe.wait_ge(r_ev, RH * l + h - 1)
                    v = proj[:, :, C_RV + DH * h:C_RV + DH * h + DH]
                    o, a = ps[:, 2 + h % 2, :], ra[:, h % 2, :]
                    pe.matmul(o[:, 0:DH], a[:, 0:P], v[:, 0, :], start=True, stop=True)
                    pe.matmul(o[:, DH:2 * DH], a[:, P:T], v[:, 0, :], start=True, stop=False)
                    pe.matmul(o[:, DH:2 * DH], a[:, T:T + P], v[:, 1, :], start=False, stop=True).then_inc(r_o, 1)

                r_scores(0)
                for h in range(RH):
                    if h + 1 < RH:
                        r_scores(h + 1)
                    r_values(h)

                def d_scores(h):
                    if h >= 2:
                        pe.wait_ge(d_m, DIFH * l + h - 1)
                    for m in range(2):
                        rows = slice(64 * m, 64 * m + 64)
                        s = ps[:, 4 + 2 * (h % 2) + m, :]
                        q, k = dT[rows, h, :], dT[rows, DIFH + h, :]
                        pe.matmul(s[:, 0:P], q[:, 0:P], k[:, 0:P], start=True, stop=True)
                        last = pe.matmul(s[:, P:P + T], q[:, P:T], k, start=True, stop=True)
                    last.then_inc(d_s, 1)

                def d_values(h):
                    pe.wait_ge(d_w, DIFH * l + h + 1)
                    if h == 0:
                        pe.wait_ge(r_a, RH * (l + 1))
                    else:
                        pe.wait_ge(d_wt, DIFH * l + h)
                    for n in range(3):
                        last = pe.transpose(ps[:, 0, n * P:n * P + P], dw[:, n * P:n * P + P], ident[:])
                    last.then_inc(d_pt, 1)
                    pe.wait_ge(d_wt, DIFH * l + h + 1)
                    if h < 2:
                        pe.wait_ge(r_ev, RH * (l + 1))
                    else:
                        pe.wait_ge(d_ev, DIFH * l + h - 1)
                    v = proj[:, :, C_DV + DH * h:C_DV + DH * h + DH]
                    o = ps[:, 2 + h % 2, :]
                    pe.matmul(o[:, 0:DH], dwT[:, 0:P], v[:, 0, :], start=True, stop=True)
                    pe.matmul(o[:, DH:2 * DH], dwT[:, P:T], v[:, 0, :], start=True, stop=False)
                    pe.matmul(o[:, DH:2 * DH], dwT[:, T:T + P], v[:, 1, :], start=False, stop=True).then_inc(d_o, 1)

                d_scores(0)
                for h in range(DIFH):
                    if h + 1 < DIFH:
                        d_scores(h + 1)
                    d_values(h)

                pe.wait_ge(lru_in, 16 * 7 * (l + 1))
                pe.wait_ge(d_ev, DIFH * (l + 1))
                pe.transpose(ps[0:LBW, 3, 0:64], lru_rows[:], ident[0:64, 0:64]).then_inc(l_row, 1)
                pe.wait_ge(d_m, DIFH * (l + 1))
                for u in range(4):
                    for f in range(2):
                        col = C_LX + LBW * (2 * u + f)
                        for b in range(TB):
                            last = pe.transpose(ps[0:LBW, 4 + u, f * T + b * P:f * T + b * P + P],
                                                proj[:, b, col:col + LBW], ident[:])
                    last.then_inc(l_xt, 1)
                pe.wait_ge(l_par, l + 1)
                pe.wait_ge(l_x, 4 * (l + 1))
                for n in range(LB):
                    if n == 0:
                        pe.wait_ge(l_conv, l + 1)
                    pe.matmul(ps[0:LBW, n, 0:T], lru_wa[:, n, :], lru_c[:, n, :], start=True, stop=True)
                    pe.matmul(ps[0:LBW, n, T:2 * T], lru_wx[:, n, :], lru_c[:, n, :], start=True, stop=True).then_inc(l_g, 1)
                pe.wait_ge(l_h, l + 1)
                for u in range(4):
                    b, half = u // 2, u % 2
                    for f in range(4):
                        last = pe.transpose(ps[:, 4 + u, f * LBW:f * LBW + LBW],
                                            lru_y[:, 4 * half + f, b * P:b * P + P], ident[0:LBW, 0:LBW])
                    last.then_inc(l_ht, 1)
                turn(T_OUT[l])
                panels(G[f"out{l}"])

        @block.vector
        def _(dve):
            dl = Links(dve, dve_link)
            link = dl.link
            dve.nop().then_inc(lo_done, AHEAD)
            for start, n in ((evac_done, 2), (x_done, 2), (head_norm, 1), (s5_rot, 1), (s5_q, 2), (s5_z, 1),
                             (at_bias, 2), (at_o, 1)):
                dve.nop().then_inc(start, n)

            def split(g, q, ks):
                for k in ks:
                    dve.wait_ge(hi_done, g.chunk(q, k) + 1)
                    dve.wait_ge(chunk_used, g.chunk(q, k) + 1)
                    dve.tensor_tensor(wlo[:, k % SPLIT], raw[:, k % RAW], whi[:, k % SPLIT].bitcast(F32),
                                      ALU.subtract).then_inc(lo_done, 1)

            def product(g, q, j):
                dve.wait_ge(chunk_used, g.done(q))
                dve.wait_ge(evac_done, g.evacuated(q) - 1)
                dve.tensor_tensor(hbuf[:], panel_ps(j), gbuf[:], ALU.mult).then_inc(evac_done, 1)

            def residual(g, q, j):
                dve.wait_ge(chunk_used, g.done(q))
                cols = x[:, :, bass.ds(q * PANEL, PANEL)]
                dve.tensor_tensor(cols, panel_ps(j), cols, ALU.add).then_inc(evac_done, 1)

            def hidden_lo(fi, i):
                for u in range(2):
                    dve.wait_ge(x_hi_done, fi * 2 + (u + 1))
                    tiles = bass.ds(i * 4 + 2 * u, 2)
                    dve.tensor_tensor(hl[:, tiles, :], ps[:, 4 + u, :].rearrange("p (a t) -> p a t", a=2),
                                      hh[:, tiles, :].bitcast(F32), ALU.subtract).then_inc(x_done, 1)

            def panels(g, evac):
                def one(q, j, first=False):
                    split(g, q, range(2))
                    if not first:
                        evac(q - 1, 1 - j)
                    split(g, q, range(2, g.chunks))
                one(0, 0, True)
                one(1, 1)
                pairs = g.panels // 2
                if pairs > 2:
                    with dve.Fori(1, pairs) as i:
                        for j in range(2):
                            one(i * 2 + j, j)
                elif pairs == 2:
                    for j in range(2):
                        one(2 + j, j)
                last = 2 * pairs - 1
                if g.panels % 2:
                    one(g.panels - 1, 0)
                    last = g.panels - 1
                evac(last, last % 2)

            def root_mean(ready, count, ms, sd):
                dve.wait_ge(ready, count)
                dve.tensor_scalar(msq[:], ssq[:], 1.0 / D, EPS, ALU.mult, ALU.add).then_inc(ms, 1)
                dve.wait_ge(*sd)
                link(dve.reciprocal(rstd[:], sdev[:]))

            def norm(v):
                root_mean(nrm_ssq, 2 * v + 2, nrm_ms, (nrm_sd, v + 1))
                for b in range(TB):
                    dve.tensor_scalar(tok[:, b, :], x[:, b, :], rstd[:, b:b + 1], None, ALU.mult).then_inc(xn_ready, 1)

            def turn_lo(v):
                gain = TURNS[v]
                for u in range(8):
                    dve.wait_ge(tr_hi, 8 * v + u + 1)
                    for kk in range(2):
                        kt = 2 * u + kk
                        scale = 1.0 if gain is None else gains[:, GAINS.index(gain), kt:kt + 1]
                        last = dve.scalar_tensor_tensor(xl[:, kt, :], ps[:, 4 + u % 4, kk * T:(kk + 1) * T], scale,
                                                        xh[:, kt, :].bitcast(F32), ALU.mult, ALU.subtract)
                    last.then_inc(tr_lo, 1)

            def exp_to(dst, src, n, r, e, bits):
                link(dve.tensor_scalar(n, src, 1.0 / math.log(2.0), MAGIC, ALU.mult, ALU.add))
                link(dve.tensor_scalar(n, n, MAGIC, -127.0, ALU.subtract, ALU.max))
                link(dve.scalar_tensor_tensor(r, n, -0.693359375, src, ALU.mult, ALU.add))
                link(dve.scalar_tensor_tensor(r, n, 2.12194440054690583e-4, r, ALU.mult, ALU.add))
                link(dve.tensor_scalar(e, r, 1.0 / math.factorial(8), None, ALU.mult))
                for k in range(7, 0, -1):
                    link(dve.scalar_tensor_tensor(e, e, 1.0 / math.factorial(k), r, ALU.add, ALU.mult))
                link(dve.tensor_scalar(bits, n, 127.0, float(2**23), ALU.add, ALU.mult))
                link(dve.scalar_tensor_tensor(dst, e, 1.0, bits.bitcast(F32), ALU.add, ALU.mult))

            def turns_of(phi, ang, n):
                link(dve.tensor_scalar(n, ang, 1.0 / (2 * math.pi), MAGIC, ALU.mult, ALU.add))
                link(dve.tensor_scalar(n, n, MAGIC, None, ALU.subtract))
                for part in (C1, C2, C3):
                    link(dve.scalar_tensor_tensor(ang, n, -part, ang, ALU.mult, ALU.add))
                link(dve.tensor_scalar(phi, ang, 1.0 / (2 * math.pi), 0.5, ALU.mult, ALU.min))
                return dve.tensor_scalar(phi, phi, -0.5, None, ALU.max)

            V = lambda n: par[:, n, :]
            dve.wait_ge(s5_in, 16 * 9)
            dve.tensor_copy(dt_wide[:], dt_rows[:].unsqueeze(2).to_broadcast([64, 2, 64])).then_inc(s5_dt_wide, 1)
            norm(N_MIX0)
            dve.wait_ge(s5_a_tr, 1)
            dve.tensor_scalar(V(0), ps[:, 1, 0:64], -1e-4, None, ALU.min)
            link(dve.tensor_copy(V(1), ps[:, 1, 64:128]))
            dve.wait_ge(s5_dt_tr, 1)
            link(dve.tensor_copy(V(19), ps[:, 2, 0:64]))
            exp_to(V(2), V(19), V(6), V(7), V(17), V(18).bitcast(I32))
            link(dve.tensor_tensor(V(3), V(0), V(2), ALU.mult))
            exp_to(V(4), V(3), V(6), V(7), V(17), V(18).bitcast(I32))
            link(dve.tensor_tensor(V(5), V(1), V(2), ALU.mult))
            turns_of(V(8), V(5), V(6)).then_inc(s5_par, 1)
            dve.wait_ge(s5_exp, 2)
            link(dve.tensor_tensor(V(12), V(4), V(11), ALU.mult))
            link(dve.tensor_tensor(V(13), V(4), V(10), ALU.mult))
            link(dve.tensor_tensor(V(14), V(0), V(0), ALU.mult))
            link(dve.tensor_tensor(V(17), V(1), V(1), ALU.mult))
            link(dve.tensor_tensor(V(14), V(14), V(17), ALU.add))
            link(dve.reciprocal(V(14), V(14)))
            link(dve.tensor_scalar(V(12), V(12), -1.0, None, ALU.add))
            for dst, (a, b), op in ((15, (0, 1), ALU.add), (16, (1, 0), ALU.subtract)):
                x_, y_ = (12, 13) if dst == 15 else (13, 12)
                link(dve.tensor_tensor(V(17), V(x_), V(0), ALU.mult))
                link(dve.tensor_tensor(V(18), V(y_), V(1), ALU.mult))
                link(dve.tensor_tensor(V(17), V(17), V(18), op))
                link(dve.tensor_tensor(V(dst), V(17), V(14), ALU.mult))
            wide = lambda n: V(n).unsqueeze(2).to_broadcast([P, 64, 16])
            tmp = whole[:].rearrange("p a t -> p (a t)").rearrange("p (j h) -> p j h", h=16)
            for dst, (m, n), op in ((bb_re, (b_re, b_im), ALU.subtract), (bb_im, (b_im, b_re), ALU.add)):
                link(dve.tensor_tensor(dst[:], m[:], wide(15), ALU.mult))
                link(dve.tensor_tensor(tmp, n[:], wide(16), ALU.mult))
                last = dve.tensor_tensor(dst[:], dst[:], tmp, op)
                if dst is bb_re:
                    link(last)
            last.then_inc(s5_par, 1)

            def s5_round(i, j):
                dve.wait_ge(s5_turn, i + 1)
                dve.wait_ge(s5_frac, i + 1)
                dve.tensor_scalar(whole[:], turn[:, j], MAGIC, MAGIC, ALU.add, ALU.subtract).then_inc(s5_whole, 1)

            def s5_states(i, j, ahead=True, behind=True):
                cos, sin = cs[:, j, 0], cs[:, j, 1]
                dve.wait_ge(s5_cs, i + 3)
                dve.wait_ge(s5_b, i + 2)
                in_re, in_im = ps[:, 0:4, 0:T], ps[:, 0:4, T:2 * T]
                dve.tensor_tensor(p4[:, 0], in_re, cos, ALU.mult)
                dve.tensor_tensor(p4[:, 1], in_im, sin, ALU.mult)
                dve.tensor_tensor(p4[:, 2], in_im, cos, ALU.mult)
                dve.tensor_tensor(p4[:, 3], in_re, sin, ALU.mult).then_inc(s5_rot, 1)
                if ahead:
                    s5_round(i + 1, 1 - j)
                dve.wait_ge(s5_rot, i + 2)
                dve.tensor_tensor(p4[:, 0], p4[:, 0], p4[:, 1], ALU.add)
                dve.tensor_tensor(p4[:, 2], p4[:, 2], p4[:, 3], ALU.subtract).then_inc(s5_link, 1)
                dve.wait_ge(s5_link, i * 2 + 1)
                for s in range(4):
                    mag = par[:, 4, bass.ds(i * 4 + s, 1)].to_broadcast([P, T])
                    for part, dst in ((0, r_re), (2, r_im)):
                        last = dve.tensor_tensor_scan(dst[:, s, :], mag, p4[:, part, s, :], 0.0, ALU.mult, ALU.add)
                last.then_inc(s5_link, 1)
                dve.wait_ge(s5_link, i * 2 + 2)
                dve.wait_ge(s5_y, i + 1)
                dve.tensor_tensor(q4[:, 0], r_re[:], cos, ALU.mult)
                dve.tensor_tensor(q4[:, 1], r_im[:], sin, ALU.mult)
                dve.tensor_tensor(q4[:, 2], r_re[:], sin, ALU.mult)
                dve.tensor_tensor(q4[:, 3], r_im[:], cos, ALU.mult).then_inc(s5_q, 1)
                if behind:
                    s5_skip(i - 1)

            def s5_skip(i):
                dve.wait_ge(s5_y, i + 2)
                u = uT[:, bass.ds(i, 1), :].rearrange("p a t -> p (a t)")
                dve.scalar_tensor_tensor(u, u, gains[:, GAINS.index("skip"), bass.ds(i, 1)], ps[:, 5, 0:T],
                                         ALU.mult, ALU.add).then_inc(s5_z, 1)

            s5_round(0, 0)
            s5_states(0, 0, behind=False)
            with dve.Fori(0, KT // 2 - 1) as n:
                for j in range(2):
                    s5_states(n * 2 + (j + 1), 1 - j)
            s5_states(KT - 1, 1, ahead=False)
            s5_skip(KT - 1)
            for n in range(4):
                dve.wait_ge(s5_gh, n + 1)
                dve.tensor_tensor(xl[:, 4 * n:4 * n + 4, :], uT[:, 4 * n:4 * n + 4, :],
                                  xh[:, 4 * n:4 * n + 4, :].bitcast(F32), ALU.subtract).then_inc(s5_gl, 1)

            def glu(q, j):
                if j == 0:
                    return
                g = G["glu"]
                product(g, q, j)
                dve.wait_ge(evac_done, g.evacuated(q))
                cols = x[:, :, bass.ds((q - 1) * (PANEL // 2), PANEL)]
                dve.tensor_tensor(cols, cols, hbuf[:], ALU.add).then_inc(glu_added, 1)

            panels(G["glu"], glu)

            def ffn(layer):
                g, x0 = G[f"gu{layer}"], (0, 27)[layer]
                def one(i, j, first=False):
                    q = i * 2 + j
                    split(g, q, range(2))
                    if j == 0 and not first:
                        dve.wait_ge(x_tr, i * 2 + (2 * x0))
                        product(g, q - 1, 1)
                    split(g, q, range(2, g.chunks))
                    if j == 0 and not first:
                        hidden_lo(i + (11 * layer - 1), i - 1)
                n = g.panels // 2
                one(0, 0, True)
                one(0, 1)
                with dve.Fori(1, n) as i:
                    for j in range(2):
                        one(i, j)
                dve.wait_ge(x_tr, 2 * n + 2 * x0)
                product(g, 2 * n - 1, 1)
                hidden_lo(11 * layer + n - 1, n - 1)
                panels(G[f"dn{layer}"], lambda q, j: residual(G[f"dn{layer}"], q, j))

            norm(N_FFN0)
            turn_lo(T_FFN0)
            ffn(0)
            norm(N_KV)
            turn_lo(T_KV)

            def head_rms(g, q, n, xi):
                dve.wait_ge(evac_done, g.evacuated(q))
                dve.wait_ge(x_tr, xi * 2 + 2)
                by_head = lambda t: t[:].rearrange("p b (h e) -> p b h e", e=DH)
                dve.tensor_tensor(hbuf[:], gbuf[:], gbuf[:], ALU.mult).then_inc(head_link, 1)
                dve.wait_ge(head_link, n * 3 + 1)
                dve.tensor_reduce(hssq[:, 0], by_head(hbuf), AX.X, ALU.add).then_inc(head_link, 1)
                dve.wait_ge(head_link, n * 3 + 2)
                dve.tensor_scalar(hssq[:, 0], hssq[:, 0], 1.0 / DH, EPS, ALU.mult, ALU.add).then_inc(hd_ms, 1)
                dve.wait_ge(hd_sd, n + 1)
                dve.reciprocal(hssq[:, 2], hssq[:, 1]).then_inc(head_link, 1)
                dve.wait_ge(head_link, n * 3 + 3)
                dve.tensor_tensor(by_head(hbuf), by_head(gbuf), hssq[:, 2].unsqueeze(3).to_broadcast([P, TB, 4, DH]),
                                  ALU.mult).then_inc(head_norm, 1)

            panels(G["k"], lambda q, j: head_rms(G["k"], q, q, q + 11))
            panels(G["v"], lambda q, j: None)
            turn_lo(T_MIX1)
            panels(G["q"], lambda q, j: head_rms(G["q"], q, q + 4, q + 15))
            dve.wait_ge(at_in, 64)
            dve.tensor_scalar(gqk[:], qkg[:, 0:NG], qkg[:, NG:NG + 1], DH ** -0.5, ALU.mult, ALU.mult).then_inc(gqk_ready, 1)

            def at_a(h, j):
                dve.wait_ge(at_sc, h + 1)
                for g in range(NG):
                    for lo, width, src in ((g * P, P, ps[:, 3 * j, g * P:g * P + P]),
                                           (3 * P + g * T, T, ps[:, 3 * j + 1 + g // 2, (g % 2) * T:(g % 2) * T + T])):
                        last = dve.scalar_tensor_tensor(score[:, j, lo:lo + width], dist[:, lo:lo + width],
                                                        slope[:, bass.ds(h, 1), g:g + 1].rearrange("p a b -> p (a b)"),
                                                        src, ALU.mult, ALU.add)
                last.then_inc(at_bias, 1)
                dve.wait_ge(at_bias, h + 3)
                dve.tensor_reduce(negm[:, 2 * j:2 * j + 1], score[:, j, 0:384], AX.X, ALU.max, negate=True)
                dve.tensor_reduce(negm[:, 2 * j + 1:2 * j + 2], score[:, j, 384:1152], AX.X, ALU.max,
                                  negate=True).then_inc(at_max, 1)

            def at_b(h, j):
                dve.wait_ge(at_exp, h + 1)
                s, o = score[:, j], wsum[:, j]
                dve.reciprocal(rden[:, 2 * j:2 * j + 2], den[:, 2 * j:2 * j + 2])
                dve.tensor_tensor(o[:, 0:P], s[:, 0:P], s[:, P:2 * P], ALU.add)
                dve.tensor_tensor(o[:, P:3 * P], s[:, 384:384 + T], s[:, 384 + T:384 + 2 * T], ALU.add).then_inc(dve_link, 1)
                dve.wait_ge(dve_link, h * 2 + (at_base + 1))
                dve.tensor_tensor(o[:, 0:P], o[:, 0:P], s[:, 2 * P:3 * P], ALU.add)
                dve.tensor_tensor(o[:, P:3 * P], o[:, P:3 * P], s[:, 384 + 2 * T:1152], ALU.add).then_inc(dve_link, 1)
                dve.wait_ge(dve_link, h * 2 + (at_base + 2))
                dve.tensor_scalar(o[:, 0:P], o[:, 0:P], rden[:, 2 * j:2 * j + 1], None, ALU.mult)
                dve.tensor_scalar(o[:, P:3 * P], o[:, P:3 * P], rden[:, 2 * j + 1:2 * j + 2], None,
                                  ALU.mult).then_inc(at_w, 1)

            def at_c(h, j):
                dve.wait_ge(at_oh, h + 1)
                flat = lambda t: t[:, bass.ds(h, 1), :].rearrange("p a t -> p (a t)")
                dve.tensor_tensor(flat(xl), ps[:, 7, 0:T], flat(xh).bitcast(F32), ALU.subtract).then_inc(at_o, 1)

            at_base = dl.n
            heads_in_turn(dve, at_a, at_b, at_c)
            dl.n += 2 * HEADS
            panels(G["o"], lambda q, j: residual(G["o"], q, j))
            norm(N_FFN1)
            turn_lo(T_FFN1)
            ffn(1)

            dve.wait_ge(b2_in, 64)
            link(dve.tensor_copy(pos_f, pos_i[:]))
            for b in range(TB):
                link(dve.tensor_scalar(rope_t[:, 2, b], inv[:], pos_f[:, b:b + 1], None, ALU.mult))
            turns_of(rope_t[:, 0], rope_t[:, 2], rope_t[:, 3]).then_inc(rope_ang, 1)

            for l in range(NLAYER2):
                lam_init = 0.8 - 0.6 * math.exp(-0.3 * l)
                dve.wait_ge(b2l_in, 16 * 5 * (l + 1))
                link(dve.tensor_tensor(lam_p[:], lam_v[:, 0:4:2, :], lam_v[:, 1:4:2, :], ALU.mult))
                dve.tensor_reduce(lam_e, lam_p[:], AX.X, ALU.add).then_inc(lam_dot, 1)
                dve.wait_ge(lam_exp, l + 1)
                link(dve.tensor_tensor(lam_col, lam_e[:, 0:1], lam_e[:, 1:2], ALU.subtract))
                link(dve.tensor_scalar(lam_col, lam_col, lam_init, None, ALU.add))
                link(dve.tensor_scalar(sub_g[:], sub_g[:], 1.0 - lam_init, None, ALU.mult))
                norm(N_PRE[l])
                turn_lo(T_PRE[l])
                panels(G[f"in{l}"], lambda q, j: None)

                dve.wait_ge(evac_done, G[f"in{l}"].all_evacuated)
                dve.wait_ge(rope_ready, 1)
                for b in range(TB):
                    for col, n, half, first in ((C_RQ, 2 * RH, DH // 2, 0), (C_DQ, 4 * DIFH, DH // 4, 64)):
                        v = proj[:, b, col:col + n * 2 * half].rearrange("p (h s e) -> p h s e", s=2, e=half)
                        x1, x2 = v[:, :, 0, :], v[:, :, 1, :]
                        t = [rope_a[:, k, 0:n * half].rearrange("p (h e) -> p h e", e=half) for k in range(4)]
                        cos, sin = (rope_cs[:, k, b, first:first + half].unsqueeze(1).to_broadcast([P, n, half])
                                    for k in range(2))
                        dve.tensor_tensor(t[0], x1, cos, ALU.mult)
                        dve.tensor_tensor(t[1], x2, sin, ALU.mult)
                        dve.tensor_tensor(t[2], x2, cos, ALU.mult)
                        link(dve.tensor_tensor(t[3], x1, sin, ALU.mult))
                        dve.tensor_tensor(x1, t[0], t[1], ALU.subtract)
                        last = dve.tensor_tensor(x2, t[2], t[3], ALU.add)
                        if b == TB - 1 and first:
                            last.then_inc(rope_done, 1)
                        else:
                            link(last)

                for h in range(RH):
                    dve.wait_ge(r_s, RH * l + h + 1)
                    if h >= 2:
                        dve.wait_ge(r_o, RH * l + h - 1)
                    dve.tensor_tensor(ra[:, h % 2, :], ps[:, h % 2, 0:384], decay[:, h, :], ALU.mult).then_inc(r_a, 1)

                def d_a(h):
                    dve.wait_ge(d_s, DIFH * l + h + 1)
                    for m in range(2):
                        last = dve.scalar_tensor_tensor(ds[:, h % 2, m, :], ps[:, 4 + 2 * (h % 2) + m, 0:384],
                                                        (DH // 2) ** -0.5, causal[:], ALU.mult, ALU.add)
                    last.then_inc(d_m, 1)
                    dve.wait_ge(d_m, DIFH * l + h + 1)
                    for m in range(2):
                        for b, (lo, hi) in enumerate(((0, 128), (128, 384))):
                            last = dve.tensor_reduce(dnegm[:, 2 * m + b:2 * m + b + 1], ds[:, h % 2, m, lo:hi],
                                                     AX.X, ALU.max, negate=True)
                    last.then_inc(d_max, 1)

                def d_b(h):
                    dve.wait_ge(d_exp, DIFH * l + h + 1)
                    link(dve.reciprocal(drden, dden))
                    dve.tensor_scalar(dlr, drden[:, 2:4], lam_col, None, ALU.mult)
                    for b, (lo, hi) in enumerate(((0, 128), (128, 384))):
                        last = dve.tensor_scalar(ds[:, h % 2, 0, lo:hi], ds[:, h % 2, 0, lo:hi], drden[:, b:b + 1],
                                                 None, ALU.mult)
                    link(last)
                    for b, (lo, hi) in enumerate(((0, 128), (128, 384))):
                        last = dve.tensor_scalar(ds[:, h % 2, 1, lo:hi], ds[:, h % 2, 1, lo:hi], dlr[:, b:b + 1],
                                                 None, ALU.mult)
                    link(last)
                    if h:
                        dve.wait_ge(d_pt, DIFH * l + h)
                    dve.tensor_tensor(dw[:], ds[:, h % 2, 0, :], ds[:, h % 2, 1, :], ALU.subtract).then_inc(d_w, 1)

                for h in range(DIFH):
                    d_a(h)
                    d_b(h)

                mixed = tok[:, :, 0:RW + DW]
                by_head = lambda t: t.rearrange("p b (h e) -> p b h e", e=DH)
                dve.wait_ge(r_ev, RH * (l + 1))
                dve.wait_ge(d_ev, DIFH * (l + 1))
                link(dve.tensor_tensor(sq2[:], mixed, mixed, ALU.mult))
                heads2 = hs2.rearrange("p (b h) -> p b h", b=TB)
                link(dve.tensor_reduce(heads2, by_head(sq2[:]), AX.X, ALU.add))
                dve.tensor_scalar(hs2, hs2, 1.0 / DH, EPS, ALU.mult, ALU.add).then_inc(h_ms, 1)
                dve.wait_ge(h_sd, l + 1)
                link(dve.reciprocal(hs2, hs2_sd))
                for b in range(TB):
                    last = dve.tensor_tensor(by_head(mixed)[:, b], by_head(mixed)[:, b],
                                             heads2[:, b].unsqueeze(2).to_broadcast([P, RH + DIFH, DH]), ALU.mult)
                last.then_inc(h_done, 1)
                dve.wait_ge(h_done, 5 * l + 1)
                for b in range(TB):
                    dif = tok[:, b, RW:RW + DW].rearrange("p (h e) -> p h e", e=DH)
                    last = dve.tensor_tensor(dif, dif, sub_g[:].unsqueeze(1).to_broadcast([P, DIFH, DH]), ALU.mult)
                last.then_inc(h_done, 1)
                dve.wait_ge(gates_done, 3 * (l + 1))
                dve.wait_ge(h_done, 5 * l + 2)
                dve.tensor_tensor(tok[:, :, 0:RW], tok[:, :, 0:RW], proj[:, :, C_RG:C_RG + RW], ALU.mult).then_inc(h_done, 1)
                dve.tensor_tensor(tok[:, :, RW:RW + DW], tok[:, :, RW:RW + DW], proj[:, :, C_DG:C_DG + DW],
                                  ALU.mult).then_inc(h_done, 1)
                dve.memset(lru_x[:, :, 0:3], 0.0).then_inc(h_done, 1)

                dve.wait_ge(l_par, l + 1)
                z = lru_p[:, 7, :]
                tt = lambda n: lru_t[:, n, :]
                dve.scalar_tensor_tensor(tt(0), z, -1.0, z, ALU.mult, ALU.max).then_inc(l_e, 1)
                dve.wait_ge(l_e2, l + 1)
                link(dve.tensor_scalar(tt(2), tt(1), 2.0, None, ALU.add))
                link(dve.reciprocal(tt(2), tt(2)))
                link(dve.tensor_tensor(tt(2), tt(2), tt(1), ALU.mult))
                link(dve.tensor_tensor(tt(3), tt(2), tt(2), ALU.mult))
                link(dve.tensor_scalar(tt(4), tt(3), 1.0 / 19, None, ALU.mult))
                for k in range(17, 1, -2):
                    link(dve.scalar_tensor_tensor(tt(4), tt(4), 1.0 / k, tt(3), ALU.add, ALU.mult))
                link(dve.scalar_tensor_tensor(tt(4), tt(4), 1.0, tt(2), ALU.add, ALU.mult))
                link(dve.tensor_scalar(tt(5), z, 0.0, 8.0, ALU.min, ALU.mult))
                link(dve.scalar_tensor_tensor(tt(5), tt(4), -16.0, tt(5), ALU.mult, ALU.add))

                dve.wait_ge(l_x, 4 * (l + 1))
                dve.wait_ge(h_done, 5 * l + 5)
                for k in range(4):
                    for n in range(LB):
                        src = lru_x[:, n, k:k + T]
                        if k == 0:
                            last = dve.tensor_scalar(lru_c[:, n, :], src, lru_p[:, 0, n:n + 1], lru_p[:, 4, n:n + 1],
                                                     ALU.mult, ALU.add)
                        else:
                            last = dve.scalar_tensor_tensor(lru_c[:, n, :], src, lru_p[:, k, n:n + 1],
                                                            lru_c[:, n, :], ALU.mult, ALU.add)
                    if k < 3:
                        link(last)
                last.then_inc(l_conv, 1)
                dve.wait_ge(l_sig, LB * (l + 1))
                dve.tensor_tensor(lru_r[:], lru_r[:], tt(5).unsqueeze(2).to_broadcast([LBW, LB, T]), ALU.mult).then_inc(l_la, 1)
                link(dve.tensor_tensor(lru_i[:], lru_i[:], lru_c[:], ALU.mult))
                dve.wait_ge(l_a, 3 * l + 3)
                dve.scalar_tensor_tensor(lru_r[:], lru_r[:], 1.0, lru_y[:], ALU.add, ALU.mult).then_inc(l_m, 1)
                dve.wait_ge(l_mq, l + 1)
                link(dve.tensor_tensor(lru_i[:], lru_i[:], lru_y[:], ALU.mult))
                for n in range(LB):
                    last = dve.tensor_tensor_scan(lru_y[:, n, :], lru_x[:, n, 0:T], lru_i[:, n, :], 0.0, ALU.mult, ALU.add)
                last.then_inc(l_h, 1)
                for u in range(4):
                    b, half = u // 2, u % 2
                    dve.wait_ge(l_ht, 4 * l + u + 1)
                    c0 = half * 4 * LBW
                    dve.tensor_tensor(tok[:, b, RW + DW + c0:RW + DW + c0 + 384], ps[:, 4 + u, 0:384],
                                      proj[:, b, C_LG + c0:C_LG + c0 + 384], ALU.mult).then_inc(mix_done, 1)

                turn_lo(T_OUT[l])
                panels(G[f"out{l}"], lambda q, j: None)
                root_mean(y_ssq, 2 * l + 2, y_ms, (y_sd, l + 1))
                dve.wait_ge(pg_in, 16 * (l + 1))
                for b in range(TB):
                    last = dve.scalar_tensor_tensor(tok[:, b, :], tok[:, b, :], rstd[:, b:b + 1], post_g[:],
                                                    ALU.mult, ALU.mult)
                link(last)
                dve.wait_ge(evac_done, G[f"out{l}"].all_evacuated)
                for b in range(TB):
                    dve.tensor_tensor(x[:, b, :], x[:, b, :], tok[:, b, :], ALU.add).then_inc(res_added, 1)


def tables():
    t = np.arange(T)
    c = {"ident": np.eye(P, dtype=np.float32)}
    c["tval"] = np.broadcast_to(t - P, (P, T)).astype(np.float32)
    rows = np.arange(P)[:, None]
    c["parity"] = np.concatenate([(rows // 16) % 2 == np.arange(2), rows // 64 == np.arange(2)], axis=1).astype(np.float32)
    d = t[:, None] - t[None, :]
    keep = [(d >= 0) & (d % dil == 0) & (d <= win) for win, dil in ((128, 1), (512, 4), (2048, 16))]
    far = [np.where(k, d, BIG).astype(np.float32) for k in keep]
    c["dist"] = np.concatenate([f[0:P, 0:P] for f in far] + [f[P:T, :] for f in far], axis=1)
    s = np.exp2(-8.0 * np.arange(1, NG * HEADS + 1) / (NG * HEADS)).reshape(HEADS, NG)
    c["slope"] = np.broadcast_to(-s, (P, HEADS, NG)).astype(np.float32)
    mask = np.where(d >= 0, 0.0, -BIG)
    c["causal"] = np.concatenate([mask[0:P, 0:P], mask[P:T, :]], axis=1).astype(np.float32)
    log_g = np.log1p(-np.exp2(-5.0 - np.arange(RH)))
    full = np.where(d >= 0, np.exp(np.maximum(d, 0)[None] * log_g[:, None, None]), 0.0) * DH ** -0.5
    full = full.transpose(2, 0, 1)
    c["decay"] = np.concatenate([full[0:P], full[P:T, :, P:T]], axis=2).astype(np.float32)
    inv_r = 1.0 / (10000.0 ** np.linspace(0.0, 1.0, DH // 2))
    inv_d = 1.0 / (10000.0 ** (np.arange(0, DH // 2, 2) / (DH // 2)))
    c["inv"] = np.broadcast_to(np.concatenate([inv_r, inv_d]), (P, 96)).astype(np.float32)
    return {k: np.ascontiguousarray(v) for k, v in c.items()}


def kernel(**inputs):
    import concourse.bacc as bacc
    from concourse.bass_utils import run_bass_kernel_spmd

    nc = bacc.Bacc("TRN2", target_bir_lowering=False, num_devices=1)
    arrays, w, c = {}, {}, {}
    for group, source, prefix in ((w, inputs, "in"), (c, tables(), "const")):
        for name, a in source.items():
            a = np.ascontiguousarray(a)
            key = f"{prefix}_{name}"
            arrays[key] = a
            group[name] = nc.dram_tensor(key, a.shape, mybir.dt.from_np(a.dtype), kind="ExternalInput").ap()
    out = nc.dram_tensor("out_x", (1, T, D), F32, kind="ExternalOutput").ap()
    with nc.allow_non_contiguous_dma(reason="a few small parameter vectors and tables go to columns"):
        program(nc, w, c, out)
    r = run_bass_kernel_spmd(nc, [arrays], core_ids=[0])
    return r.results[0]["out_x"]
```

```python
import math
from contextlib import ExitStack

import numpy as np

import concourse.bass as bass
from concourse import mybir

F32 = mybir.dt.float32
F32R = mybir.dt.float32r
BF16 = mybir.dt.bfloat16
I32 = mybir.dt.int32
ALU = mybir.AluOpType
ACT = mybir.ActivationFunctionType
AX = mybir.AxisListType

P = 128
T = 256
TB = T // P
D = 2048
KT = D // P
DFF = 5632
EPS = 1e-6
PANEL = 512
CK = 2
RAW = 8
AHEAD = 6
SPLIT = 2
HEADS, DH = 16, 128
NG = 3
RH, DIFH = 6, 4
RW, DW, LW = RH * DH, DIFH * DH, 768
LB, LBW = 8, 96
DIN = 4 * RW + 4 * DW + 2 * LW
C_RQ, C_RK, C_RV, C_RG = 0, RW, 2 * RW, 3 * RW
C_DQ, C_DK, C_DV, C_DG = 4 * RW, 4 * RW + DW, 4 * RW + 2 * DW, 4 * RW + 3 * DW
C_LX, C_LG = 4 * RW + 4 * DW, 4 * RW + 4 * DW + LW
NLAYER2 = 2
BIG = 1.0e30
MAGIC = 12582912.0
TWO_PI_BELOW = 6.2831850
C1 = 6.28125
C2 = float(np.float32(round((2 * math.pi - C1) * 2**21) / 2**21))
C3 = 2 * math.pi - C1 - C2
KB = 1024


class Gemm:

    def __init__(self, name, w, chunks, panels, cols, chunk0, panel0, slot_uses):
        self.name, self.w, self.chunks, self.panels, self.cols = name, w, chunks, panels, cols
        self.chunk0, self.panel0, self.slot_uses = chunk0, panel0, list(slot_uses)
        self.first = int(name == "glu")
        self.per = [chunks // RAW + (s < chunks % RAW) for s in range(RAW)]

    def chunk(self, q, k):
        return q * self.chunks + (self.chunk0 + k)

    def raw_count(self, q, k):
        s = k % RAW
        return q * (16 * self.per[s]) + 16 * (self.slot_uses[s] + k // RAW + 1)

    def done(self, q):
        return (q + 1) * self.chunks + (self.chunk0 + SPLIT)

    def evacuated(self, q):
        return q + (self.panel0 + 3)

    @property
    def all_evacuated(self):
        return self.panel0 + self.panels + 2


def plan(w):
    plain = lambda i, j: i * (2 * PANEL) + j * PANEL
    table = [
        ("glu", w["w_glu"][0], D, 8, lambda i, j: i * PANEL + ((1 - j) * D - PANEL)),
        ("gu0", w["w_gate_up"][0], D, 22, lambda i, j: i * PANEL + j * DFF),
        ("dn0", w["w_down"][0], DFF, 4, plain),
        ("k", w["w_kv"], D, 4, plain),
        ("v", w["w_kv"], D, 4, lambda i, j: i * (2 * PANEL) + (j * PANEL + D)),
        ("q", w["w_q"][0], D, 12, plain),
        ("o", w["w_o"][0], D, 4, plain),
        ("gu1", w["w_gate_up"][1], D, 22, lambda i, j: i * PANEL + j * DFF),
        ("dn1", w["w_down"][1], DFF, 4, plain),
    ]
    for l in range(NLAYER2):
        table += [(f"in{l}", w["w_in_2"][l], D, 13, plain), (f"out{l}", w["w_out_2"][l], D, 4, plain)]
    gemms, chunk0, panel0, uses = {}, 0, 0, [0] * RAW
    for name, ap, k, panels, cols in table:
        g = Gemm(name, ap, k // (P * CK), panels, cols, chunk0, panel0, uses)
        gemms[name] = g
        chunk0 += g.chunks * panels
        panel0 += panels
        uses = [u + n * panels for u, n in zip(uses, g.per)]
    return gemms


def in_turn(eng, steps, count=HEADS):
    def edge(n):
        for offset, step in steps:
            if 0 <= n + offset < count:
                step(n + offset, (n + offset) % 2)

    for n in range(-3, 2):
        edge(n)
    with eng.Fori(1, count // 2 - 2) as i:
        for j in range(2):
            for offset, step in steps:
                step(i * 2 + (j + offset), (j + offset) % 2)
    for n in range(count - 4, count + 2):
        edge(n)


class Links:

    def __init__(self, eng, sem):
        self.eng, self.sem, self.n = eng, sem, 0

    def link(self, instruction):
        self.n += 1
        instruction.then_inc(self.sem, 1)
        self.eng.wait_ge(self.sem, self.n)


GAINS = ["mix0", "ffn0", "kv", "mix1", "ffn1", "pre0", "pre1", "skip"]
TURNS = ["mix0", "ffn0", "kv", "mix1", "ffn1", "pre0", None, "pre1", None]
T_MIX0, T_FFN0, T_KV, T_MIX1, T_FFN1 = range(5)
T_PRE, T_OUT = (5, 7), (6, 8)
N_MIX0, N_FFN0, N_KV, N_FFN1 = range(4)
N_PRE = (4, 5)
NORM_OF = {T_FFN0: N_FFN0, T_KV: N_KV, T_FFN1: N_FFN1, T_PRE[0]: N_PRE[0], T_PRE[1]: N_PRE[1]}


def program(nc, w, c, out):
    G = plan(w)
    with ExitStack() as ctx:
        def sb(name, shape, dt=F32):
            return ctx.enter_context(nc.sbuf_tensor(name, shape, dt))

        def sem(name):
            return ctx.enter_context(nc.semaphore(name))

        x = sb("x_res", [P, TB, D])
        raw = sb("raw", [P, RAW, CK, PANEL])
        whi = sb("w_hi", [P, SPLIT, CK, PANEL], F32R)
        wlo = sb("w_lo", [P, SPLIT, CK, PANEL], F32R)
        ident = sb("ident", [P, P])
        gains = sb("gains", [P, len(GAINS), KT])
        half_pi = sb("half_pi", [P, 1])
        ssq = sb("ssq", [P, TB])
        msq = sb("msq", [P, TB])
        sdev = sb("sdev", [P, TB])
        rstd = sb("rstd", [P, TB])
        y_sums = sb("y_sums", [P, TB, D // PANEL])
        ps = ctx.enter_context(nc.psum_tensor("ps", [P, 8, 512], F32))

        def at(kb, name, shape, dt=F32):
            with ExitStack() as scope:
                if kb:
                    scope.enter_context(nc.sbuf_tensor(f"before_{name}", [P, int(kb * KB // 4)], F32))
                return scope.enter_context(nc.sbuf_tensor(name, shape, dt))

        xh = at(0, "x_hi", [P, KT, T], F32R)
        xl = at(16, "x_lo", [P, KT, T], F32R)
        gbuf = at(32, "gbuf", [P, TB, PANEL])
        hbuf = at(36, "hbuf", [P, TB, PANEL])
        junk = at(32, "junk", [P, D], BF16)
        tok = at(40, "tok", [P, TB, D])
        hh = at(40, "h_hi", [P, DFF // P, T], F32R)
        hl = at(84, "h_lo", [P, DFF // P, T], F32R)

        raw_ready = [sem(f"raw_ready{s}") for s in range(RAW)]
        hi_done = sem("hi_done")
        lo_done = sem("lo_done")
        chunk_used = sem("chunk_used")
        evac_done = sem("evac_done")
        glu_added = sem("glu_added")
        x_tr = sem("x_tr")
        x_hi_done = sem("x_hi_done")
        x_done = sem("x_done")
        head_norm = sem("head_norm")
        hd_ms = sem("hd_ms")
        hd_sd = sem("hd_sd")
        nrm_ssq, nrm_ms, nrm_sd, xn_ready = sem("nrm_ssq"), sem("nrm_ms"), sem("nrm_sd"), sem("xn_ready")
        tr_ready, tr_hi, tr_lo = sem("tr_ready"), sem("tr_hi"), sem("tr_lo")
        head_link, s5_link = sem("head_link"), sem("s5_link")
        x_in, ident_in, par_in, out_done = sem("x_in"), sem("ident_in"), sem("par_in"), sem("out_done")
        gain_tr, gain_ready, const_ready = sem("gain_tr"), sem("gain_ready"), sem("const_ready")
        dve_link, act_link, pool_link, pe_link = sem("dve_link"), sem("act_link"), sem("pool_link"), sem("pe_link")

        q4 = at(0, "s5_q4", [P, 4, 4, T])
        r_re = at(16, "s5_r_re", [P, 4, T])
        r_im = at(20, "s5_r_im", [P, 4, T])
        cs = at(24, "s5_cs", [P, 2, 2, 4, T])
        p4 = at(40, "s5_p4", [P, 4, 4, T])
        uT = at(56, "s5_uT", [P, KT, T])
        bb_re = at(72, "s5_bb_re", [P, 64, 16])
        bb_im = at(76, "s5_bb_im", [P, 64, 16])
        c_re = at(80, "s5_c_re", [P, KT, 64])
        c_im = at(84, "s5_c_im", [P, KT, 64])
        turn = at(88, "s5_turn", [P, 2, 4, T])
        whole = at(96, "s5_whole", [P, 4, T])
        tval = at(100, "s5_tval", [P, T])
        us = at(131, "s5_us", [P, 2, T])
        bx = at(102, "s5_bx", [P, 2, 4, 2, 16])
        cx = at(103, "s5_cx", [P, 2, 2, 64])
        bt = at(104, "s5_bt", [P, 2, 2, P])
        ct3 = at(128, "s5_ct3", [P, 2, 3, P])
        b_re = at(107, "s5_b_re", [P, 64, 16])
        b_im = at(111, "s5_b_im", [P, 64, 16])
        par = at(115, "s5_par", [P, 20, 64])
        a_rows = at(121, "s5_a_rows", [P, P])
        dt_rows = at(121.5, "s5_dt_rows", [64, 2])
        dt_wide = at(122, "s5_dt_wide", [64, 2, 64])
        parity = at(122.5, "s5_parity", [P, 4])
        gain_rows = at(123, "gain_rows", [P, P])
        absf = at(124, "s5_absf", [P, 4, T])
        s5_in, s5_bc_in = sem("s5_in"), sem("s5_bc_in")
        s5_a_tr, s5_dt_wide, s5_dt_tr = sem("s5_a_tr"), sem("s5_dt_wide"), sem("s5_dt_tr")
        s5_log, s5_exp = sem("s5_log"), sem("s5_exp")
        s5_par = sem("s5_par")
        s5_stage = sem("s5_stage")
        s5_tr = sem("s5_tr")
        s5_mats = sem("s5_mats")
        s5_b = sem("s5_b")
        s5_rot = sem("s5_rot")
        s5_add = sem("s5_add")
        s5_re = sem("s5_re")
        s5_turn, s5_whole, s5_frac = sem("s5_turn"), sem("s5_whole"), sem("s5_frac")
        s5_cs = sem("s5_cs")
        s5_q = sem("s5_q")
        s5_qp = sem("s5_qp")
        s5_y = sem("s5_y")
        s5_z = sem("s5_z")
        s5_g, s5_gh, s5_gl = sem("s5_g"), sem("s5_gh"), sem("s5_gl")

        qT = at(40, "qT", [P, NG * HEADS, T])
        kT = at(88, "kT", [P, HEADS, T])
        vt = at(104, "v_tok", [P, TB, HEADS * DH])
        dist = at(120, "dist", [P, NG * 128 + NG * 256])
        qst = at(124.5, "q_stage", [P, 2, NG, T])
        score = at(130.5, "score", [P, 2, 1152])
        wsum = at(32, "wsum", [P, 2, 384])
        wT = at(35, "wT", [P, 384])
        vst = at(36.5, "v_stage", [P, 2, TB, DH])
        slope = at(139.5, "slope", [P, HEADS, NG])
        at_small = at(139.75, "at_small", [P, 16])
        negm, den, rden = at_small[:, 0:4], at_small[:, 4:8], at_small[:, 8:12]
        qkg = at(140.25, "qk_gain", [P, 4])
        gqk = at(140.5, "gqk", [P, NG])
        hssq = at(139.875, "hssq", [P, 3, TB, 4])
        at_in, gqk_ready = sem("at_in"), sem("gqk_ready")
        at_sum, at_qs, at_vs, at_sc, at_bias, at_max = sem("at_sum"), sem("at_qs"), sem("at_vs"), sem("at_sc"), sem("at_bias"), sem("at_max")
        at_exp, at_w, at_pt, at_wt = sem("at_exp"), sem("at_w"), sem("at_pt"), sem("at_wt")
        at_pv, at_oh, at_o = sem("at_pv"), sem("at_oh"), sem("at_o")

        rope_a = at(0, "rope_a", [P, 4, 768])
        rT = at(12, "ret_T", [P, 2 * RH, T])
        dT = at(24, "dif_T", [P, 2 * DIFH, T])
        sq2 = at(0, "sq2", [P, TB, RW + DW])
        dw = at(32, "dif_w", [P, 384])
        dwT = at(33.5, "dif_wT", [P, 384])
        sub_g = at(141, "sub_g", [P, DH])
        lam_v = at(141.5, "lam_v", [P, 4, 64])
        lam_p = at(140, "lam_p", [P, 2, 64])
        proj = at(56, "proj", [P, TB, DIN])
        post_g = at(56, "post_g", [P, D])
        yg = at(64, "yg", [P, TB, D])
        decay = at(108, "decay", [P, RH, 384])
        rope_cs = at(117, "rope_cs", [P, 2, TB, 96])
        rope_t = at(118.5, "rope_t", [P, 4, TB, 96])
        pos_i = at(121.5, "pos_i", [P, TB], I32)
        inv = at(121.75, "inv_freq", [P, 96])
        causal = at(122.25, "causal", [P, 384])
        m2 = at(123.75, "m2_small", [P, 64])
        ra = at(124, "ret_a", [P, 2, 384])
        ds = at(127, "dif_s", [P, 2, 2, 384])
        lru_x = at(0, "lru_x", [LBW, LB, T + 3])
        lru_c = at(8.25, "lru_c", [LBW, LB, T])
        lru_i = at(16.25, "lru_i", [LBW, LB, T])
        lru_y = at(24.25, "lru_y", [LBW, LB, T])
        lru_r = at(124, "lru_r", [LBW, LB, T])
        lru_wa = at(133, "lru_wa", [LBW, LB, LBW])
        lru_wx = at(136, "lru_wx", [LBW, LB, LBW])
        lru_rows = at(139, "lru_rows", [64, LBW])
        lru_p = at(139.5, "lru_p", [LBW, 8, LB])
        lru_t = at(139.75, "lru_t", [LBW, 6, LB])
        pos_f, lam_e, lam_col = m2[:, 0:2], m2[:, 2:4], m2[:, 4:5]
        hs2, hs2_sd = m2[:, 5:25], m2[:, 25:45]
        dnegm, dden, drden, dlr = m2[:, 45:49], m2[:, 49:53], m2[:, 53:57], m2[:, 57:59]
        b2_in, b2l_in, lru_in, pg_in = sem("b2_in"), sem("b2l_in"), sem("lru_in"), sem("pg_in")
        rope_ang, rope_ready, rope_done = sem("rope_ang"), sem("rope_ready"), sem("rope_done")
        lam_dot, lam_exp = sem("lam_dot"), sem("lam_exp")
        gates_done = sem("gates_done")
        a_tr, a_ev = sem("a_tr"), sem("a_ev")
        r_s, r_a, r_o, r_ev = sem("r_s"), sem("r_a"), sem("r_o"), sem("r_ev")
        d_s, d_m, d_max, d_exp, d_w = sem("d_s"), sem("d_m"), sem("d_max"), sem("d_exp"), sem("d_w")
        d_pt, d_wt, d_o, d_ev = sem("d_pt"), sem("d_wt"), sem("d_o"), sem("d_ev")
        h_ms, h_sd, h_done = sem("h_ms"), sem("h_sd"), sem("h_done")
        l_row, l_par, l_e, l_e2, l_l8 = sem("l_row"), sem("l_par"), sem("l_e"), sem("l_e2"), sem("l_l8")
        l_xt, l_x, l_conv, l_g, l_sig = sem("l_xt"), sem("l_x"), sem("l_conv"), sem("l_g"), sem("l_sig")
        l_la, l_a, l_m, l_mq, l_h = sem("l_la"), sem("l_a"), sem("l_m"), sem("l_mq"), sem("l_h")
        l_ht, mix_done = sem("l_ht"), sem("mix_done")
        rstd_ready, y_ssq, y_ms, y_sd, res_added = sem("rstd_ready"), sem("y_ssq"), sem("y_ms"), sem("y_sd"), sem("res_added")

        yg_done = sem("yg_done")

        block = ctx.enter_context(nc.Block())

        def panel_ps(j):
            return ps[:, 2 * j:2 * j + 2, :]

        def x_written(v, n):
            return [(x_in, 32), (glu_added, n + 1), (evac_done, G["dn0"].evacuated(n)),
                    (evac_done, G["o"].evacuated(n)), (evac_done, G["dn1"].evacuated(n)),
                    (res_added, n + 1)][v]

        @block.sync
        def _(sp):
            sp.dma_start(a_rows[0:64, :], w["ssm_a_re"][0].rearrange("(j g) p -> j (g p)", g=2)).then_inc(s5_in, 16)
            sp.dma_start(a_rows[64:128, :], w["ssm_a_im"][0].rearrange("(j g) p -> j (g p)", g=2)).then_inc(s5_in, 16)
            sp.dma_start(dt_rows[:], w["ssm_log_dt"][0].rearrange("(j g) -> j g", g=2)).then_inc(s5_in, 16)
            sp.dma_start(tval[:], c["tval"]).then_inc(s5_in, 16)
            sp.dma_start(ident[:], c["ident"]).then_inc(ident_in, 16)
            for b in range(TB):
                sp.dma_start(x[:, b], w["x"][0, b * P:b * P + P]).then_inc(x_in, 16)
            rows = [w["mix_norm"][0], w["ffn_norm"][0], w["kv_norm"], w["mix_norm"][1], w["ffn_norm"][1],
                    w["pre_norm_g_2"][0], w["pre_norm_g_2"][1], w["ssm_d"][0]]
            for n, row in enumerate(rows):
                sp.dma_start(gain_rows[KT * n:KT * n + KT, :], row.rearrange("(k p) -> k p", p=P)).then_inc(par_in, 16)

            def load(g, q, col):
                for k in range(g.chunks):
                    sp.wait_ge(lo_done, g.chunk(q, k) + 1)
                    sp.dma_start(raw[:, k % RAW], g.w[k * CK * P:(k + 1) * CK * P, bass.ds(col, PANEL)]
                                 .rearrange("(t p) n -> p t n", p=P)).then_inc(raw_ready[k % RAW], 16)

            for g in G.values():
                with sp.Fori(g.first, g.panels // 2 + g.first) as i:
                    for j in range(2):
                        load(g, i * 2 + (j - 2 * g.first), g.cols(i, j))
                if g.panels % 2:
                    load(g, g.panels - 1, g.cols(g.panels // 2, 0))
            for n in range(D // PANEL):
                sp.wait_ge(res_added, 4 * (NLAYER2 - 1) + n + 1)
                cols = slice(n * PANEL, n * PANEL + PANEL)
                sp.dma_start(out[0, :, cols].rearrange("(b p) d -> p b d", p=P), x[:, :, cols]).then_inc(out_done, 16)
            sp.wait_ge(out_done, 16 * (D // PANEL))

        @block.gpsimd
        def _(pool):
            pl = Links(pool, pool_link)
            for start, n in ((s5_frac, 1), (s5_add, 1), (s5_qp, 2)):
                pool.nop().then_inc(start, n)
            pl.link(pool.memset(half_pi[:], math.pi / 2))
            pool.nop().then_inc(const_ready, 1)
            state_major = lambda a: a[0].rearrange("(j g) p h -> (g p) j h", g=2)
            pool.dma_start(parity[:], c["parity"]).then_inc(s5_bc_in, 16)
            pool.dma_start(b_re[:], state_major(w["ssm_b_re"])).then_inc(s5_bc_in, 16)
            pool.dma_start(b_im[:], state_major(w["ssm_b_im"])).then_inc(s5_bc_in, 16)
            pool.dma_start(c_re[:], w["ssm_c_re"][0].rearrange("g h p -> (g h) p")
                           .rearrange("(k q) p -> q k p", q=P)).then_inc(s5_bc_in, 16)
            pool.dma_start(c_im[:], w["ssm_c_im"][0].rearrange("g h p -> (g h) p")
                           .rearrange("(k q) p -> q k p", q=P)).then_inc(s5_bc_in, 16)
            pool.wait_ge(s5_bc_in, 16 * 5)
            pool.wait_ge(s5_par, 2)
            pool.wait_ge(tr_hi, 8)

            def s5_stages(i, j):
                pool.wait_ge(s5_tr, i + 1)
                for n, b in enumerate((bb_re, bb_im)):
                    pool.tensor_tensor(bx[:, n], b[:, bass.ds(i * 4, 4), :].unsqueeze(2).to_broadcast([P, 4, 2, 16]),
                                       parity[:, 2:4].unsqueeze(1).unsqueeze(3).to_broadcast([P, 4, 2, 16]), ALU.mult)
                for n, cc in enumerate((c_re, c_im)):
                    last = pool.tensor_tensor(cx[:, n], cc[:, bass.ds(i, 1), :].to_broadcast([P, 2, 64]),
                                              parity[:, 0:2].unsqueeze(2).to_broadcast([P, 2, 64]), ALU.mult)
                last.then_inc(s5_stage, 1)

            def s5_fraction(i, j):
                pool.wait_ge(s5_whole, i + 1)
                pool.tensor_tensor(turn[:, j], turn[:, j], whole[:], ALU.subtract).then_inc(s5_frac, 1)

            def s5_rotated_im(i, j):
                pool.wait_ge(s5_rot, i + 2)
                pool.tensor_tensor(p4[:, 2], p4[:, 2], p4[:, 3], ALU.subtract).then_inc(s5_add, 1)

            def s5_re_products(i, j):
                pool.wait_ge(s5_re, i + 1)
                pool.wait_ge(s5_y, i + 2)
                pool.tensor_tensor(q4[:, 2], r_re[:], cs[:, j, 1], ALU.mult)
                pool.tensor_tensor(q4[:, 0], r_re[:], cs[:, j, 0], ALU.mult).then_inc(s5_qp, 1)

            in_turn(pool, [(0, s5_rotated_im), (0, s5_re_products), (2, s5_fraction), (3, s5_stages)], KT)

            pool.wait_ge(x_done, 2 * 11 + 2)
            pool.wait_ge(evac_done, G["dn0"].all_evacuated)
            pool.dma_start(dist[:], c["dist"]).then_inc(at_in, 16)
            pool.dma_start(slope[:], c["slope"]).then_inc(at_in, 16)
            pool.dma_start(qkg[:, 0:NG], w["q_norm"][0].rearrange("g e -> e g"),
                           ).then_inc(at_in, 16)
            pool.dma_start(qkg[:, NG:NG + 1], w["k_norm"].rearrange("(e a) -> e a", a=1)).then_inc(at_in, 16)
            pool.wait_ge(gqk_ready, 1)
            pool.wait_ge(x_done, 2 * 27 + 2)
            pool.wait_ge(evac_done, G["q"].all_evacuated)

            def at_queries(h, j):
                pool.wait_ge(at_sc, h + 1)
                pool.tensor_tensor(qst[:, j], qT[:].rearrange("p (g h) t -> p g h t", g=NG)[:, :, bass.ds(h, 1), :]
                                   .rearrange("p g a t -> p g (a t)"),
                                   gqk[:].unsqueeze(2).to_broadcast([P, NG, T]), ALU.mult).then_inc(at_qs, 1)

            def at_values(h, j):
                pool.wait_ge(at_pv, h + 1)
                pool.tensor_copy(vst[:, j], vt[:, :, bass.ds(h * DH, DH)]).then_inc(at_vs, 1)

            def at_sums(h, j):
                pool.wait_ge(at_exp, h + 1)
                pool.wait_ge(at_pt, h + 1)
                s, o = score[:, j], wsum[:, j]
                group = lambda g: ((o[:, 0:P], s[:, g * P:g * P + P]),
                                   (o[:, P:3 * P], s[:, 384 + g * T:384 + g * T + T]))
                for (dst, first), (_, second) in zip(group(0), group(1)):
                    last = pool.tensor_tensor(dst, first, second, ALU.add)
                last.then_inc(at_sum, 1)
                pool.wait_ge(at_sum, h * 2 + 1)
                for dst, third in group(2):
                    last = pool.tensor_tensor(dst, dst, third, ALU.add)
                last.then_inc(at_sum, 1)

            in_turn(pool, [(3, at_queries), (0, at_sums), (0, at_values)])

            pool.wait_ge(evac_done, G["dn1"].all_evacuated)
            for dst, src in ((decay, c["decay"]), (inv, c["inv"]), (causal, c["causal"])):
                pool.dma_start(dst[:], src).then_inc(b2_in, 16)
            pool.dma_start(pos_i[:], w["positions_2"][0].rearrange("(b p) -> p b", p=P)).then_inc(b2_in, 16)
            for l in range(NLAYER2):
                if l:
                    pool.wait_ge(mix_done, 4 * l)
                for n, name in enumerate(("q1", "k1", "q2", "k2")):
                    pool.dma_start(lam_v[:, n, :], w[f"diff_lambda_{name}_2"][l].partition_broadcast(P)).then_inc(b2l_in, 16)
                pool.dma_start(sub_g[:], w["diff_subln_g_2"][l].partition_broadcast(P)).then_inc(b2l_in, 16)
                pool.dma_start(lru_rows[0:32, :], w["lru_conv_w_2"][l].rearrange("a (n p) -> (a n) p", p=LBW)).then_inc(lru_in, 16)
                for n, name in enumerate(("conv_b", "ba", "bx", "lambda")):
                    pool.dma_start(lru_rows[32 + 8 * n:40 + 8 * n, :], w[f"lru_{name}_2"][l]
                                   .rearrange("(n p) -> n p", p=LBW)).then_inc(lru_in, 16)
                pool.dma_start(lru_wa[:], w["lru_wa_2"][l].rearrange("n k j -> k n j")).then_inc(lru_in, 16)
                pool.dma_start(lru_wx[:], w["lru_wx_2"][l].rearrange("n k j -> k n j")).then_inc(lru_in, 16)
                pool.wait_ge(tr_ready, 8 * T_OUT[l] + 8)
                pool.wait_ge(mix_done, 4 * l + 4)
                pool.dma_start(post_g[:], w["post_norm_g_2"][l].partition_broadcast(P)).then_inc(pg_in, 16)

        @block.scalar
        def _(act):
            al = Links(act, act_link)

            def split(g, q, ks):
                for k in ks:
                    act.wait_ge(raw_ready[k % RAW], g.raw_count(q, k))
                    act.wait_ge(chunk_used, g.chunk(q, k) + 1)
                    act.activation(whi[:, k % SPLIT], raw[:, k % RAW], ACT.Copy).then_inc(hi_done, 1)

            def whole_panel(g, q):
                act.wait_ge(chunk_used, g.done(q))

            def gate(g, q, j, func, scaled=True):
                whole_panel(g, q)
                act.wait_ge(evac_done, g.evacuated(q) - 1)
                for b in range(TB):
                    last = act.activation(gbuf[:, b], ps[:, 2 * j + b, :], func,
                                          scale=rstd[:, b:b + 1] if scaled else 1.0)
                last.then_inc(evac_done, 1)

            def store(g, q, j, dst, scaled=False):
                whole_panel(g, q)
                for b in range(TB):
                    last = act.activation(dst[:, b], ps[:, 2 * j + b, :], ACT.Copy,
                                          scale=rstd[:, b:b + 1] if scaled else 1.0)
                last.then_inc(evac_done, 1)

            def raw_heads(g, q, j, n):
                whole_panel(g, q)
                act.wait_ge(head_norm, n + 1)
                for b in range(TB):
                    last = act.activation(gbuf[:, b], ps[:, 2 * j + b, :], ACT.Copy, scale=rstd[:, b:b + 1])
                last.then_inc(evac_done, 1)

            def head_sd(n):
                act.wait_ge(hd_ms, n + 1)
                act.activation(hssq[:, 1], hssq[:, 0], ACT.Sqrt).then_inc(hd_sd, 1)

            def hidden_hi(xi, i):
                for u in range(2):
                    act.wait_ge(x_tr, xi * 2 + (u + 3))
                    act.activation(hh[:, bass.ds(i * 4 + 2 * u, 2), :],
                                   ps[:, 4 + u, :].rearrange("p (a t) -> p a t", a=2), ACT.Copy).then_inc(x_hi_done, 1)

            def heads_T(xi, dst, h0):
                for u in range(2):
                    act.wait_ge(x_tr, xi * 2 + (u + 3))
                    act.activation(dst[:, bass.ds(h0 + 2 * u, 2), :],
                                   ps[:, 4 + u, :].rearrange("p (a t) -> p a t", a=2), ACT.Copy).then_inc(x_done, 1)

            def sums_of_squares(v):
                act.wait_ge(*x_written(v, 3))
                for b in range(TB):
                    if b:
                        act.wait_ge(nrm_ssq, 2 * v + b)
                    act.activation(junk[:], x[:, b, :], ACT.Square, accum_out=ssq[:, b:b + 1]).then_inc(nrm_ssq, 1)

            def root(v):
                act.wait_ge(nrm_ms, v + 1)
                act.activation(sdev[:], msq[:], ACT.Sqrt).then_inc(nrm_sd, 1)

            def turn_hi(v, u):
                gain = TURNS[v]
                act.wait_ge(tr_ready, 8 * v + u + 1)
                for kk in range(2):
                    kt = 2 * u + kk
                    src = ps[:, 4 + u % 4, kk * T:(kk + 1) * T]
                    dst = uT[:, kt, :] if v == T_MIX0 else xh[:, kt, :]
                    scale = 1.0 if gain is None else gains[:, GAINS.index(gain), kt:kt + 1]
                    last = act.activation(dst, src, ACT.Copy, scale=scale)
                last.then_inc(tr_hi, 1)

            def first_panel(g, pending=None, late=None, v=None, pending_mid=None):
                split(g, 0, [0])
                if pending:
                    pending()
                for k in range(g.chunks):
                    if v is not None:
                        turn_hi(v, k)
                    if k:
                        split(g, 0, [k])
                    if k == 5 and v in NORM_OF:
                        sums_of_squares(NORM_OF[v])
                    if k == 4 and pending_mid:
                        pending_mid()
                    if k == 6 and v in NORM_OF:
                        root(NORM_OF[v])
                    if k == 7 and late:
                        late()

            def panels(g, evac, after=None, pending=None, late=None, v=None, mid=None, pending_mid=None):
                first_panel(g, pending, late, v, pending_mid)
                if v in NORM_OF:
                    act.wait_ge(rstd_ready, NORM_OF[v])

                def one(q, j):
                    split(g, q, range(2))
                    evac(q - 1, 1 - j)
                    split(g, q, range(2, 5))
                    if mid:
                        mid(q - 1, 1 - j)
                    split(g, q, range(5, g.chunks))
                    if after:
                        after(q - 1, 1 - j)
                one(1, 1)
                pairs = g.panels // 2
                if pairs > 2:
                    with act.Fori(1, pairs) as i:
                        for j in range(2):
                            one(i * 2 + j, j)
                elif pairs == 2:
                    for j in range(2):
                        one(2 + j, j)
                last = 2 * pairs - 1
                if g.panels % 2:
                    one(g.panels - 1, 0)
                    last = g.panels - 1
                return (lambda: evac(last, last % 2)), (lambda: after(last, last % 2)) if after else None

            act.nop().then_inc(s5_mats, 1)
            act.nop().then_inc(s5_cs, 1)
            act.nop().then_inc(at_wt, 1)
            act.wait_ge(const_ready, 1)
            act.wait_ge(s5_in, 16 * 4)
            act.wait_ge(x_in, 32)
            for b in range(TB):
                if b:
                    act.wait_ge(nrm_ssq, b)
                act.activation(junk[:], x[:, b, :], ACT.Square, accum_out=ssq[:, b:b + 1]).then_inc(nrm_ssq, 1)
            act.wait_ge(s5_par, 1)
            act.activation(par[:, 10, :], par[:, 8, :], ACT.Sin, scale=TWO_PI_BELOW).then_inc(s5_exp, 1)
            al.link(act.activation(par[:, 9, :], par[:, 8, :], ACT.Abs))
            act.activation(par[:, 11, :], par[:, 9, :], ACT.Sin, bias=half_pi[:], scale=-TWO_PI_BELOW).then_inc(s5_exp, 1)
            root(N_MIX0)
            act.wait_ge(gain_tr, 1)
            act.activation(gains[:].rearrange("p a k -> p (a k)"), ps[:, 0, 0:P], ACT.Copy).then_inc(gain_ready, 1)
            act.wait_ge(gain_ready, 1)
            for u in range(8):
                turn_hi(T_MIX0, u)

            def s5_turns(i, j):
                for s in range(4):
                    last = act.activation(turn[:, j, s], tval[:], ACT.Copy, scale=par[:, 8, bass.ds(i * 4 + s, 1)])
                last.then_inc(s5_turn, 1)

            def s5_trig(i, j):
                act.wait_ge(s5_frac, i + 2)
                act.wait_ge(s5_q, i + 1)
                act.wait_ge(s5_qp, i + 1)
                act.activation(cs[:, j, 1], turn[:, j], ACT.Sin, scale=TWO_PI_BELOW)
                act.wait_ge(s5_cs, i + 1)
                act.activation(absf[:], turn[:, j], ACT.Abs).then_inc(act_link, 1)
                act.wait_ge(act_link, i + 2)
                act.activation(cs[:, j, 0], absf[:], ACT.Sin, bias=half_pi[:], scale=-TWO_PI_BELOW).then_inc(s5_cs, 1)

            def s5_matrices(i, j):
                act.wait_ge(s5_tr, i + 2)
                act.wait_ge(s5_b, i + 1)
                act.wait_ge(s5_y, i + 1)
                act.activation(us[:, j], uT[:, bass.ds(i, 1), :].rearrange("p a t -> p (a t)"), ACT.Copy)
                act.activation(bt[:, j], ps[:, 4, 0:2 * P].rearrange("p (a t) -> p a t", a=2), ACT.Copy)
                act.activation(ct3[:, j, 0, :], ps[:, 4, 2 * P:3 * P], ACT.Copy)
                act.activation(ct3[:, j, 1:3, :], ps[:, 4, 2 * P:4 * P].rearrange("p (a t) -> p a t", a=2),
                               ACT.Copy, scale=-1.0).then_inc(s5_mats, 1)

            assert al.n == 1
            in_turn(act, [(2, s5_turns), (1, s5_trig), (2, s5_matrices)], KT)
            al.n += KT
            for n in range(4):
                act.wait_ge(s5_z, 4 * n + 5)
                act.activation(uT[:, 4 * n:4 * n + 4, :], uT[:, 4 * n:4 * n + 4, :], ACT.Gelu_apprx_tanh).then_inc(s5_g, 1)
            for n in range(4):
                act.wait_ge(s5_g, n + 1)
                act.activation(xh[:, 4 * n:4 * n + 4, :], uT[:, 4 * n:4 * n + 4, :], ACT.Copy).then_inc(s5_gh, 1)

            panels(G["glu"], lambda q, j: gate(G["glu"], q, j, ACT.Sigmoid, False) if j == 0 else None)

            def ffn(layer, v, pending=None):
                g, x0 = G[f"gu{layer}"], (0, 27)[layer]
                def one(i, j):
                    q = i * 2 + j
                    split(g, q, range(2))
                    if j == 1:
                        gate(g, q - 1, 0, ACT.Silu)
                    split(g, q, range(2, g.chunks))
                    if j == 0:
                        hidden_hi(i + (x0 - 1), i - 1)
                first_panel(g, pending, None, v)
                act.wait_ge(rstd_ready, NORM_OF[v])
                one(0, 1)
                with act.Fori(1, g.panels // 2) as i:
                    for j in range(2):
                        one(i, j)
                n = g.panels // 2
                panels(G[f"dn{layer}"], lambda q, j: None, late=lambda: hidden_hi(n + x0 - 1, n - 1))

            ffn(0, T_FFN0)
            def head_panels(g, n0, dst, **more):
                mid = lambda q, j: head_sd(q + n0)
                evac, after = panels(g, lambda q, j: raw_heads(g, q, j, q + n0),
                                     lambda q, j: heads_T(q + (n0 + 11), dst, q * 4), mid=mid, **more)
                return evac, lambda: mid(g.panels - 1, 1), after

            last_heads, last_root, last_T = head_panels(G["k"], 0, kT, v=T_KV)
            last_v, _ = panels(G["v"], lambda q, j: store(G["v"], q, j, vt[:, :, bass.ds(q * PANEL, PANEL)], True),
                               pending=last_heads, pending_mid=last_root, late=last_T)
            last_heads, last_root, last_T = head_panels(G["q"], 4, qT, v=T_MIX1, pending=last_v)
            last_heads()
            last_root()
            last_T()

            def at_a(h, j):
                act.wait_ge(at_max, h + 1)
                for b, (lo, hi) in enumerate(((0, 384), (384, 1152))):
                    last = act.activation(score[:, j, lo:hi], score[:, j, lo:hi], ACT.Exp,
                                          bias=negm[:, 2 * j + b:2 * j + b + 1],
                                          accum_out=den[:, 2 * j + b:2 * j + b + 1])
                last.then_inc(at_exp, 1)

            def at_b(h, j):
                act.wait_ge(at_pt, h + 3)
                act.wait_ge(at_pv, h + 2)
                act.activation(wT[:], ps[:, 6, 0:384], ACT.Copy).then_inc(at_wt, 1)

            def at_c(h, j):
                act.wait_ge(at_pv, h + 3)
                act.activation(xh[:, bass.ds(h, 1), :].rearrange("p a t -> p (a t)"), ps[:, 7, 0:T],
                               ACT.Copy).then_inc(at_oh, 1)

            in_turn(act, [(-1, at_b), (-2, at_c), (1, at_a)])
            panels(G["o"], lambda q, j: None)
            ffn(1, T_FFN1)

            def rope_tables():
                act.wait_ge(rope_ang, 1)
                act.activation(rope_cs[:, 1], rope_t[:, 0], ACT.Sin, scale=TWO_PI_BELOW)
                al.link(act.activation(rope_t[:, 1], rope_t[:, 0], ACT.Abs))
                act.activation(rope_cs[:, 0], rope_t[:, 1], ACT.Sin, bias=half_pi[:],
                               scale=-TWO_PI_BELOW).then_inc(rope_ready, 1)

            last_out = None
            for l in range(NLAYER2):
                def small(l=l):
                    if l == 0:
                        rope_tables()
                    act.wait_ge(lam_dot, l + 1)
                    act.activation(lam_e, lam_e, ACT.Exp).then_inc(lam_exp, 1)

                g = G[f"in{l}"]
                last_in, _ = panels(g, lambda q, j: store(g, q, j, proj[:, :, bass.ds(q * PANEL, PANEL)], True),
                                    pending=last_out, late=small, v=T_PRE[l])
                last_in()
                for col, width in ((C_RG, RW), (C_DG, DW), (C_LG, LW)):
                    act.wait_ge(evac_done, g.all_evacuated)
                    act.activation(proj[:, :, col:col + width], proj[:, :, col:col + width],
                                   ACT.Silu).then_inc(gates_done, 1)
                for u in range(10):
                    act.wait_ge(a_tr, 10 * l + u + 1)
                    dst = rT[:, 2 * u:2 * u + 2, :] if u < 6 else dT[:, 2 * u - 12:2 * u - 10, :]
                    act.activation(dst, ps[:, 4 + u % 4, :].rearrange("p (a t) -> p a t", a=2),
                                   ACT.Copy).then_inc(a_ev, 1)
                for h in range(RH):
                    act.wait_ge(r_o, RH * l + h + 1)
                    act.activation(tok[:, :, DH * h:DH * h + DH], ps[:, 2 + h % 2, 0:TB * DH]
                                   .rearrange("p (b e) -> p b e", b=TB), ACT.Copy).then_inc(r_ev, 1)

                def d_a(h):
                    act.wait_ge(d_max, DIFH * l + h + 1)
                    for m in range(2):
                        for b, (lo, hi) in enumerate(((0, 128), (128, 384))):
                            n = 2 * m + b
                            last = act.activation(ds[:, h % 2, m, lo:hi], ds[:, h % 2, m, lo:hi], ACT.Exp,
                                                  bias=dnegm[:, n:n + 1], accum_out=dden[:, n:n + 1])
                    last.then_inc(d_exp, 1)

                def d_b(h):
                    act.wait_ge(d_pt, DIFH * l + h + 1)
                    act.activation(dwT[:], ps[:, 0, 0:384], ACT.Copy).then_inc(d_wt, 1)
                    act.wait_ge(d_o, DIFH * l + h + 1)
                    act.activation(tok[:, :, RW + DH * h:RW + DH * h + DH], ps[:, 2 + h % 2, 0:TB * DH]
                                   .rearrange("p (b e) -> p b e", b=TB), ACT.Copy).then_inc(d_ev, 1)

                for h in range(DIFH):
                    d_a(h)
                    d_b(h)
                act.wait_ge(h_ms, l + 1)
                act.activation(hs2_sd, hs2, ACT.Sqrt).then_inc(h_sd, 1)

                act.wait_ge(l_row, l + 1)
                act.activation(lru_p[:].rearrange("p a n -> p (a n)"), ps[0:LBW, 3, 0:64], ACT.Copy).then_inc(l_par, 1)
                act.wait_ge(l_e, l + 1)
                act.activation(lru_t[:, 1, :], lru_t[:, 0, :], ACT.Exp, scale=-1.0).then_inc(l_e2, 1)
                act.wait_ge(h_done, 5 * l + 1)
                for u in range(4):
                    act.wait_ge(l_xt, 4 * l + u + 1)
                    act.activation(lru_x[:, 2 * u:2 * u + 2, 3:T + 3], ps[0:LBW, 4 + u, :]
                                   .rearrange("p (a t) -> p a t", a=2), ACT.Copy).then_inc(l_x, 1)
                for n in range(LB):
                    act.wait_ge(l_g, LB * l + n + 1)
                    act.activation(lru_r[:, n, :], ps[0:LBW, n, 0:T], ACT.Sigmoid, bias=lru_p[:, 5, n:n + 1])
                    act.activation(lru_i[:, n, :], ps[0:LBW, n, T:2 * T], ACT.Sigmoid,
                                   bias=lru_p[:, 6, n:n + 1]).then_inc(l_sig, 1)
                act.wait_ge(l_la, l + 1)
                act.activation(lru_x[:, :, 0:T], lru_r[:], ACT.Exp).then_inc(l_a, 1)
                act.activation(lru_y[:], lru_r[:], ACT.Tanh, scale=-1.0).then_inc(l_a, 1)
                act.wait_ge(l_a, 3 * l + 2)
                act.activation(lru_r[:], lru_x[:, :, 0:T], ACT.Square).then_inc(l_a, 1)
                act.wait_ge(l_m, l + 1)
                act.activation(lru_y[:], lru_r[:], ACT.Sqrt).then_inc(l_mq, 1)
                g = G[f"out{l}"]

                def out_panel(q, j, g=g, l=l):
                    cols = bass.ds(q * PANEL, PANEL)
                    store(g, q, j, tok[:, :, cols])
                    act.wait_ge(evac_done, g.evacuated(q))
                    for b in range(TB):
                        act.wait_ge(y_ssq, q * 2 + (8 * l + b))
                        act.activation(junk[:, 0:PANEL], tok[:, b, cols], ACT.Square,
                                       accum_out=y_sums[:, b, bass.ds(q, 1)]).then_inc(y_ssq, 1)

                last_panel, _ = panels(g, out_panel, v=T_OUT[l])

                def last_out(last_panel=last_panel, l=l):
                    last_panel()
                    act.wait_ge(y_ms, l + 1)
                    act.activation(sdev[:], msq[:], ACT.Sqrt).then_inc(y_sd, 1)
            last_out()

        @block.tensor
        def _(pe):
            pe.nop().then_inc(chunk_used, SPLIT)
            pe.nop().then_inc(s5_tr, 1)
            for start in (s5_b, s5_y, x_tr, at_sc, at_pt, at_pv):
                pe.nop().then_inc(start, 2)

            def chunk(g, q, j, k, hi, lo):
                pe.wait_ge(lo_done, g.chunk(q, k) + (AHEAD + 1))
                for t in range(CK):
                    kt = CK * k + t
                    for b in range(TB):
                        tokens = slice(b * P, b * P + P)
                        for n, (xs, ws) in enumerate(((hi, whi), (hi, wlo), (lo, whi))):
                            last = pe.matmul(ps[:, 2 * j + b, :], xs[:, kt, tokens], ws[:, k % SPLIT, t, :],
                                             start=kt == 0 and n == 0,
                                             stop=kt == CK * g.chunks - 1 and n == 2)
                last.then_inc(chunk_used, 1)

            def panel(g, q, j, hi=xh, lo=xl, between=None):
                pe.wait_ge(evac_done, g.evacuated(q) - 2)
                for k in range(g.chunks):
                    chunk(g, q, j, k, hi, lo)
                    if between and k == 6:
                        between()

            def panels(g, hi=xh, lo=xl, after=None, first=panel):
                def one(q, j):
                    panel(g, q, j, hi, lo, (lambda: after(q - 1, 1 - j)) if after else None)
                first(g, 0, 0, hi, lo)
                one(1, 1)
                pairs = g.panels // 2
                if pairs > 2:
                    with pe.Fori(1, pairs) as i:
                        for j in range(2):
                            one(i * 2 + j, j)
                elif pairs == 2:
                    for j in range(2):
                        one(2 + j, j)
                if g.panels % 2:
                    one(g.panels - 1, 0)

            def turn_hbuf(xi, ready, count):
                pe.wait_ge(ready, count)
                for u in range(2):
                    pe.wait_ge(x_done, xi * 2 + (u + 1))
                    for f in range(2):
                        for b in range(TB):
                            last = pe.transpose(ps[:, 4 + u, f * T + b * P:f * T + b * P + P],
                                                hbuf[:, b, (2 * u + f) * P:(2 * u + f + 1) * P], ident[:])
                    last.then_inc(x_tr, 1)

            def source_ready(v, u):
                if v == T_MIX0:
                    pe.wait_ge(xn_ready, 2)
                elif v in NORM_OF:
                    pe.wait_ge(*x_written(NORM_OF[v], u // 2))
                elif v in T_OUT:
                    pe.wait_ge(mix_done, 4 * T_OUT.index(v) + 4)

            def turn_unit(v, u):
                source = x if v in NORM_OF or v == T_MIX1 else tok
                source_ready(v, u)
                if u >= 4:
                    pe.wait_ge(*((tr_hi, u - 3) if v == T_MIX0 else (tr_lo, 8 * (v - 1) + u - 3)))
                for kk in range(2):
                    for b in range(TB):
                        last = pe.transpose(ps[:, 4 + u % 4, kk * T + b * P:kk * T + b * P + P],
                                            source[:, b, (2 * u + kk) * P:(2 * u + kk + 1) * P], ident[:])
                last.then_inc(tr_ready, 1)

            def turned(v):
                def first(g, q, j, hi, lo):
                    for u in range(4):
                        turn_unit(v, u)
                    pe.wait_ge(evac_done, g.evacuated(0) - 2)
                    for k in range(g.chunks):
                        pe.wait_ge(tr_lo, 8 * (v - 1) + k + 1)
                        chunk(g, 0, 0, k, hi, lo)
                        if k + 4 < 8:
                            turn_unit(v, k + 4)
                return first

            pe.wait_ge(ident_in, 16)
            pe.wait_ge(s5_in, 16 * 4)
            pe.transpose(ps[:, 1, 0:P], a_rows[:], ident[:]).then_inc(s5_a_tr, 1)
            pe.wait_ge(s5_dt_wide, 1)
            pe.transpose(ps[:, 2, 0:64], dt_wide[:].rearrange("p a b -> p (a b)"), ident[0:64, 0:64]).then_inc(s5_dt_tr, 1)
            pe.wait_ge(par_in, 16 * len(GAINS))
            pe.transpose(ps[:, 0, 0:P], gain_rows[:], ident[:]).then_inc(gain_tr, 1)
            for u in range(8):
                turn_unit(T_MIX0, u)

            def s5_transposes(i, j):
                pe.wait_ge(s5_stage, i + 1)
                pe.wait_ge(s5_mats, i + 1)
                mats = [bx[:, 0].rearrange("p a g h -> p (a g h)"), bx[:, 1].rearrange("p a g h -> p (a g h)"),
                        cx[:, 0].rearrange("p g h -> p (g h)"), cx[:, 1].rearrange("p g h -> p (g h)")]
                for n, m in enumerate(mats):
                    last = pe.transpose(ps[:, 4, n * P:n * P + P], m, ident[:])
                last.then_inc(s5_tr, 1)

            def s5_in_products(i, j):
                pe.wait_ge(s5_mats, i + 2)
                pe.wait_ge(s5_rot, i + 1)
                for s in range(4):
                    rows = slice(32 * s, 32 * s + 32)
                    for m in range(2):
                        last = pe.matmul(ps[:, s, m * T:m * T + T], bt[rows, j, m, :], us[rows, j, :], start=True, stop=True)
                last.then_inc(s5_b, 1)

            def s5_outputs(i, j):
                pe.wait_ge(s5_q, i + 3)
                pe.wait_ge(s5_qp, i + 3)
                pe.wait_ge(s5_z, i + 1)
                for s in range(4):
                    rows = slice(32 * s, 32 * s + 32)
                    for n, m in enumerate((0, 1, 2, 2)):
                        last = pe.matmul(ps[rows, 5, 0:T], ct3[:, j, m, rows], q4[:, n, s, :], start=n == 0, stop=n == 3)
                last.then_inc(s5_y, 1)

            in_turn(pe, [(2, s5_transposes), (1, s5_in_products), (0, s5_outputs)], KT)

            def after_s5(g, q, j, hi, lo):
                for k in range(g.chunks):
                    pe.wait_ge(s5_gl, k // 2 + 1)
                    chunk(g, 0, 0, k, hi, lo)

            panels(G["glu"], first=after_s5)

            def ffn(layer, v):
                g, x0, n = G[f"gu{layer}"], (0, 27)[layer], G[f"gu{layer}"].panels // 2
                def hidden(i):
                    turn_hbuf(i + x0, evac_done, g.evacuated(i * 2 + 1))
                turned(v)(g, 0, 0, xh, xl)
                panel(g, 1, 1)
                with pe.Fori(1, n) as i:
                    panel(g, i * 2, 0, between=lambda: hidden(i - 1))
                    panel(g, i * 2 + 1, 1)

                def first(d, q, j, hi, lo):
                    pe.wait_ge(x_done, 2 * (x0 + n))
                    for k in range(d.chunks):
                        if k == 0:
                            pe.wait_ge(evac_done, d.evacuated(0) - 2)
                        if k == d.chunks - 2:
                            pe.wait_ge(x_done, 2 * (x0 + n) + 2)
                        chunk(d, 0, 0, k, hi, lo)
                        if k == 6:
                            hidden(n - 1)
                panels(G[f"dn{layer}"], hh, hl, first=first)

            ffn(0, T_FFN0)
            k_heads = lambda q, j: turn_hbuf(q + 11, head_norm, q + 2)
            q_heads = lambda q, j: turn_hbuf(q + 15, head_norm, q + 6)
            panels(G["k"], after=k_heads, first=turned(T_KV))
            panels(G["v"], first=lambda g, q, j, hi, lo: panel(g, 0, 0, hi, lo, lambda: k_heads(3, 1)))
            panels(G["q"], after=q_heads, first=turned(T_MIX1))
            q_heads(11, 1)

            def at_scores(h, j):
                pe.wait_ge(at_qs, h + 1)
                pe.wait_ge(at_bias, h + 1)
                for g in range(NG):
                    pe.matmul(ps[:, 3 * j, g * P:g * P + P], qst[:, j, g, 0:P],
                              kT[:, bass.ds(h, 1), 0:P].rearrange("p a t -> p (a t)"), start=True, stop=True)
                for g in range(NG):
                    last = pe.matmul(ps[:, 3 * j + 1 + g // 2, (g % 2) * T:(g % 2) * T + T], qst[:, j, g, P:T],
                                     kT[:, bass.ds(h, 1), :].rearrange("p a t -> p (a t)"), start=True, stop=True)
                last.then_inc(at_sc, 1)

            def at_turn(h, j):
                pe.wait_ge(at_w, h + 1)
                pe.wait_ge(at_wt, h + 1)
                for n in range(3):
                    last = pe.transpose(ps[:, 6, n * P:n * P + P], wsum[:, j, n * P:n * P + P], ident[:])
                last.then_inc(at_pt, 1)

            def at_values(h, j):
                pe.wait_ge(at_wt, h + 2)
                pe.wait_ge(at_vs, h + 1)
                pe.wait_ge(at_o, h + 1)
                o = ps[:, 7, 0:T]
                pe.matmul(o, vst[:, j, 0, :], wT[:, 0:T], start=True, stop=False)
                pe.matmul(o[:, P:T], vst[:, j, 1, :], wT[:, T:T + P], start=False, stop=True).then_inc(at_pv, 1)

            in_turn(pe, [(2, at_scores), (-1, at_values), (0, at_turn)])
            pe.wait_ge(at_o, HEADS + 1)
            panels(G["o"])
            ffn(1, T_FFN1)

            for l in range(NLAYER2):
                panels(G[f"in{l}"], first=turned(T_PRE[l]))
                pe.wait_ge(rope_done, l + 1)
                for u in range(10):
                    if u >= 4:
                        pe.wait_ge(a_ev, 10 * l + u - 3)
                    for f in range(2):
                        i = 2 * u + f
                        col = C_RQ + P * i if u < 6 else C_DQ + P * (i - 12)
                        for b in range(TB):
                            last = pe.transpose(ps[:, 4 + u % 4, f * T + b * P:f * T + b * P + P],
                                                proj[:, b, col:col + P], ident[:])
                    last.then_inc(a_tr, 1)
                pe.wait_ge(a_ev, 10 * l + 10)

                def r_scores(h):
                    if h >= 2:
                        pe.wait_ge(r_a, RH * l + h - 1)
                    q, k = rT[:, h, :], rT[:, RH + h, :]
                    pe.matmul(ps[:, h % 2, 0:T], k[:, 0:P], q, start=True, stop=True)
                    pe.matmul(ps[:, h % 2, T:T + P], k[:, P:T], q[:, P:T], start=True, stop=True).then_inc(r_s, 1)

                def r_values(h):
                    pe.wait_ge(r_a, RH * l + h + 1)
                    if h >= 2:
                        pe.wait_ge(r_ev, RH * l + h - 1)
                    v = proj[:, :, C_RV + DH * h:C_RV + DH * h + DH]
                    o, a = ps[:, 2 + h % 2, :], ra[:, h % 2, :]
                    pe.matmul(o[:, 0:DH], a[:, 0:P], v[:, 0, :], start=True, stop=True)
                    pe.matmul(o[:, DH:2 * DH], a[:, P:T], v[:, 0, :], start=True, stop=False)
                    pe.matmul(o[:, DH:2 * DH], a[:, T:T + P], v[:, 1, :], start=False, stop=True).then_inc(r_o, 1)

                r_scores(0)
                for h in range(RH):
                    if h + 1 < RH:
                        r_scores(h + 1)
                    r_values(h)

                def d_scores(h):
                    if h >= 2:
                        pe.wait_ge(d_m, DIFH * l + h - 1)
                    for m in range(2):
                        rows = slice(64 * m, 64 * m + 64)
                        s = ps[:, 4 + 2 * (h % 2) + m, :]
                        q, k = dT[rows, h, :], dT[rows, DIFH + h, :]
                        pe.matmul(s[:, 0:P], q[:, 0:P], k[:, 0:P], start=True, stop=True)
                        last = pe.matmul(s[:, P:P + T], q[:, P:T], k, start=True, stop=True)
                    last.then_inc(d_s, 1)

                def d_values(h):
                    pe.wait_ge(d_w, DIFH * l + h + 1)
                    if h == 0:
                        pe.wait_ge(r_a, RH * (l + 1))
                    else:
                        pe.wait_ge(d_wt, DIFH * l + h)
                    for n in range(3):
                        last = pe.transpose(ps[:, 0, n * P:n * P + P], dw[:, n * P:n * P + P], ident[:])
                    last.then_inc(d_pt, 1)
                    pe.wait_ge(d_wt, DIFH * l + h + 1)
                    if h < 2:
                        pe.wait_ge(r_ev, RH * (l + 1))
                    else:
                        pe.wait_ge(d_ev, DIFH * l + h - 1)
                    v = proj[:, :, C_DV + DH * h:C_DV + DH * h + DH]
                    o = ps[:, 2 + h % 2, :]
                    pe.matmul(o[:, 0:DH], dwT[:, 0:P], v[:, 0, :], start=True, stop=True)
                    pe.matmul(o[:, DH:2 * DH], dwT[:, P:T], v[:, 0, :], start=True, stop=False)
                    pe.matmul(o[:, DH:2 * DH], dwT[:, T:T + P], v[:, 1, :], start=False, stop=True).then_inc(d_o, 1)

                d_scores(0)
                for h in range(DIFH):
                    if h + 1 < DIFH:
                        d_scores(h + 1)
                    d_values(h)

                pe.wait_ge(lru_in, 16 * 7 * (l + 1))
                pe.wait_ge(d_ev, DIFH * (l + 1))
                pe.transpose(ps[0:LBW, 3, 0:64], lru_rows[:], ident[0:64, 0:64]).then_inc(l_row, 1)
                pe.wait_ge(d_m, DIFH * (l + 1))
                for u in range(4):
                    for f in range(2):
                        col = C_LX + LBW * (2 * u + f)
                        for b in range(TB):
                            last = pe.transpose(ps[0:LBW, 4 + u, f * T + b * P:f * T + b * P + P],
                                                proj[:, b, col:col + LBW], ident[:])
                    last.then_inc(l_xt, 1)
                pe.wait_ge(l_par, l + 1)
                pe.wait_ge(l_x, 4 * (l + 1))
                for n in range(LB):
                    if n == 0:
                        pe.wait_ge(l_conv, l + 1)
                    pe.matmul(ps[0:LBW, n, 0:T], lru_wa[:, n, :], lru_c[:, n, :], start=True, stop=True)
                    pe.matmul(ps[0:LBW, n, T:2 * T], lru_wx[:, n, :], lru_c[:, n, :], start=True, stop=True).then_inc(l_g, 1)
                pe.wait_ge(l_h, l + 1)
                for u in range(4):
                    b, half = u // 2, u % 2
                    for f in range(4):
                        last = pe.transpose(ps[:, 4 + u, f * LBW:f * LBW + LBW],
                                            lru_y[:, 4 * half + f, b * P:b * P + P], ident[0:LBW, 0:LBW])
                    last.then_inc(l_ht, 1)
                panels(G[f"out{l}"], first=turned(T_OUT[l]))

        @block.vector
        def _(dve):
            dl = Links(dve, dve_link)
            link = dl.link
            dve.nop().then_inc(lo_done, AHEAD)
            for start, n in ((evac_done, 2), (x_done, 2), (head_norm, 1), (s5_rot, 1), (s5_q, 2), (s5_z, 1),
                             (at_bias, 2), (at_o, 1)):
                dve.nop().then_inc(start, n)

            def split(g, q, ks):
                for k in ks:
                    dve.wait_ge(hi_done, g.chunk(q, k) + 1)
                    dve.wait_ge(chunk_used, g.chunk(q, k) + 1)
                    dve.tensor_tensor(wlo[:, k % SPLIT], raw[:, k % RAW], whi[:, k % SPLIT].bitcast(F32),
                                      ALU.subtract).then_inc(lo_done, 1)

            def product(g, q, j, scaled=True):
                dve.wait_ge(chunk_used, g.done(q))
                dve.wait_ge(evac_done, g.evacuated(q) - 1)
                for b in range(TB):
                    last = dve.scalar_tensor_tensor(hbuf[:, b], ps[:, 2 * j + b, :], rstd[:, b:b + 1] if scaled else 1.0,
                                                    gbuf[:, b], ALU.mult, ALU.mult)
                last.then_inc(evac_done, 1)

            def residual(g, q, j):
                dve.wait_ge(chunk_used, g.done(q))
                cols = x[:, :, bass.ds(q * PANEL, PANEL)]
                dve.tensor_tensor(cols, panel_ps(j), cols, ALU.add).then_inc(evac_done, 1)

            def hidden_lo(fi, i):
                for u in range(2):
                    dve.wait_ge(x_hi_done, fi * 2 + (u + 1))
                    tiles = bass.ds(i * 4 + 2 * u, 2)
                    dve.tensor_tensor(hl[:, tiles, :], ps[:, 4 + u, :].rearrange("p (a t) -> p a t", a=2),
                                      hh[:, tiles, :].bitcast(F32), ALU.subtract).then_inc(x_done, 1)

            def mean(v):
                dve.wait_ge(nrm_ssq, 2 * v + 2)
                dve.tensor_scalar(msq[:], ssq[:], 1.0 / D, EPS, ALU.mult, ALU.add).then_inc(nrm_ms, 1)

            def inverse(v):
                dve.wait_ge(nrm_sd, v + 1)
                if v == N_MIX0:
                    link(dve.reciprocal(rstd[:], sdev[:]))
                else:
                    dve.reciprocal(rstd[:], sdev[:]).then_inc(rstd_ready, 1)
                    dve.wait_ge(rstd_ready, v)

            def turn_lo(v, u):
                gain = TURNS[v]
                dve.wait_ge(tr_hi, 8 * v + u + 1)
                for kk in range(2):
                    kt = 2 * u + kk
                    scale = 1.0 if gain is None else gains[:, GAINS.index(gain), kt:kt + 1]
                    last = dve.scalar_tensor_tensor(xl[:, kt, :], ps[:, 4 + u % 4, kk * T:(kk + 1) * T], scale,
                                                    xh[:, kt, :].bitcast(F32), ALU.mult, ALU.subtract)
                last.then_inc(tr_lo, 1)

            def first_panel(g, pending=None, late=None, v=None, pending_mid=None):
                split(g, 0, [0])
                if pending:
                    pending()
                for k in range(g.chunks):
                    if v is not None:
                        turn_lo(v, k)
                    if k:
                        split(g, 0, [k])
                    if k == 4 and pending_mid:
                        pending_mid()
                    if k == 6 and v in NORM_OF:
                        mean(NORM_OF[v])
                    if k == 7 and v in NORM_OF:
                        inverse(NORM_OF[v])
                    if k == 7 and late:
                        late()

            def panels(g, evac, pending=None, late=None, v=None, mid=None, pending_mid=None):
                def one(q, j):
                    split(g, q, range(2))
                    evac(q - 1, 1 - j)
                    split(g, q, range(2, 5))
                    if mid:
                        mid(q - 1, 1 - j)
                    split(g, q, range(5, g.chunks))
                first_panel(g, pending, late, v, pending_mid)
                one(1, 1)
                pairs = g.panels // 2
                if pairs > 2:
                    with dve.Fori(1, pairs) as i:
                        for j in range(2):
                            one(i * 2 + j, j)
                elif pairs == 2:
                    for j in range(2):
                        one(2 + j, j)
                last = 2 * pairs - 1
                if g.panels % 2:
                    one(g.panels - 1, 0)
                    last = g.panels - 1
                return lambda: evac(last, last % 2)

            def exp_to(dst, src, n, r, e, bits):
                link(dve.tensor_scalar(n, src, 1.0 / math.log(2.0), MAGIC, ALU.mult, ALU.add))
                link(dve.tensor_scalar(n, n, MAGIC, -127.0, ALU.subtract, ALU.max))
                link(dve.scalar_tensor_tensor(r, n, -0.693359375, src, ALU.mult, ALU.add))
                link(dve.scalar_tensor_tensor(r, n, 2.12194440054690583e-4, r, ALU.mult, ALU.add))
                link(dve.tensor_scalar(e, r, 1.0 / math.factorial(8), None, ALU.mult))
                for k in range(7, 0, -1):
                    link(dve.scalar_tensor_tensor(e, e, 1.0 / math.factorial(k), r, ALU.add, ALU.mult))
                link(dve.tensor_scalar(bits, n, 127.0, float(2**23), ALU.add, ALU.mult))
                link(dve.scalar_tensor_tensor(dst, e, 1.0, bits.bitcast(F32), ALU.add, ALU.mult))

            def turns_of(phi, ang, n):
                link(dve.tensor_scalar(n, ang, 1.0 / (2 * math.pi), MAGIC, ALU.mult, ALU.add))
                link(dve.tensor_scalar(n, n, MAGIC, None, ALU.subtract))
                for part in (C1, C2, C3):
                    link(dve.scalar_tensor_tensor(ang, n, -part, ang, ALU.mult, ALU.add))
                link(dve.tensor_scalar(phi, ang, 1.0 / (2 * math.pi), 0.5, ALU.mult, ALU.min))
                return dve.tensor_scalar(phi, phi, -0.5, None, ALU.max)

            V = lambda n: par[:, n, :]
            dve.wait_ge(s5_in, 16 * 4)
            dve.tensor_copy(dt_wide[:], dt_rows[:].unsqueeze(2).to_broadcast([64, 2, 64])).then_inc(s5_dt_wide, 1)
            dve.wait_ge(s5_a_tr, 1)
            dve.tensor_scalar(V(0), ps[:, 1, 0:64], -1e-4, None, ALU.min)
            link(dve.tensor_copy(V(1), ps[:, 1, 64:128]))
            dve.wait_ge(s5_dt_tr, 1)
            link(dve.tensor_copy(V(19), ps[:, 2, 0:64]))
            exp_to(V(2), V(19), V(6), V(7), V(17), V(18).bitcast(I32))
            link(dve.tensor_tensor(V(3), V(0), V(2), ALU.mult))
            exp_to(V(4), V(3), V(6), V(7), V(17), V(18).bitcast(I32))
            link(dve.tensor_tensor(V(5), V(1), V(2), ALU.mult))
            turns_of(V(8), V(5), V(6)).then_inc(s5_par, 1)
            mean(N_MIX0)
            inverse(N_MIX0)
            for b in range(TB):
                dve.tensor_scalar(tok[:, b, :], x[:, b, :], rstd[:, b:b + 1], None, ALU.mult).then_inc(xn_ready, 1)
            dve.wait_ge(s5_exp, 2)
            link(dve.tensor_tensor(V(12), V(4), V(11), ALU.mult))
            link(dve.tensor_tensor(V(13), V(4), V(10), ALU.mult))
            link(dve.tensor_tensor(V(14), V(0), V(0), ALU.mult))
            link(dve.tensor_tensor(V(17), V(1), V(1), ALU.mult))
            link(dve.tensor_tensor(V(14), V(14), V(17), ALU.add))
            link(dve.reciprocal(V(14), V(14)))
            link(dve.tensor_scalar(V(12), V(12), -1.0, None, ALU.add))
            for dst, (a, b), op in ((15, (0, 1), ALU.add), (16, (1, 0), ALU.subtract)):
                x_, y_ = (12, 13) if dst == 15 else (13, 12)
                link(dve.tensor_tensor(V(17), V(x_), V(0), ALU.mult))
                link(dve.tensor_tensor(V(18), V(y_), V(1), ALU.mult))
                link(dve.tensor_tensor(V(17), V(17), V(18), op))
                link(dve.tensor_tensor(V(dst), V(17), V(14), ALU.mult))
            dve.wait_ge(s5_bc_in, 16 * 5)
            wide = lambda n: V(n).unsqueeze(2).to_broadcast([P, 64, 16])
            tmp = whole[:].rearrange("p a t -> p (a t)").rearrange("p (j h) -> p j h", h=16)
            for dst, (m, n), op in ((bb_re, (b_re, b_im), ALU.subtract), (bb_im, (b_im, b_re), ALU.add)):
                link(dve.tensor_tensor(dst[:], m[:], wide(15), ALU.mult))
                link(dve.tensor_tensor(tmp, n[:], wide(16), ALU.mult))
                last = dve.tensor_tensor(dst[:], dst[:], tmp, op)
                if dst is bb_re:
                    link(last)
            last.then_inc(s5_par, 1)

            def s5_round(i, j):
                dve.wait_ge(s5_turn, i + 1)
                dve.wait_ge(s5_frac, i + 1)
                dve.tensor_scalar(whole[:], turn[:, j], MAGIC, MAGIC, ALU.add, ALU.subtract).then_inc(s5_whole, 1)

            def s5_rotate(i, j):
                cos, sin = cs[:, j, 0], cs[:, j, 1]
                dve.wait_ge(s5_cs, i + 2)
                dve.wait_ge(s5_b, i + 3)
                dve.wait_ge(s5_add, i + 1)
                in_re, in_im = ps[:, 0:4, 0:T], ps[:, 0:4, T:2 * T]
                dve.tensor_tensor(p4[:, 2], in_im, cos, ALU.mult)
                dve.tensor_tensor(p4[:, 3], in_re, sin, ALU.mult)
                dve.tensor_tensor(p4[:, 0], in_re, cos, ALU.mult)
                dve.tensor_tensor(p4[:, 1], in_im, sin, ALU.mult).then_inc(s5_rot, 1)

            def s5_scan(i, j, part, dst):
                for s in range(4):
                    mag = par[:, 4, bass.ds(i * 4 + s, 1)].to_broadcast([P, T])
                    last = dve.tensor_tensor_scan(dst[:, s, :], mag, p4[:, part, s, :], 0.0, ALU.mult, ALU.add)
                return last

            def s5_states(i, j):
                dve.wait_ge(s5_rot, i + 2)
                dve.tensor_tensor(p4[:, 0], p4[:, 0], p4[:, 1], ALU.add).then_inc(s5_link, 1)
                dve.wait_ge(s5_link, i * 2 + 1)
                dve.wait_ge(s5_qp, i + 2)
                s5_scan(i, j, 0, r_re).then_inc(s5_re, 1)
                dve.wait_ge(s5_add, i + 2)
                s5_scan(i, j, 2, r_im).then_inc(s5_link, 1)
                dve.wait_ge(s5_link, i * 2 + 2)
                dve.wait_ge(s5_y, i + 2)
                dve.tensor_tensor(q4[:, 1], r_im[:], cs[:, j, 1], ALU.mult)
                dve.tensor_tensor(q4[:, 3], r_im[:], cs[:, j, 0], ALU.mult).then_inc(s5_q, 1)

            def s5_skip(i, j):
                dve.wait_ge(s5_y, i + 3)
                u = uT[:, bass.ds(i, 1), :].rearrange("p a t -> p (a t)")
                dve.scalar_tensor_tensor(u, u, gains[:, GAINS.index("skip"), bass.ds(i, 1)], ps[:, 5, 0:T],
                                         ALU.mult, ALU.add).then_inc(s5_z, 1)

            dve.wait_ge(s5_par, 2)
            in_turn(dve, [(0, s5_rotate), (0, s5_states), (2, s5_round), (-1, s5_skip)], KT)
            for n in range(4):
                dve.wait_ge(s5_gh, n + 1)
                dve.tensor_tensor(xl[:, 4 * n:4 * n + 4, :], uT[:, 4 * n:4 * n + 4, :],
                                  xh[:, 4 * n:4 * n + 4, :].bitcast(F32), ALU.subtract).then_inc(s5_gl, 1)

            def glu(q, j):
                if j == 0:
                    return
                g = G["glu"]
                product(g, q, j, False)
                dve.wait_ge(evac_done, g.evacuated(q))
                cols = x[:, :, bass.ds((q - 1) * (PANEL // 2), PANEL)]
                dve.tensor_tensor(cols, cols, hbuf[:], ALU.add).then_inc(glu_added, 1)

            last_glu = panels(G["glu"], glu)

            def ffn(layer, v, pending):
                g, x0, n = G[f"gu{layer}"], (0, 27)[layer], G[f"gu{layer}"].panels // 2
                def last_product(i):
                    dve.wait_ge(x_tr, i * 2 + (2 * x0))
                    product(g, i * 2 - 1, 1)
                def one(i, j):
                    split(g, i * 2 + j, range(2))
                    if j == 0:
                        last_product(i)
                    split(g, i * 2 + j, range(2, g.chunks))
                    if j == 0:
                        hidden_lo(i + (11 * layer - 1), i - 1)
                first_panel(g, pending, None, v)
                one(0, 1)
                with dve.Fori(1, n) as i:
                    for j in range(2):
                        one(i, j)
                return panels(G[f"dn{layer}"], lambda q, j: residual(G[f"dn{layer}"], q, j),
                              pending=lambda: last_product(n), late=lambda: hidden_lo(11 * layer + n - 1, n - 1))

            last_dn = ffn(0, T_FFN0, last_glu)

            by_head = lambda t: t[:].rearrange("p b (h e) -> p b h e", e=DH)

            def head_squares(g, q, n, xi):
                dve.wait_ge(evac_done, g.evacuated(q))
                dve.wait_ge(x_tr, xi * 2 + 2)
                dve.tensor_tensor(hbuf[:], gbuf[:], gbuf[:], ALU.mult).then_inc(head_link, 1)
                dve.wait_ge(head_link, n * 3 + 1)
                dve.tensor_reduce(hssq[:, 0], by_head(hbuf), AX.X, ALU.add).then_inc(head_link, 1)
                dve.wait_ge(head_link, n * 3 + 2)
                dve.tensor_scalar(hssq[:, 0], hssq[:, 0], 1.0 / DH, EPS, ALU.mult, ALU.add).then_inc(hd_ms, 1)

            def head_rms(n):
                dve.wait_ge(hd_sd, n + 1)
                dve.reciprocal(hssq[:, 2], hssq[:, 1]).then_inc(head_link, 1)
                dve.wait_ge(head_link, n * 3 + 3)
                dve.tensor_tensor(by_head(hbuf), by_head(gbuf), hssq[:, 2].unsqueeze(3).to_broadcast([P, TB, 4, DH]),
                                  ALU.mult).then_inc(head_norm, 1)

            last_k = panels(G["k"], lambda q, j: head_squares(G["k"], q, q, q + 11), pending=last_dn, v=T_KV,
                            mid=lambda q, j: head_rms(q))
            panels(G["v"], lambda q, j: None, pending=last_k, pending_mid=lambda: head_rms(3))
            last_q = panels(G["q"], lambda q, j: head_squares(G["q"], q, q + 4, q + 15), v=T_MIX1,
                            mid=lambda q, j: head_rms(q + 4))
            last_q()
            head_rms(15)
            dve.wait_ge(at_in, 64)
            dve.tensor_scalar(gqk[:], qkg[:, 0:NG], qkg[:, NG:NG + 1], DH ** -0.5, ALU.mult, ALU.mult).then_inc(gqk_ready, 1)

            def at_a(h, j):
                dve.wait_ge(at_sc, h + 3)
                for g in range(NG):
                    for lo, width, src in ((g * P, P, ps[:, 3 * j, g * P:g * P + P]),
                                           (3 * P + g * T, T, ps[:, 3 * j + 1 + g // 2, (g % 2) * T:(g % 2) * T + T])):
                        last = dve.scalar_tensor_tensor(score[:, j, lo:lo + width], dist[:, lo:lo + width],
                                                        slope[:, bass.ds(h, 1), g:g + 1].rearrange("p a b -> p (a b)"),
                                                        src, ALU.mult, ALU.add)
                last.then_inc(at_bias, 1)

            def at_top(h, j):
                dve.wait_ge(at_bias, h + 3)
                dve.tensor_reduce(negm[:, 2 * j:2 * j + 1], score[:, j, 0:384], AX.X, ALU.max, negate=True)
                dve.tensor_reduce(negm[:, 2 * j + 1:2 * j + 2], score[:, j, 384:1152], AX.X, ALU.max,
                                  negate=True).then_inc(at_max, 1)

            def at_b(h, j):
                dve.wait_ge(at_exp, h + 1)
                o = wsum[:, j]
                dve.reciprocal(rden[:, 2 * j:2 * j + 2], den[:, 2 * j:2 * j + 2]).then_inc(dve_link, 1)
                dve.wait_ge(dve_link, h + (at_base + 1))
                dve.wait_ge(at_sum, h * 2 + 2)
                dve.tensor_scalar(o[:, 0:P], o[:, 0:P], rden[:, 2 * j:2 * j + 1], None, ALU.mult)
                dve.tensor_scalar(o[:, P:3 * P], o[:, P:3 * P], rden[:, 2 * j + 1:2 * j + 2], None,
                                  ALU.mult).then_inc(at_w, 1)

            def at_c(h, j):
                dve.wait_ge(at_oh, h + 1)
                flat = lambda t: t[:, bass.ds(h, 1), :].rearrange("p a t -> p (a t)")
                dve.tensor_tensor(flat(xl), ps[:, 7, 0:T], flat(xh).bitcast(F32), ALU.subtract).then_inc(at_o, 1)

            at_base = dl.n
            in_turn(dve, [(1, at_a), (-2, at_c), (1, at_top), (0, at_b)])
            dl.n += HEADS
            last_o = panels(G["o"], lambda q, j: residual(G["o"], q, j))
            last_x = ffn(1, T_FFN1, last_o)

            def angles():
                dve.wait_ge(b2_in, 64)
                link(dve.tensor_copy(pos_f, pos_i[:]))
                for b in range(TB):
                    link(dve.tensor_scalar(rope_t[:, 2, b], inv[:], pos_f[:, b:b + 1], None, ALU.mult))
                turns_of(rope_t[:, 0], rope_t[:, 2], rope_t[:, 3]).then_inc(rope_ang, 1)

            def lam_of(l, lam_init):
                dve.wait_ge(b2l_in, 16 * 5 * (l + 1))
                link(dve.tensor_tensor(lam_p[:], lam_v[:, 0:4:2, :], lam_v[:, 1:4:2, :], ALU.mult))
                dve.tensor_reduce(lam_e, lam_p[:], AX.X, ALU.add).then_inc(lam_dot, 1)
                dve.wait_ge(lam_exp, l + 1)
                link(dve.tensor_tensor(lam_col, lam_e[:, 0:1], lam_e[:, 1:2], ALU.subtract))
                link(dve.tensor_scalar(lam_col, lam_col, lam_init, None, ALU.add))
                link(dve.tensor_scalar(sub_g[:], sub_g[:], 1.0 - lam_init, None, ALU.mult))

            for l in range(NLAYER2):
                def small(l=l):
                    if l == 0:
                        angles()
                    lam_of(l, 0.8 - 0.6 * math.exp(-0.3 * l))

                panels(G[f"in{l}"], lambda q, j: None, pending=last_x, late=small, v=T_PRE[l])

                dve.wait_ge(evac_done, G[f"in{l}"].all_evacuated)
                dve.wait_ge(rope_ready, 1)
                for b in range(TB):
                    for col, n, half, first in ((C_RQ, 2 * RH, DH // 2, 0), (C_DQ, 4 * DIFH, DH // 4, 64)):
                        v = proj[:, b, col:col + n * 2 * half].rearrange("p (h s e) -> p h s e", s=2, e=half)
                        x1, x2 = v[:, :, 0, :], v[:, :, 1, :]
                        t = [rope_a[:, k, 0:n * half].rearrange("p (h e) -> p h e", e=half) for k in range(4)]
                        cos, sin = (rope_cs[:, k, b, first:first + half].unsqueeze(1).to_broadcast([P, n, half])
                                    for k in range(2))
                        dve.tensor_tensor(t[0], x1, cos, ALU.mult)
                        dve.tensor_tensor(t[1], x2, sin, ALU.mult)
                        dve.tensor_tensor(t[2], x2, cos, ALU.mult)
                        link(dve.tensor_tensor(t[3], x1, sin, ALU.mult))
                        dve.tensor_tensor(x1, t[0], t[1], ALU.subtract)
                        last = dve.tensor_tensor(x2, t[2], t[3], ALU.add)
                        if b == TB - 1 and first:
                            last.then_inc(rope_done, 1)
                        else:
                            link(last)

                for h in range(RH):
                    dve.wait_ge(r_s, RH * l + h + 1)
                    if h >= 2:
                        dve.wait_ge(r_o, RH * l + h - 1)
                    dve.tensor_tensor(ra[:, h % 2, :], ps[:, h % 2, 0:384], decay[:, h, :], ALU.mult).then_inc(r_a, 1)

                def d_a(h):
                    dve.wait_ge(d_s, DIFH * l + h + 1)
                    for m in range(2):
                        last = dve.scalar_tensor_tensor(ds[:, h % 2, m, :], ps[:, 4 + 2 * (h % 2) + m, 0:384],
                                                        (DH // 2) ** -0.5, causal[:], ALU.mult, ALU.add)
                    last.then_inc(d_m, 1)
                    dve.wait_ge(d_m, DIFH * l + h + 1)
                    for m in range(2):
                        for b, (lo, hi) in enumerate(((0, 128), (128, 384))):
                            last = dve.tensor_reduce(dnegm[:, 2 * m + b:2 * m + b + 1], ds[:, h % 2, m, lo:hi],
                                                     AX.X, ALU.max, negate=True)
                    last.then_inc(d_max, 1)

                def d_b(h):
                    dve.wait_ge(d_exp, DIFH * l + h + 1)
                    link(dve.reciprocal(drden, dden))
                    dve.tensor_scalar(dlr, drden[:, 2:4], lam_col, None, ALU.mult)
                    for b, (lo, hi) in enumerate(((0, 128), (128, 384))):
                        last = dve.tensor_scalar(ds[:, h % 2, 0, lo:hi], ds[:, h % 2, 0, lo:hi], drden[:, b:b + 1],
                                                 None, ALU.mult)
                    link(last)
                    for b, (lo, hi) in enumerate(((0, 128), (128, 384))):
                        last = dve.tensor_scalar(ds[:, h % 2, 1, lo:hi], ds[:, h % 2, 1, lo:hi], dlr[:, b:b + 1],
                                                 None, ALU.mult)
                    link(last)
                    if h:
                        dve.wait_ge(d_pt, DIFH * l + h)
                    dve.tensor_tensor(dw[:], ds[:, h % 2, 0, :], ds[:, h % 2, 1, :], ALU.subtract).then_inc(d_w, 1)

                for h in range(DIFH):
                    d_a(h)
                    d_b(h)

                mixed = tok[:, :, 0:RW + DW]
                by_head = lambda t: t.rearrange("p b (h e) -> p b h e", e=DH)
                dve.wait_ge(r_ev, RH * (l + 1))
                dve.wait_ge(d_ev, DIFH * (l + 1))
                link(dve.tensor_tensor(sq2[:], mixed, mixed, ALU.mult))
                heads2 = hs2.rearrange("p (b h) -> p b h", b=TB)
                link(dve.tensor_reduce(heads2, by_head(sq2[:]), AX.X, ALU.add))
                dve.tensor_scalar(hs2, hs2, 1.0 / DH, EPS, ALU.mult, ALU.add).then_inc(h_ms, 1)
                dve.wait_ge(h_sd, l + 1)
                link(dve.reciprocal(hs2, hs2_sd))
                for b in range(TB):
                    last = dve.tensor_tensor(by_head(mixed)[:, b], by_head(mixed)[:, b],
                                             heads2[:, b].unsqueeze(2).to_broadcast([P, RH + DIFH, DH]), ALU.mult)
                last.then_inc(h_done, 1)
                dve.wait_ge(h_done, 5 * l + 1)
                for b in range(TB):
                    dif = tok[:, b, RW:RW + DW].rearrange("p (h e) -> p h e", e=DH)
                    last = dve.tensor_tensor(dif, dif, sub_g[:].unsqueeze(1).to_broadcast([P, DIFH, DH]), ALU.mult)
                last.then_inc(h_done, 1)
                dve.wait_ge(gates_done, 3 * (l + 1))
                dve.wait_ge(h_done, 5 * l + 2)
                dve.tensor_tensor(tok[:, :, 0:RW], tok[:, :, 0:RW], proj[:, :, C_RG:C_RG + RW], ALU.mult).then_inc(h_done, 1)
                dve.tensor_tensor(tok[:, :, RW:RW + DW], tok[:, :, RW:RW + DW], proj[:, :, C_DG:C_DG + DW],
                                  ALU.mult).then_inc(h_done, 1)
                dve.memset(lru_x[:, :, 0:3], 0.0).then_inc(h_done, 1)

                dve.wait_ge(l_par, l + 1)
                z = lru_p[:, 7, :]
                tt = lambda n: lru_t[:, n, :]
                dve.scalar_tensor_tensor(tt(0), z, -1.0, z, ALU.mult, ALU.max).then_inc(l_e, 1)
                dve.wait_ge(l_e2, l + 1)
                link(dve.tensor_scalar(tt(2), tt(1), 2.0, None, ALU.add))
                link(dve.reciprocal(tt(2), tt(2)))
                link(dve.tensor_tensor(tt(2), tt(2), tt(1), ALU.mult))
                link(dve.tensor_tensor(tt(3), tt(2), tt(2), ALU.mult))
                link(dve.tensor_scalar(tt(4), tt(3), 1.0 / 19, None, ALU.mult))
                for k in range(17, 1, -2):
                    link(dve.scalar_tensor_tensor(tt(4), tt(4), 1.0 / k, tt(3), ALU.add, ALU.mult))
                link(dve.scalar_tensor_tensor(tt(4), tt(4), 1.0, tt(2), ALU.add, ALU.mult))
                link(dve.tensor_scalar(tt(5), z, 0.0, 8.0, ALU.min, ALU.mult))
                link(dve.scalar_tensor_tensor(tt(5), tt(4), -16.0, tt(5), ALU.mult, ALU.add))

                dve.wait_ge(l_x, 4 * (l + 1))
                dve.wait_ge(h_done, 5 * l + 5)
                for k in range(4):
                    for n in range(LB):
                        src = lru_x[:, n, k:k + T]
                        if k == 0:
                            last = dve.tensor_scalar(lru_c[:, n, :], src, lru_p[:, 0, n:n + 1], lru_p[:, 4, n:n + 1],
                                                     ALU.mult, ALU.add)
                        else:
                            last = dve.scalar_tensor_tensor(lru_c[:, n, :], src, lru_p[:, k, n:n + 1],
                                                            lru_c[:, n, :], ALU.mult, ALU.add)
                    if k < 3:
                        link(last)
                last.then_inc(l_conv, 1)
                dve.wait_ge(l_sig, LB * (l + 1))
                dve.tensor_tensor(lru_r[:], lru_r[:], tt(5).unsqueeze(2).to_broadcast([LBW, LB, T]), ALU.mult).then_inc(l_la, 1)
                link(dve.tensor_tensor(lru_i[:], lru_i[:], lru_c[:], ALU.mult))
                dve.wait_ge(l_a, 3 * l + 3)
                dve.scalar_tensor_tensor(lru_r[:], lru_r[:], 1.0, lru_y[:], ALU.add, ALU.mult).then_inc(l_m, 1)
                dve.wait_ge(l_mq, l + 1)
                link(dve.tensor_tensor(lru_i[:], lru_i[:], lru_y[:], ALU.mult))
                for n in range(LB):
                    last = dve.tensor_tensor_scan(lru_y[:, n, :], lru_x[:, n, 0:T], lru_i[:, n, :], 0.0, ALU.mult, ALU.add)
                last.then_inc(l_h, 1)
                for u in range(4):
                    b, half = u // 2, u % 2
                    dve.wait_ge(l_ht, 4 * l + u + 1)
                    c0 = half * 4 * LBW
                    dve.tensor_tensor(tok[:, b, RW + DW + c0:RW + DW + c0 + 384], ps[:, 4 + u, 0:384],
                                      proj[:, b, C_LG + c0:C_LG + c0 + 384], ALU.mult).then_inc(mix_done, 1)

                g = G[f"out{l}"]

                def out_panel(q, j, g=g):
                    dve.wait_ge(evac_done, g.evacuated(q))
                    cols = bass.ds(q * PANEL, PANEL)
                    dve.tensor_tensor(yg[:, :, cols], tok[:, :, cols],
                                      post_g[:, cols].unsqueeze(1).to_broadcast([P, TB, PANEL]), ALU.mult).then_inc(yg_done, 1)

                last_panel = panels(g, out_panel, v=T_OUT[l], late=lambda: dve.wait_ge(pg_in, 16 * (l + 1)))

                def last_x(l=l, last_panel=last_panel):
                    last_panel()
                    dve.wait_ge(y_ssq, 8 * (l + 1))
                    link(dve.tensor_reduce(ssq[:], y_sums[:], AX.X, ALU.add))
                    dve.tensor_scalar(msq[:], ssq[:], 1.0 / D, EPS, ALU.mult, ALU.add).then_inc(y_ms, 1)
                    dve.wait_ge(y_sd, l + 1)
                    link(dve.reciprocal(rstd[:], sdev[:]))
                    dve.wait_ge(yg_done, 4 * (l + 1))
                    for n in range(D // PANEL):
                        cols = slice(n * PANEL, n * PANEL + PANEL)
                        for b in range(TB):
                            last = dve.scalar_tensor_tensor(x[:, b, cols], yg[:, b, cols], rstd[:, b:b + 1],
                                                            x[:, b, cols], ALU.mult, ALU.add)
                        last.then_inc(res_added, 1)
            last_x()


def tables():
    t = np.arange(T)
    c = {"ident": np.eye(P, dtype=np.float32)}
    c["tval"] = np.broadcast_to(t - P, (P, T)).astype(np.float32)
    rows = np.arange(P)[:, None]
    c["parity"] = np.concatenate([(rows // 16) % 2 == np.arange(2), rows // 64 == np.arange(2)], axis=1).astype(np.float32)
    d = t[:, None] - t[None, :]
    keep = [(d >= 0) & (d % dil == 0) & (d <= win) for win, dil in ((128, 1), (512, 4), (2048, 16))]
    far = [np.where(k, d, BIG).astype(np.float32) for k in keep]
    c["dist"] = np.concatenate([f[0:P, 0:P] for f in far] + [f[P:T, :] for f in far], axis=1)
    s = np.exp2(-8.0 * np.arange(1, NG * HEADS + 1) / (NG * HEADS)).reshape(HEADS, NG)
    c["slope"] = np.broadcast_to(-s, (P, HEADS, NG)).astype(np.float32)
    mask = np.where(d >= 0, 0.0, -BIG)
    c["causal"] = np.concatenate([mask[0:P, 0:P], mask[P:T, :]], axis=1).astype(np.float32)
    log_g = np.log1p(-np.exp2(-5.0 - np.arange(RH)))
    full = np.where(d >= 0, np.exp(np.maximum(d, 0)[None] * log_g[:, None, None]), 0.0) * DH ** -0.5
    full = full.transpose(2, 0, 1)
    c["decay"] = np.concatenate([full[0:P], full[P:T, :, P:T]], axis=2).astype(np.float32)
    inv_r = 1.0 / (10000.0 ** np.linspace(0.0, 1.0, DH // 2))
    inv_d = 1.0 / (10000.0 ** (np.arange(0, DH // 2, 2) / (DH // 2)))
    c["inv"] = np.broadcast_to(np.concatenate([inv_r, inv_d]), (P, 96)).astype(np.float32)
    return {k: np.ascontiguousarray(v) for k, v in c.items()}


def kernel(**inputs):
    import concourse.bacc as bacc
    from concourse.bass_utils import run_bass_kernel_spmd

    nc = bacc.Bacc("TRN2", target_bir_lowering=False, num_devices=1)
    arrays, w, c = {}, {}, {}
    for group, source, prefix in ((w, inputs, "in"), (c, tables(), "const")):
        for name, a in source.items():
            a = np.ascontiguousarray(a)
            key = f"{prefix}_{name}"
            arrays[key] = a
            group[name] = nc.dram_tensor(key, a.shape, mybir.dt.from_np(a.dtype), kind="ExternalInput").ap()
    out = nc.dram_tensor("out_x", (1, T, D), F32, kind="ExternalOutput").ap()
    with nc.allow_non_contiguous_dma(reason="a few small parameter vectors and tables go to columns"):
        program(nc, w, c, out)
    r = run_bass_kernel_spmd(nc, [arrays], core_ids=[0])
    return r.results[0]["out_x"]
```

```python
import math
from contextlib import ExitStack

import numpy as np

import concourse.bass as bass
from concourse import mybir

F32 = mybir.dt.float32
F32R = mybir.dt.float32r
BF16 = mybir.dt.bfloat16
I32 = mybir.dt.int32
ALU = mybir.AluOpType
ACT = mybir.ActivationFunctionType
AX = mybir.AxisListType

P = 128
T = 256
TB = T // P
D = 2048
KT = D // P
DFF = 5632
EPS = 1e-6
PANEL = 512
CK = 2
RAW = 8
AHEAD = 6
SPLIT = 2
HEADS, DH = 16, 128
NG = 3
RH, DIFH = 6, 4
RW, DW, LW = RH * DH, DIFH * DH, 768
LB, LBW = 8, 96
DIN = 4 * RW + 4 * DW + 2 * LW
C_RQ, C_RK, C_RV, C_RG = 0, RW, 2 * RW, 3 * RW
C_DQ, C_DK, C_DV, C_DG = 4 * RW, 4 * RW + DW, 4 * RW + 2 * DW, 4 * RW + 3 * DW
CONV = 4
C_LX, C_LG = 4 * RW + 4 * DW, 4 * RW + 4 * DW + LW
NLAYER2 = 2
NIN = DIN // PANEL
FIRST_IN = C_LX // PANEL
BIG = 1.0e30
MAGIC = 12582912.0
TWO_PI_BELOW = 6.2831850
C1 = 6.28125
C2 = float(np.float32(round((2 * math.pi - C1) * 2**21) / 2**21))
C3 = 2 * math.pi - C1 - C2
KB = 1024


class Gemm:

    def __init__(self, name, w, chunks, panels, cols, chunk0, panel0, slot_uses):
        self.name, self.w, self.chunks, self.panels, self.cols = name, w, chunks, panels, cols
        self.chunk0, self.panel0, self.slot_uses = chunk0, panel0, list(slot_uses)
        self.first = int(name == "glu")
        self.per = [chunks // RAW + (s < chunks % RAW) for s in range(RAW)]

    def chunk(self, q, k):
        return q * self.chunks + (self.chunk0 + k)

    def raw_count(self, q, k):
        s = k % RAW
        return q * (16 * self.per[s]) + 16 * (self.slot_uses[s] + k // RAW + 1)

    def done(self, q):
        return (q + 1) * self.chunks + (self.chunk0 + SPLIT)

    def evacuated(self, q):
        return q + (self.panel0 + 3)

    @property
    def all_evacuated(self):
        return self.panel0 + self.panels + 2


def plan(w):
    plain = lambda i, j: i * (2 * PANEL) + j * PANEL
    table = [
        ("glu", w["w_glu"][0], D, 8, lambda i, j: i * PANEL + ((1 - j) * D - PANEL)),
        ("gu0", w["w_gate_up"][0], D, 22, lambda i, j: i * PANEL + j * DFF),
        ("dn0", w["w_down"][0], DFF, 4, plain),
        ("k", w["w_kv"], D, 4, plain),
        ("v", w["w_kv"], D, 4, lambda i, j: i * (2 * PANEL) + (j * PANEL + D)),
        ("q", w["w_q"][0], D, 12, plain),
        ("o", w["w_o"][0], D, 4, plain),
        ("gu1", w["w_gate_up"][1], D, 22, lambda i, j: i * PANEL + j * DFF),
        ("dn1", w["w_down"][1], DFF, 4, plain),
    ]
    for l in range(NLAYER2):
        table += [(f"in{l}", w["w_in_2"][l], D, 13, plain), (f"out{l}", w["w_out_2"][l], D, 4, plain)]
    gemms, chunk0, panel0, uses = {}, 0, 0, [0] * RAW
    for name, ap, k, panels, cols in table:
        g = Gemm(name, ap, k // (P * CK), panels, cols, chunk0, panel0, uses)
        gemms[name] = g
        chunk0 += g.chunks * panels
        panel0 += panels
        uses = [u + n * panels for u, n in zip(uses, g.per)]
    return gemms


def in_turn(eng, steps, count=HEADS):
    def edge(n):
        for offset, step in steps:
            if 0 <= n + offset < count:
                step(n + offset, (n + offset) % 2)

    for n in range(-3, 2):
        edge(n)
    with eng.Fori(1, count // 2 - 2) as i:
        for j in range(2):
            for offset, step in steps:
                step(i * 2 + (j + offset), (j + offset) % 2)
    for n in range(count - 4, count + 2):
        edge(n)


class Links:

    def __init__(self, eng, sem):
        self.eng, self.sem, self.n = eng, sem, 0

    def link(self, instruction):
        self.n += 1
        instruction.then_inc(self.sem, 1)
        self.eng.wait_ge(self.sem, self.n)


GAINS = ["mix0", "ffn0", "kv", "mix1", "ffn1", "pre0", "pre1", "skip"]
TURNS = ["mix0", "ffn0", "kv", "mix1", "ffn1", "pre0", None, "pre1", None]
T_MIX0, T_FFN0, T_KV, T_MIX1, T_FFN1 = range(5)
T_PRE, T_OUT = (5, 7), (6, 8)
N_MIX0, N_FFN0, N_KV, N_FFN1 = range(4)
N_PRE = (4, 5)
NORM_OF = {T_FFN0: N_FFN0, T_KV: N_KV, T_FFN1: N_FFN1, T_PRE[0]: N_PRE[0], T_PRE[1]: N_PRE[1]}


def program(nc, w, c, out):
    G = plan(w)
    with ExitStack() as ctx:
        def sb(name, shape, dt=F32):
            return ctx.enter_context(nc.sbuf_tensor(name, shape, dt))

        def sem(name):
            return ctx.enter_context(nc.semaphore(name))

        x = sb("x_res", [P, TB, D])
        raw = sb("raw", [P, RAW, CK, PANEL])
        whi = sb("w_hi", [P, SPLIT, CK, PANEL], F32R)
        wlo = sb("w_lo", [P, SPLIT, CK, PANEL], F32R)
        ident = sb("ident", [P, P])
        gains = sb("gains", [P, len(GAINS), KT])
        half_pi = sb("half_pi", [P, 1])
        ssq = sb("ssq", [P, TB])
        msq = sb("msq", [P, TB])
        sdev = sb("sdev", [P, TB])
        rstd = sb("rstd", [P, TB])
        y_sums = sb("y_sums", [P, TB, D // PANEL])
        ps = ctx.enter_context(nc.psum_tensor("ps", [P, 8, 512], F32))

        def at(kb, name, shape, dt=F32):
            with ExitStack() as scope:
                if kb:
                    scope.enter_context(nc.sbuf_tensor(f"before_{name}", [P, int(kb * KB // 4)], F32))
                return scope.enter_context(nc.sbuf_tensor(name, shape, dt))

        xh = at(0, "x_hi", [P, KT, T], F32R)
        xl = at(16, "x_lo", [P, KT, T], F32R)
        gbuf = at(32, "gbuf", [P, TB, PANEL])
        hbuf = at(36, "hbuf", [P, TB, PANEL])
        junk = at(32, "junk", [P, D], BF16)
        tok = at(40, "tok", [P, TB, D])
        hh = at(40, "h_hi", [P, DFF // P, T], F32R)
        hl = at(84, "h_lo", [P, DFF // P, T], F32R)

        raw_ready = [sem(f"raw_ready{s}") for s in range(RAW)]
        hi_done = sem("hi_done")
        lo_done = sem("lo_done")
        chunk_used = sem("chunk_used")
        evac_done = sem("evac_done")
        glu_added = sem("glu_added")
        x_tr = sem("x_tr")
        x_hi_done = sem("x_hi_done")
        x_done = sem("x_done")
        head_norm = sem("head_norm")
        hd_ms = sem("hd_ms")
        hd_sd = sem("hd_sd")
        nrm_ssq, nrm_ms, nrm_sd, xn_ready = sem("nrm_ssq"), sem("nrm_ms"), sem("nrm_sd"), sem("xn_ready")
        tr_ready, tr_hi, tr_lo = sem("tr_ready"), sem("tr_hi"), sem("tr_lo")
        head_link, s5_link = sem("head_link"), sem("s5_link")
        x_in, ident_in, par_in, out_done = sem("x_in"), sem("ident_in"), sem("par_in"), sem("out_done")
        gain_tr, gain_ready, const_ready = sem("gain_tr"), sem("gain_ready"), sem("const_ready")
        dve_link, act_link, pool_link, pe_link = sem("dve_link"), sem("act_link"), sem("pool_link"), sem("pe_link")

        q4 = at(0, "s5_q4", [P, 4, 4, T])
        r_re = at(16, "s5_r_re", [P, 4, T])
        r_im = at(20, "s5_r_im", [P, 4, T])
        cs = at(24, "s5_cs", [P, 2, 2, 4, T])
        p4 = at(40, "s5_p4", [P, 4, 4, T])
        uT = at(56, "s5_uT", [P, KT, T])
        bb_re = at(72, "s5_bb_re", [P, 64, 16])
        bb_im = at(76, "s5_bb_im", [P, 64, 16])
        c_re = at(80, "s5_c_re", [P, KT, 64])
        c_im = at(84, "s5_c_im", [P, KT, 64])
        turn = at(88, "s5_turn", [P, 2, 4, T])
        whole = at(96, "s5_whole", [P, 4, T])
        tval = at(100, "s5_tval", [P, T])
        us = at(131, "s5_us", [P, 2, T])
        bx = at(102, "s5_bx", [P, 2, 4, 2, 16])
        cx = at(103, "s5_cx", [P, 2, 2, 64])
        bt = at(104, "s5_bt", [P, 2, 2, P])
        ct3 = at(128, "s5_ct3", [P, 2, 3, P])
        b_re = at(107, "s5_b_re", [P, 64, 16])
        b_im = at(111, "s5_b_im", [P, 64, 16])
        par = at(115, "s5_par", [P, 20, 64])
        a_rows = at(121, "s5_a_rows", [P, P])
        dt_rows = at(121.5, "s5_dt_rows", [64, 2])
        dt_wide = at(122, "s5_dt_wide", [64, 2, 64])
        parity = at(122.5, "s5_parity", [P, 4])
        gain_rows = at(123, "gain_rows", [P, P])
        absf = at(124, "s5_absf", [P, 4, T])
        s5_in, s5_bc_in = sem("s5_in"), sem("s5_bc_in")
        s5_a_tr, s5_dt_wide, s5_dt_tr = sem("s5_a_tr"), sem("s5_dt_wide"), sem("s5_dt_tr")
        s5_log, s5_exp = sem("s5_log"), sem("s5_exp")
        s5_par = sem("s5_par")
        s5_stage = sem("s5_stage")
        s5_tr = sem("s5_tr")
        s5_bt = sem("s5_bt")
        s5_ct = sem("s5_ct")
        s5_b = sem("s5_b")
        s5_rot = sem("s5_rot")
        s5_add = sem("s5_add")
        s5_re = sem("s5_re")
        s5_turn, s5_whole, s5_frac = sem("s5_turn"), sem("s5_whole"), sem("s5_frac")
        s5_cs = sem("s5_cs")
        s5_q = sem("s5_q")
        s5_qp = sem("s5_qp")
        s5_y = sem("s5_y")
        s5_z = sem("s5_z")
        s5_g, s5_gh, s5_gl = sem("s5_g"), sem("s5_gh"), sem("s5_gl")

        qT = at(40, "qT", [P, NG * HEADS, T])
        kT = at(88, "kT", [P, HEADS, T])
        vt = at(104, "v_tok", [P, TB, HEADS * DH])
        dist = at(120, "dist", [P, NG * 128 + NG * 256])
        qst = at(124.5, "q_stage", [P, 2, NG, T])
        score = at(130.5, "score", [P, 2, 1152])
        wsum = at(32, "wsum", [P, 2, 384])
        wT = at(35, "wT", [P, 384])
        vst = at(36.5, "v_stage", [P, 2, TB, DH])
        slope = at(139.5, "slope", [P, HEADS, NG])
        at_small = at(139.75, "at_small", [P, 16])
        negm, den, rden = at_small[:, 0:4], at_small[:, 4:8], at_small[:, 8:12]
        qkg = at(140.25, "qk_gain", [P, 4])
        gqk = at(140.5, "gqk", [P, NG])
        hssq = at(139.875, "hssq", [P, 3, TB, 4])
        at_inv = sem("at_inv")
        at_in, gqk_ready = sem("at_in"), sem("gqk_ready")
        at_sum, at_qs, at_vs, at_sc, at_bias, at_max = sem("at_sum"), sem("at_qs"), sem("at_vs"), sem("at_sc"), sem("at_bias"), sem("at_max")
        at_exp, at_w, at_pt, at_wt = sem("at_exp"), sem("at_w"), sem("at_pt"), sem("at_wt")
        at_pv, at_oh, at_o = sem("at_pv"), sem("at_oh"), sem("at_o")

        rope_a = at(32, "rope_a", [P, 4, 512])
        sq2 = at(32, "sq2", [P, TB, RW])
        dw = at(133, "dif_w", [P, 384])
        dwT = at(134.5, "dif_wT", [P, 384])
        sub_g = at(141, "sub_g", [P, DH])
        lam_v = at(141.5, "lam_v", [P, 4, 64])
        lam_p = at(140, "lam_p", [P, 2, 64])
        proj = at(56, "proj", [P, TB, DIN])
        ret_T = [at(56 + 26 * n, f"ret_T{n}", [P, RH, T]) for n in range(TB)]
        dif_T = [at(68 + 26 * n, f"dif_T{n}", [P, DIFH, T]) for n in range(TB)]
        post_g = at(56, "post_g", [P, D])
        yg = at(64, "yg", [P, TB, D])
        decay = at(108, "decay", [P, RH, 384])
        rope_cs = at(117, "rope_cs", [P, 2, TB, 96])
        rope_t = at(118.5, "rope_t", [P, 4, TB, 96])
        pos_i = at(121.5, "pos_i", [P, TB], I32)
        inv = at(121.75, "inv_freq", [P, 96])
        causal = at(122.25, "causal", [P, 384])
        m2 = at(123.75, "m2_small", [P, 64])
        ra = at(124, "ret_a", [P, 2, 384])
        ds = at(127, "dif_s", [P, 2, 2, 384])
        lru_x = at(40, "lru_x", [LBW, LB, T + 3])
        lru_c = at(32, "lru_c", [LBW, LB, T])
        lru_i = at(64, "lru_i", [LBW, LB, T])
        lru_y = at(90, "lru_y", [LBW, LB, T])
        lru_r = at(124, "lru_r", [LBW, LB, T])
        lru_wa = at(133, "lru_wa", [LBW, LB, LBW])
        lru_wx = at(136, "lru_wx", [LBW, LB, LBW])
        lru_rows = at(139, "lru_rows", [64, LBW])
        lru_p = at(139.5, "lru_p", [LBW, 8, LB])
        lru_t = at(139.75, "lru_t", [LBW, 6, LB])
        pos_f, lam_e, lam_col = m2[:, 0:2], m2[:, 2:4], m2[:, 4:5]
        hs_ret, hs_ret_sd, hs_dif, hs_dif_sd = m2[:, 5:17], m2[:, 17:29], m2[:, 29:37], m2[:, 37:45]
        dif_small = at(136, "dif_small", [P, 2, 16])
        dnegm, dden, drden, dlr = (dif_small[:, :, n:n + 4] for n in (0, 4, 8, 12))
        b2_in, b2l_in, lru_in, pg_in = sem("b2_in"), sem("b2l_in"), sem("lru_in"), sem("pg_in")
        rope_ang, rope_ready, rope_done = sem("rope_ang"), sem("rope_ready"), sem("rope_done")
        lam_dot, lam_exp = sem("lam_dot"), sem("lam_exp")
        gates_done = sem("gates_done")
        a_tr, a_ev = sem("a_tr"), sem("a_ev")
        r_s, r_a, r_o, r_ev = sem("r_s"), sem("r_a"), sem("r_o"), sem("r_ev")
        d_s, d_m, d_max, d_exp, d_w = sem("d_s"), sem("d_m"), sem("d_max"), sem("d_exp"), sem("d_w")
        d_pt, d_wt, d_o, d_ev = sem("d_pt"), sem("d_wt"), sem("d_o"), sem("d_ev")
        h_ms, h_sd, dg_ready = sem("h_ms"), sem("h_sd"), sem("dg_ready")
        l_row, l_par, l_e, l_e2, l_l8 = sem("l_row"), sem("l_par"), sem("l_e"), sem("l_e2"), sem("l_l8")
        l_xt, l_x, l_conv, l_g, l_sig = sem("l_xt"), sem("l_x"), sem("l_conv"), sem("l_g"), sem("l_sig")
        l_la, l_a, l_m, l_mq, l_h = sem("l_la"), sem("l_a"), sem("l_m"), sem("l_mq"), sem("l_h")
        l_ht, mix_lru, mix_ret, mix_dif = sem("l_ht"), sem("mix_lru"), sem("mix_ret"), sem("mix_dif")
        rstd_ready, y_ssq, y_ms, y_sd, res_added = sem("rstd_ready"), sem("y_ssq"), sem("y_ms"), sem("y_sd"), sem("res_added")

        d_den = sem("d_den")
        yg_done, sub_ready = sem("yg_done"), sem("sub_ready")

        block = ctx.enter_context(nc.Block())

        def ret_tile(i):
            part, n = [(0, i), (1, i - 4), (0, i - 4), (1, i - 6)][(i >= 4) + (i >= 8) + (i >= 10)]
            return ret_T[part], n

        def panel_ps(j):
            return ps[:, 2 * j:2 * j + 2, :]

        def x_written(v, n):
            return [(x_in, 32), (glu_added, n + 1), (evac_done, G["dn0"].evacuated(n)),
                    (evac_done, G["o"].evacuated(n)), (evac_done, G["dn1"].evacuated(n)),
                    (res_added, n + 1)][v]

        @block.sync
        def _(sp):
            sp.dma_start(a_rows[0:64, :], w["ssm_a_re"][0].rearrange("(j g) p -> j (g p)", g=2)).then_inc(s5_in, 16)
            sp.dma_start(a_rows[64:128, :], w["ssm_a_im"][0].rearrange("(j g) p -> j (g p)", g=2)).then_inc(s5_in, 16)
            sp.dma_start(dt_rows[:], w["ssm_log_dt"][0].rearrange("(j g) -> j g", g=2)).then_inc(s5_in, 16)
            sp.dma_start(tval[:], c["tval"]).then_inc(s5_in, 16)
            sp.dma_start(ident[:], c["ident"]).then_inc(ident_in, 16)
            for b in range(TB):
                sp.dma_start(x[:, b], w["x"][0, b * P:b * P + P]).then_inc(x_in, 16)
            rows = [w["mix_norm"][0], w["ffn_norm"][0], w["kv_norm"], w["mix_norm"][1], w["ffn_norm"][1],
                    w["pre_norm_g_2"][0], w["pre_norm_g_2"][1], w["ssm_d"][0]]
            for n, row in enumerate(rows):
                sp.dma_start(gain_rows[KT * n:KT * n + KT, :], row.rearrange("(k p) -> k p", p=P)).then_inc(par_in, 16)

            def load(g, q, col):
                for k in range(g.chunks):
                    sp.wait_ge(lo_done, g.chunk(q, k) + 1)
                    sp.dma_start(raw[:, k % RAW], g.w[k * CK * P:(k + 1) * CK * P, bass.ds(col, PANEL)]
                                 .rearrange("(t p) n -> p t n", p=P)).then_inc(raw_ready[k % RAW], 16)

            sp.wait_ge(s5_bc_in, 16 * 5)
            for g in G.values():
                if g.name.startswith("in"):
                    for q in range(NIN - FIRST_IN):
                        load(g, q, (FIRST_IN + q) * PANEL)
                    with sp.Fori(1, FIRST_IN // 2 + 1) as i:
                        for j in range(2):
                            load(g, i * 2 + (j + 1), i * (2 * PANEL) + (j - 2) * PANEL)
                    continue
                with sp.Fori(g.first, g.panels // 2 + g.first) as i:
                    for j in range(2):
                        load(g, i * 2 + (j - 2 * g.first), g.cols(i, j))
                if g.panels % 2:
                    load(g, g.panels - 1, g.cols(g.panels // 2, 0))
            for n in range(D // PANEL):
                sp.wait_ge(res_added, 4 * (NLAYER2 - 1) + n + 1)
                cols = slice(n * PANEL, n * PANEL + PANEL)
                sp.dma_start(out[0, :, cols].rearrange("(b p) d -> p b d", p=P), x[:, :, cols]).then_inc(out_done, 16)
            sp.wait_ge(out_done, 16 * (D // PANEL))

        @block.gpsimd
        def _(pool):
            pl = Links(pool, pool_link)
            for start, n in ((s5_frac, 1), (s5_add, 1), (s5_qp, 2), (at_sum, 3)):
                pool.nop().then_inc(start, n)
            pl.link(pool.memset(half_pi[:], math.pi / 2))
            pool.nop().then_inc(const_ready, 1)
            state_major = lambda a: a[0].rearrange("(j g) p h -> (g p) j h", g=2)
            pool.dma_start(parity[:], c["parity"]).then_inc(s5_bc_in, 16)
            pool.dma_start(b_re[:], state_major(w["ssm_b_re"])).then_inc(s5_bc_in, 16)
            pool.dma_start(b_im[:], state_major(w["ssm_b_im"])).then_inc(s5_bc_in, 16)
            pool.dma_start(c_re[:], w["ssm_c_re"][0].rearrange("g h p -> (g h) p")
                           .rearrange("(k q) p -> q k p", q=P)).then_inc(s5_bc_in, 16)
            pool.dma_start(c_im[:], w["ssm_c_im"][0].rearrange("g h p -> (g h) p")
                           .rearrange("(k q) p -> q k p", q=P)).then_inc(s5_bc_in, 16)
            pool.wait_ge(s5_bc_in, 16 * 5)
            pool.wait_ge(s5_par, 2)
            pool.wait_ge(tr_hi, 8)

            def s5_stages(i, j):
                pool.wait_ge(s5_tr, i + 1)
                for n, b in enumerate((bb_re, bb_im)):
                    pool.tensor_tensor(bx[:, n], b[:, bass.ds(i * 4, 4), :].unsqueeze(2).to_broadcast([P, 4, 2, 16]),
                                       parity[:, 2:4].unsqueeze(1).unsqueeze(3).to_broadcast([P, 4, 2, 16]), ALU.mult)
                for n, cc in enumerate((c_re, c_im)):
                    last = pool.tensor_tensor(cx[:, n], cc[:, bass.ds(i, 1), :].to_broadcast([P, 2, 64]),
                                              parity[:, 0:2].unsqueeze(2).to_broadcast([P, 2, 64]), ALU.mult)
                last.then_inc(s5_stage, 1)

            def s5_fraction(i, j):
                pool.wait_ge(s5_whole, i + 1)
                pool.tensor_tensor(turn[:, j], turn[:, j], whole[:], ALU.subtract).then_inc(s5_frac, 1)

            def s5_rotated_im(i, j):
                pool.wait_ge(s5_rot, i + 2)
                pool.tensor_tensor(p4[:, 2], p4[:, 2], p4[:, 3], ALU.subtract).then_inc(s5_add, 1)

            def s5_re_products(i, j):
                pool.wait_ge(s5_re, i + 1)
                pool.wait_ge(s5_y, i + 2)
                pool.tensor_tensor(q4[:, 2], r_re[:], cs[:, j, 1], ALU.mult)
                pool.tensor_tensor(q4[:, 0], r_re[:], cs[:, j, 0], ALU.mult).then_inc(s5_qp, 1)

            in_turn(pool, [(0, s5_rotated_im), (0, s5_re_products), (2, s5_fraction), (3, s5_stages)], KT)

            pool.wait_ge(x_done, 2 * 11 + 2)
            pool.wait_ge(evac_done, G["dn0"].all_evacuated)
            pool.dma_start(dist[:], c["dist"]).then_inc(at_in, 16)
            pool.dma_start(slope[:], c["slope"]).then_inc(at_in, 16)
            pool.dma_start(qkg[:, 0:NG], w["q_norm"][0].rearrange("g e -> e g"),
                           ).then_inc(at_in, 16)
            pool.dma_start(qkg[:, NG:NG + 1], w["k_norm"].rearrange("(e a) -> e a", a=1)).then_inc(at_in, 16)
            pool.wait_ge(gqk_ready, 1)
            pool.wait_ge(x_done, 2 * 27 + 2)
            pool.wait_ge(evac_done, G["q"].all_evacuated)

            def at_queries(h, j):
                pool.wait_ge(at_sc, h + 1)
                pool.tensor_tensor(qst[:, j], qT[:].rearrange("p (g h) t -> p g h t", g=NG)[:, :, bass.ds(h, 1), :]
                                   .rearrange("p g a t -> p g (a t)"),
                                   gqk[:].unsqueeze(2).to_broadcast([P, NG, T]), ALU.mult).then_inc(at_qs, 1)

            def at_sums(h, j):
                pool.wait_ge(at_exp, h + 1)
                pool.wait_ge(at_pt, h + 1)
                s, o = score[:, j], wsum[:, j]
                group = lambda g: ((o[:, 0:P], s[:, g * P:g * P + P]),
                                   (o[:, P:3 * P], s[:, 384 + g * T:384 + g * T + T]))
                for (dst, first), (_, second) in zip(group(0), group(1)):
                    last = pool.tensor_tensor(dst, first, second, ALU.add)
                last.then_inc(at_sum, 1)
                pool.wait_ge(at_sum, h * 2 + 4)
                for dst, third in group(2):
                    last = pool.tensor_tensor(dst, dst, third, ALU.add)
                last.then_inc(at_sum, 1)

            in_turn(pool, [(0, at_sums), (3, at_queries)])

            pool.wait_ge(evac_done, G["dn1"].all_evacuated)
            for dst, src in ((decay, c["decay"]), (inv, c["inv"]), (causal, c["causal"])):
                pool.dma_start(dst[:], src).then_inc(b2_in, 16)
            pool.dma_start(pos_i[:], w["positions_2"][0].rearrange("(b p) -> p b", p=P)).then_inc(b2_in, 16)
            for l in range(NLAYER2):
                if l:
                    pool.wait_ge(mix_lru, 4 * l)
                    pool.wait_ge(mix_dif, l)
                for n, name in enumerate(("q1", "k1", "q2", "k2")):
                    pool.dma_start(lam_v[:, n, :], w[f"diff_lambda_{name}_2"][l].partition_broadcast(P)).then_inc(b2l_in, 16)
                pool.dma_start(sub_g[:], w["diff_subln_g_2"][l].partition_broadcast(P)).then_inc(b2l_in, 16)
                pool.dma_start(lru_rows[0:32, :], w["lru_conv_w_2"][l].rearrange("a (n p) -> (a n) p", p=LBW)).then_inc(lru_in, 16)
                for n, name in enumerate(("conv_b", "ba", "bx", "lambda")):
                    pool.dma_start(lru_rows[32 + 8 * n:40 + 8 * n, :], w[f"lru_{name}_2"][l]
                                   .rearrange("(n p) -> n p", p=LBW)).then_inc(lru_in, 16)
                pool.dma_start(lru_wa[:], w["lru_wa_2"][l].rearrange("n k j -> k n j")).then_inc(lru_in, 16)
                pool.dma_start(lru_wx[:], w["lru_wx_2"][l].rearrange("n k j -> k n j")).then_inc(lru_in, 16)
                pool.wait_ge(gates_done, 3 * l + 3)
                pool.wait_ge(sub_ready, l + 1)
                for b in range(TB):
                    gate_cols = proj[:, b, C_DG:C_DG + DW].rearrange("p (h e) -> p h e", e=DH)
                    last = pool.tensor_tensor(gate_cols, gate_cols, sub_g[:].unsqueeze(1).to_broadcast([P, DIFH, DH]),
                                              ALU.mult)
                last.then_inc(dg_ready, 1)
                pool.wait_ge(mix_lru, 4 * l + 4)
                pool.wait_ge(mix_ret, l + 1)
                pool.wait_ge(mix_dif, l + 1)
                pool.dma_start(post_g[:], w["post_norm_g_2"][l].partition_broadcast(P)).then_inc(pg_in, 16)

        @block.scalar
        def _(act):
            al = Links(act, act_link)

            def split(g, q, ks):
                for k in ks:
                    act.wait_ge(raw_ready[k % RAW], g.raw_count(q, k))
                    act.wait_ge(chunk_used, g.chunk(q, k) + 1)
                    act.activation(whi[:, k % SPLIT], raw[:, k % RAW], ACT.Copy).then_inc(hi_done, 1)

            def whole_panel(g, q):
                act.wait_ge(chunk_used, g.done(q))

            def gate(g, q, j, func, scaled=True):
                whole_panel(g, q)
                act.wait_ge(evac_done, g.evacuated(q) - 1)
                for b in range(TB):
                    last = act.activation(gbuf[:, b], ps[:, 2 * j + b, :], func,
                                          scale=rstd[:, b:b + 1] if scaled else 1.0)
                last.then_inc(evac_done, 1)

            def store(g, q, j, dst, scaled=False):
                whole_panel(g, q)
                for b in range(TB):
                    last = act.activation(dst[:, b], ps[:, 2 * j + b, :], ACT.Copy,
                                          scale=rstd[:, b:b + 1] if scaled else 1.0)
                last.then_inc(evac_done, 1)

            def raw_heads(g, q, j, n):
                whole_panel(g, q)
                act.wait_ge(head_norm, n + 1)
                for b in range(TB):
                    last = act.activation(gbuf[:, b], ps[:, 2 * j + b, :], ACT.Copy, scale=rstd[:, b:b + 1])
                last.then_inc(evac_done, 1)

            def head_sd(n):
                act.wait_ge(hd_ms, n + 1)
                act.activation(hssq[:, 1], hssq[:, 0], ACT.Sqrt).then_inc(hd_sd, 1)

            def hidden_hi(xi, i):
                for u in range(2):
                    act.wait_ge(x_tr, xi * 2 + (u + 3))
                    act.activation(hh[:, bass.ds(i * 4 + 2 * u, 2), :],
                                   ps[:, 4 + u, :].rearrange("p (a t) -> p a t", a=2), ACT.Copy).then_inc(x_hi_done, 1)

            def heads_T(xi, dst, h0):
                for u in range(2):
                    act.wait_ge(x_tr, xi * 2 + (u + 3))
                    act.activation(dst[:, bass.ds(h0 + 2 * u, 2), :],
                                   ps[:, 4 + u, :].rearrange("p (a t) -> p a t", a=2), ACT.Copy).then_inc(x_done, 1)

            def sums_of_squares(v):
                act.wait_ge(*x_written(v, 3))
                for b in range(TB):
                    if b:
                        act.wait_ge(nrm_ssq, 2 * v + b)
                    act.activation(junk[:], x[:, b, :], ACT.Square, accum_out=ssq[:, b:b + 1]).then_inc(nrm_ssq, 1)

            def root(v):
                act.wait_ge(nrm_ms, v + 1)
                act.activation(sdev[:], msq[:], ACT.Sqrt).then_inc(nrm_sd, 1)

            def turn_hi(v, u):
                gain = TURNS[v]
                act.wait_ge(tr_ready, 8 * v + u + 1)
                for kk in range(2):
                    kt = 2 * u + kk
                    src = ps[:, 4 + u % 4, kk * T:(kk + 1) * T]
                    dst = uT[:, kt, :] if v == T_MIX0 else xh[:, kt, :]
                    scale = 1.0 if gain is None else gains[:, GAINS.index(gain), kt:kt + 1]
                    last = act.activation(dst, src, ACT.Copy, scale=scale)
                last.then_inc(tr_hi, 1)

            def first_panel(g, pending=None, late=None, v=None, pending_mid=None):
                split(g, 0, [0])
                if pending:
                    pending()
                for k in range(g.chunks):
                    if v is not None:
                        turn_hi(v, k)
                    if k:
                        split(g, 0, [k])
                    if k == 5 and v in NORM_OF:
                        sums_of_squares(NORM_OF[v])
                    if k == 4 and pending_mid:
                        pending_mid()
                    if k == 6 and v in NORM_OF:
                        root(NORM_OF[v])
                    if k == 7 and late:
                        late()

            def panels(g, evac, after=None, pending=None, late=None, v=None, mid=None, pending_mid=None):
                first_panel(g, pending, late, v, pending_mid)
                if v in NORM_OF:
                    act.wait_ge(rstd_ready, NORM_OF[v])

                def one(q, j):
                    split(g, q, range(2))
                    evac(q - 1, 1 - j)
                    split(g, q, range(2, 5))
                    if mid:
                        mid(q - 1, 1 - j)
                    split(g, q, range(5, g.chunks))
                    if after:
                        after(q - 1, 1 - j)
                one(1, 1)
                pairs = g.panels // 2
                if pairs > 2:
                    with act.Fori(1, pairs) as i:
                        for j in range(2):
                            one(i * 2 + j, j)
                elif pairs == 2:
                    for j in range(2):
                        one(2 + j, j)
                last = 2 * pairs - 1
                if g.panels % 2:
                    one(g.panels - 1, 0)
                    last = g.panels - 1
                return (lambda: evac(last, last % 2)), (lambda: after(last, last % 2)) if after else None

            act.nop().then_inc(s5_ct, 1)
            act.nop().then_inc(s5_cs, 1)
            act.nop().then_inc(at_wt, 1)
            act.wait_ge(const_ready, 1)
            act.wait_ge(s5_in, 16 * 4)
            act.wait_ge(x_in, 32)
            for b in range(TB):
                if b:
                    act.wait_ge(nrm_ssq, b)
                act.activation(junk[:], x[:, b, :], ACT.Square, accum_out=ssq[:, b:b + 1]).then_inc(nrm_ssq, 1)
            act.wait_ge(s5_par, 1)
            act.activation(par[:, 10, :], par[:, 8, :], ACT.Sin, scale=TWO_PI_BELOW).then_inc(s5_exp, 1)
            al.link(act.activation(par[:, 9, :], par[:, 8, :], ACT.Abs))
            act.activation(par[:, 11, :], par[:, 9, :], ACT.Sin, bias=half_pi[:], scale=-TWO_PI_BELOW).then_inc(s5_exp, 1)
            root(N_MIX0)
            act.wait_ge(gain_tr, 1)
            act.activation(gains[:].rearrange("p a k -> p (a k)"), ps[:, 0, 0:P], ACT.Copy).then_inc(gain_ready, 1)
            act.wait_ge(gain_ready, 1)
            for u in range(8):
                turn_hi(T_MIX0, u)

            def s5_turns(i, j):
                for s in range(4):
                    last = act.activation(turn[:, j, s], tval[:], ACT.Copy, scale=par[:, 8, bass.ds(i * 4 + s, 1)])
                last.then_inc(s5_turn, 1)

            def s5_trig(i, j):
                act.wait_ge(s5_frac, i + 2)
                act.wait_ge(s5_q, i + 1)
                act.wait_ge(s5_qp, i + 1)
                act.activation(cs[:, j, 1], turn[:, j], ACT.Sin, scale=TWO_PI_BELOW)
                act.wait_ge(s5_cs, i + 1)
                act.activation(absf[:], turn[:, j], ACT.Abs).then_inc(act_link, 1)
                act.wait_ge(act_link, i + 2)
                act.activation(cs[:, j, 0], absf[:], ACT.Sin, bias=half_pi[:], scale=-TWO_PI_BELOW).then_inc(s5_cs, 1)

            def s5_b_matrices(i, j):
                act.wait_ge(s5_tr, i + 2)
                act.wait_ge(s5_b, i + 1)
                act.activation(us[:, j], uT[:, bass.ds(i, 1), :].rearrange("p a t -> p (a t)"), ACT.Copy)
                act.activation(bt[:, j], ps[:, 4, 0:2 * P].rearrange("p (a t) -> p a t", a=2), ACT.Copy).then_inc(s5_bt, 1)

            def s5_c_matrices(i, j):
                act.wait_ge(s5_y, i + 1)
                act.activation(ct3[:, j, 0, :], ps[:, 4, 2 * P:3 * P], ACT.Copy)
                act.activation(ct3[:, j, 1:3, :], ps[:, 4, 2 * P:4 * P].rearrange("p (a t) -> p a t", a=2),
                               ACT.Copy, scale=-1.0).then_inc(s5_ct, 1)

            assert al.n == 1
            in_turn(act, [(1, s5_trig), (1, s5_c_matrices), (2, s5_turns), (2, s5_b_matrices)], KT)
            al.n += KT
            for n in range(4):
                act.wait_ge(s5_z, 4 * n + 5)
                act.activation(uT[:, 4 * n:4 * n + 4, :], uT[:, 4 * n:4 * n + 4, :], ACT.Gelu_apprx_tanh).then_inc(s5_g, 1)
            for n in range(4):
                act.wait_ge(s5_g, n + 1)
                act.activation(xh[:, 4 * n:4 * n + 4, :], uT[:, 4 * n:4 * n + 4, :], ACT.Copy).then_inc(s5_gh, 1)

            panels(G["glu"], lambda q, j: gate(G["glu"], q, j, ACT.Sigmoid, False) if j == 0 else None)

            def ffn(layer, v, pending=None):
                g, x0 = G[f"gu{layer}"], (0, 27)[layer]
                def one(i, j):
                    q = i * 2 + j
                    split(g, q, range(2))
                    if j == 1:
                        gate(g, q - 1, 0, ACT.Silu)
                    split(g, q, range(2, g.chunks))
                    if j == 0:
                        hidden_hi(i + (x0 - 1), i - 1)
                first_panel(g, pending, None, v)
                act.wait_ge(rstd_ready, NORM_OF[v])
                one(0, 1)
                with act.Fori(1, g.panels // 2) as i:
                    for j in range(2):
                        one(i, j)
                n = g.panels // 2
                panels(G[f"dn{layer}"], lambda q, j: None, late=lambda: hidden_hi(n + x0 - 1, n - 1))

            ffn(0, T_FFN0)
            def head_panels(g, n0, dst, **more):
                mid = lambda q, j: head_sd(q + n0)
                evac, after = panels(g, lambda q, j: raw_heads(g, q, j, q + n0),
                                     lambda q, j: heads_T(q + (n0 + 11), dst, q * 4), mid=mid, **more)
                return evac, lambda: mid(g.panels - 1, 1), after

            last_heads, last_root, last_T = head_panels(G["k"], 0, kT, v=T_KV)
            last_v, _ = panels(G["v"], lambda q, j: store(G["v"], q, j, vt[:, :, bass.ds(q * PANEL, PANEL)], True),
                               pending=last_heads, pending_mid=last_root, late=last_T)
            last_heads, last_root, last_T = head_panels(G["q"], 4, qT, v=T_MIX1, pending=last_v)
            last_heads()
            last_root()
            last_T()

            def at_a(h, j):
                act.wait_ge(at_max, h + 1)
                for b, (lo, hi) in enumerate(((0, 384), (384, 1152))):
                    last = act.activation(score[:, j, lo:hi], score[:, j, lo:hi], ACT.Exp,
                                          bias=negm[:, 2 * j + b:2 * j + b + 1],
                                          accum_out=den[:, 2 * j + b:2 * j + b + 1])
                last.then_inc(at_exp, 1)

            def at_b(h, j):
                act.wait_ge(at_pt, h + 3)
                act.wait_ge(at_pv, h + 2)
                act.activation(wT[:], ps[:, 6, 0:384], ACT.Copy).then_inc(at_wt, 1)

            def at_c(h, j):
                act.wait_ge(at_pv, h + 3)
                act.activation(xh[:, bass.ds(h, 1), :].rearrange("p a t -> p (a t)"), ps[:, 7, 0:T],
                               ACT.Copy).then_inc(at_oh, 1)

            def at_stage_values(h, j):
                act.wait_ge(at_pv, h + 1)
                act.activation(vst[:, j], vt[:, :, bass.ds(h * DH, DH)], ACT.Copy).then_inc(at_vs, 1)

            def at_divide(h, j):
                act.wait_ge(at_inv, h + 1)
                act.wait_ge(at_sum, h * 2 + 5)
                for b, (lo, hi) in enumerate(((0, P), (P, 3 * P))):
                    last = act.activation(wsum[:, j, lo:hi], wsum[:, j, lo:hi], ACT.Copy,
                                          scale=rden[:, 2 * j + b:2 * j + b + 1])
                last.then_inc(at_w, 1)

            in_turn(act, [(-2, at_c), (-1, at_b), (0, at_stage_values), (0, at_divide), (1, at_a)])
            panels(G["o"], lambda q, j: None)
            ffn(1, T_FFN1)

            def rope_tables():
                act.wait_ge(rope_ang, 1)
                act.activation(rope_cs[:, 1], rope_t[:, 0], ACT.Sin, scale=TWO_PI_BELOW)
                al.link(act.activation(rope_t[:, 1], rope_t[:, 0], ACT.Abs))
                act.activation(rope_cs[:, 0], rope_t[:, 1], ACT.Sin, bias=half_pi[:],
                               scale=-TWO_PI_BELOW).then_inc(rope_ready, 1)

            last_out = None
            for l in range(NLAYER2):
                def small(l=l):
                    if l == 0:
                        rope_tables()
                    act.wait_ge(lam_dot, l + 1)
                    act.activation(lam_e, lam_e, ACT.Exp).then_inc(lam_exp, 1)

                g = G[f"in{l}"]
                def in_panel(q, steps={}):
                    for k in range(g.chunks):
                        split(g, q, [k])
                        if k == 1:
                            in_evacuate(q - 1)
                        if k in steps:
                            steps[k]()

                def in_evacuate(q):
                    store(g, q, q % 2, proj[:, :, bass.ds((q + FIRST_IN) % NIN * PANEL, PANEL)], True)

                def silu(q, n, col, width):
                    act.wait_ge(evac_done, g.evacuated(q))
                    act.activation(proj[:, :, col:col + width], proj[:, :, col:col + width],
                                   ACT.Silu).then_inc(gates_done, 1)

                def lru_inputs(units):
                    for u in units:
                        act.wait_ge(l_xt, 4 * l + u + 1)
                        act.activation(lru_x[:, 2 * u:2 * u + 2, 3:T + 3], ps[0:LBW, 4 + u, :]
                                       .rearrange("p (a t) -> p a t", a=2), ACT.Copy).then_inc(l_x, 1)

                def lru_params():
                    act.wait_ge(l_row, l + 1)
                    act.activation(lru_p[:].rearrange("p a n -> p (a n)"), ps[0:LBW, 7, 0:64], ACT.Copy).then_inc(l_par, 1)
                    lru_inputs(range(3))

                def lru_exp():
                    lru_inputs([3])
                    act.wait_ge(l_e, l + 1)
                    act.activation(lru_t[:, 1, :], lru_t[:, 0, :], ACT.Exp, scale=-1.0).then_inc(l_e2, 1)

                def lru_gate(n):
                    def step():
                        act.wait_ge(l_g, LB * l + n + 1)
                        act.activation(lru_r[:, n, :], ps[0:LBW, 4 + n % 4, 0:T], ACT.Sigmoid, bias=lru_p[:, 5, n:n + 1])
                        act.activation(lru_i[:, n, :], ps[0:LBW, 4 + n % 4, T:2 * T], ACT.Sigmoid,
                                       bias=lru_p[:, 6, n:n + 1]).then_inc(l_sig, 1)
                    return step

                def lru_decay():
                    act.wait_ge(l_la, l + 1)
                    act.activation(lru_x[:, :, 0:T], lru_r[:], ACT.Exp).then_inc(l_a, 1)
                    act.activation(lru_y[:], lru_r[:], ACT.Tanh, scale=-1.0).then_inc(l_a, 1)

                def lru_square():
                    act.wait_ge(l_a, 3 * l + 2)
                    act.activation(lru_r[:], lru_x[:, :, 0:T], ACT.Square).then_inc(l_a, 1)

                def lru_root():
                    act.wait_ge(l_m, l + 1)
                    act.activation(lru_y[:], lru_r[:], ACT.Sqrt).then_inc(l_mq, 1)

                def ret_turned(u, last):
                    def step():
                        act.wait_ge(a_tr, 10 * l + last + 1)
                        dst, n = ret_tile(2 * u)
                        act.activation(dst[:, n:n + 2, :], ps[:, 4 + u % 4, :].rearrange("p (a t) -> p a t", a=2),
                                       ACT.Copy).then_inc(a_ev, 1)
                    return step

                def dif_turned(units):
                    act.wait_ge(a_tr, 10 * l + 10)
                    for u in units:
                        act.activation(dif_T[u // 2][:, 2 * (u % 2):2 * (u % 2) + 2, :],
                                       ps[:, 4 + u, :].rearrange("p (a t) -> p a t", a=2), ACT.Copy).then_inc(a_ev, 1)

                def ret_out(h):
                    def step():
                        act.wait_ge(r_o, RH * l + h + 1)
                        act.activation(tok[:, :, DH * h:DH * h + DH], ps[:, 6 + h % 2, 0:TB * DH]
                                       .rearrange("p (b e) -> p b e", b=TB), ACT.Copy).then_inc(r_ev, 1)
                    return step

                def ret_root():
                    act.wait_ge(h_ms, 2 * l + 1)
                    act.activation(hs_ret_sd, hs_ret, ACT.Sqrt).then_inc(h_sd, 1)

                def dif_exp(h):
                    act.wait_ge(d_max, DIFH * l + h + 1)
                    for m in range(2):
                        for b, (lo, hi) in enumerate(((0, 128), (128, 384))):
                            n = 2 * m + b
                            last = act.activation(ds[:, h % 2, m, lo:hi], ds[:, h % 2, m, lo:hi], ACT.Exp,
                                                  bias=dnegm[:, h % 2, n:n + 1], accum_out=dden[:, h % 2, n:n + 1])
                    last.then_inc(d_exp, 1)

                def dif_weights(h):
                    act.wait_ge(d_pt, DIFH * l + h + 1)
                    act.activation(dwT[:], ps[:, 2, 0:384], ACT.Copy).then_inc(d_wt, 1)

                def dif_out(h):
                    act.wait_ge(d_o, DIFH * l + h + 1)
                    act.activation(tok[:, :, RW + DH * h:RW + DH * h + DH], ps[:, 3, 0:TB * DH]
                                   .rearrange("p (b e) -> p b e", b=TB), ACT.Copy).then_inc(d_ev, 1)

                first_panel(g, last_out, small, T_PRE[l])
                act.wait_ge(rstd_ready, N_PRE[l])
                in_panel(1)
                in_panel(2, {5: lru_params, 7: lru_exp})
                in_panel(3, {3: lambda: silu(2, 0, C_LG, LW)})
                in_panel(4, {n + 2: lru_gate(n) for n in range(6)})
                in_panel(5, {0: lru_gate(6), 1: lru_gate(7), 4: lru_decay, 6: lru_square})
                in_panel(6, {3: lru_root})
                in_panel(7, {6: lambda: act.wait_ge(l_ht, 4 * (l + 1))})
                in_panel(8)
                in_panel(9, {0: ret_turned(0, 3), 1: ret_turned(1, 3), 2: ret_turned(2, 3), 3: ret_turned(3, 3),
                             5: ret_turned(4, 5), 6: ret_turned(5, 5), 7: lambda: silu(8, 1, C_RG, RW)})
                in_panel(10, {n + 4: ret_out(n) for n in range(4)})
                in_panel(11, {0: ret_out(4), 1: ret_out(5), 7: ret_root})
                in_panel(12, {0: lambda: dif_turned((0, 1)), 1: lambda: dif_turned((2, 3)),
                              5: lambda: dif_exp(0), 6: lambda: dif_exp(1)})
                dif_exp(2)
                in_evacuate(12)
                dif_weights(0)
                silu(12, 2, C_DG, DW)
                dif_out(0)
                dif_weights(1)
                dif_exp(3)
                dif_out(1)
                for h in (2, 3):
                    dif_weights(h)
                    dif_out(h)
                act.wait_ge(h_ms, 2 * l + 2)
                act.activation(hs_dif_sd, hs_dif, ACT.Sqrt).then_inc(h_sd, 1)
                g = G[f"out{l}"]

                def out_panel(q, j, g=g, l=l):
                    cols = bass.ds(q * PANEL, PANEL)
                    store(g, q, j, tok[:, :, cols])
                    act.wait_ge(evac_done, g.evacuated(q))
                    for b in range(TB):
                        act.wait_ge(y_ssq, q * 2 + (8 * l + b))
                        act.activation(junk[:, 0:PANEL], tok[:, b, cols], ACT.Square,
                                       accum_out=y_sums[:, b, bass.ds(q, 1)]).then_inc(y_ssq, 1)

                last_panel, _ = panels(g, out_panel, v=T_OUT[l])

                def last_out(last_panel=last_panel, l=l):
                    last_panel()
                    act.wait_ge(y_ms, l + 1)
                    act.activation(sdev[:], msq[:], ACT.Sqrt).then_inc(y_sd, 1)
            last_out()

        @block.tensor
        def _(pe):
            pe.nop().then_inc(chunk_used, SPLIT)
            pe.nop().then_inc(s5_tr, 1)
            for start in (s5_b, s5_y, x_tr, at_sc, at_pt, at_pv):
                pe.nop().then_inc(start, 2)

            def chunk(g, q, j, k, hi, lo):
                pe.wait_ge(lo_done, g.chunk(q, k) + (AHEAD + 1))
                for t in range(CK):
                    kt = CK * k + t
                    for b in range(TB):
                        tokens = slice(b * P, b * P + P)
                        for n, (xs, ws) in enumerate(((hi, whi), (hi, wlo), (lo, whi))):
                            last = pe.matmul(ps[:, 2 * j + b, :], xs[:, kt, tokens], ws[:, k % SPLIT, t, :],
                                             start=kt == 0 and n == 0,
                                             stop=kt == CK * g.chunks - 1 and n == 2)
                last.then_inc(chunk_used, 1)

            def panel(g, q, j, hi=xh, lo=xl, between=None):
                pe.wait_ge(evac_done, g.evacuated(q) - 2)
                for k in range(g.chunks):
                    chunk(g, q, j, k, hi, lo)
                    if between and k == 6:
                        between()

            def panels(g, hi=xh, lo=xl, after=None, first=panel):
                def one(q, j):
                    panel(g, q, j, hi, lo, (lambda: after(q - 1, 1 - j)) if after else None)
                first(g, 0, 0, hi, lo)
                one(1, 1)
                pairs = g.panels // 2
                if pairs > 2:
                    with pe.Fori(1, pairs) as i:
                        for j in range(2):
                            one(i * 2 + j, j)
                elif pairs == 2:
                    for j in range(2):
                        one(2 + j, j)
                if g.panels % 2:
                    one(g.panels - 1, 0)

            def turn_hbuf(xi, ready, count):
                pe.wait_ge(ready, count)
                for u in range(2):
                    pe.wait_ge(x_done, xi * 2 + (u + 1))
                    for f in range(2):
                        for b in range(TB):
                            last = pe.transpose(ps[:, 4 + u, f * T + b * P:f * T + b * P + P],
                                                hbuf[:, b, (2 * u + f) * P:(2 * u + f + 1) * P], ident[:])
                    last.then_inc(x_tr, 1)

            def source_ready(v, u):
                if v == T_MIX0:
                    pe.wait_ge(xn_ready, 2)
                elif v in NORM_OF:
                    pe.wait_ge(*x_written(NORM_OF[v], u // 2))
                elif v in T_OUT:
                    l = T_OUT.index(v)
                    if u == 0:
                        pe.wait_ge(d_m, DIFH * (l + 1))
                    pe.wait_ge(*((mix_ret, l + 1) if u < 3 else (mix_dif, l + 1) if u < 5 else (mix_lru, 4 * (l + 1))))

            def turn_unit(v, u):
                source = x if v in NORM_OF or v == T_MIX1 else tok
                source_ready(v, u)
                if u >= 4:
                    pe.wait_ge(*((tr_hi, u - 3) if v == T_MIX0 else (tr_lo, 8 * (v - 1) + u - 3)))
                for kk in range(2):
                    for b in range(TB):
                        last = pe.transpose(ps[:, 4 + u % 4, kk * T + b * P:kk * T + b * P + P],
                                            source[:, b, (2 * u + kk) * P:(2 * u + kk + 1) * P], ident[:])
                last.then_inc(tr_ready, 1)

            def turned(v):
                def first(g, q, j, hi, lo):
                    for u in range(4):
                        turn_unit(v, u)
                    pe.wait_ge(evac_done, g.evacuated(0) - 2)
                    for k in range(g.chunks):
                        pe.wait_ge(tr_lo, 8 * (v - 1) + k + 1)
                        chunk(g, 0, 0, k, hi, lo)
                        if k + 4 < 8:
                            turn_unit(v, k + 4)
                return first

            pe.wait_ge(ident_in, 16)
            pe.wait_ge(s5_in, 16 * 4)
            pe.transpose(ps[:, 1, 0:P], a_rows[:], ident[:]).then_inc(s5_a_tr, 1)
            pe.wait_ge(s5_dt_wide, 1)
            pe.transpose(ps[:, 2, 0:64], dt_wide[:].rearrange("p a b -> p (a b)"), ident[0:64, 0:64]).then_inc(s5_dt_tr, 1)
            pe.wait_ge(par_in, 16 * len(GAINS))
            pe.transpose(ps[:, 0, 0:P], gain_rows[:], ident[:]).then_inc(gain_tr, 1)
            for u in range(8):
                turn_unit(T_MIX0, u)

            def s5_transposes(i, j):
                pe.wait_ge(s5_stage, i + 1)
                pe.wait_ge(s5_ct, i + 1)
                mats = [bx[:, 0].rearrange("p a g h -> p (a g h)"), bx[:, 1].rearrange("p a g h -> p (a g h)"),
                        cx[:, 0].rearrange("p g h -> p (g h)"), cx[:, 1].rearrange("p g h -> p (g h)")]
                for n, m in enumerate(mats):
                    last = pe.transpose(ps[:, 4, n * P:n * P + P], m, ident[:])
                last.then_inc(s5_tr, 1)

            def s5_in_products(i, j):
                pe.wait_ge(s5_bt, i + 1)
                pe.wait_ge(s5_rot, i + 1)
                for s in range(4):
                    rows = slice(32 * s, 32 * s + 32)
                    for m in range(2):
                        last = pe.matmul(ps[:, s, m * T:m * T + T], bt[rows, j, m, :], us[rows, j, :], start=True, stop=True)
                last.then_inc(s5_b, 1)

            def s5_outputs(i, j):
                pe.wait_ge(s5_q, i + 3)
                pe.wait_ge(s5_qp, i + 3)
                pe.wait_ge(s5_ct, i + 2)
                pe.wait_ge(s5_z, i + 1)
                for s in range(4):
                    rows = slice(32 * s, 32 * s + 32)
                    for n, m in enumerate((0, 1, 2, 2)):
                        last = pe.matmul(ps[rows, 5, 0:T], ct3[:, j, m, rows], q4[:, n, s, :], start=n == 0, stop=n == 3)
                last.then_inc(s5_y, 1)

            in_turn(pe, [(1, s5_in_products), (2, s5_transposes), (0, s5_outputs)], KT)

            def after_s5(g, q, j, hi, lo):
                for k in range(g.chunks):
                    pe.wait_ge(s5_gl, k // 2 + 1)
                    chunk(g, 0, 0, k, hi, lo)

            panels(G["glu"], first=after_s5)

            def ffn(layer, v):
                g, x0, n = G[f"gu{layer}"], (0, 27)[layer], G[f"gu{layer}"].panels // 2
                def hidden(i):
                    turn_hbuf(i + x0, evac_done, g.evacuated(i * 2 + 1))
                turned(v)(g, 0, 0, xh, xl)
                panel(g, 1, 1)
                with pe.Fori(1, n) as i:
                    panel(g, i * 2, 0, between=lambda: hidden(i - 1))
                    panel(g, i * 2 + 1, 1)

                def first(d, q, j, hi, lo):
                    pe.wait_ge(x_done, 2 * (x0 + n))
                    for k in range(d.chunks):
                        if k == 0:
                            pe.wait_ge(evac_done, d.evacuated(0) - 2)
                        if k == d.chunks - 2:
                            pe.wait_ge(x_done, 2 * (x0 + n) + 2)
                        chunk(d, 0, 0, k, hi, lo)
                        if k == 6:
                            hidden(n - 1)
                panels(G[f"dn{layer}"], hh, hl, first=first)

            ffn(0, T_FFN0)
            k_heads = lambda q, j: turn_hbuf(q + 11, head_norm, q + 2)
            q_heads = lambda q, j: turn_hbuf(q + 15, head_norm, q + 6)
            panels(G["k"], after=k_heads, first=turned(T_KV))
            panels(G["v"], first=lambda g, q, j, hi, lo: panel(g, 0, 0, hi, lo, lambda: k_heads(3, 1)))
            panels(G["q"], after=q_heads, first=turned(T_MIX1))
            q_heads(11, 1)

            def at_scores(h, j):
                pe.wait_ge(at_qs, h + 1)
                pe.wait_ge(at_bias, h + 1)
                for g in range(NG):
                    pe.matmul(ps[:, 3 * j, g * P:g * P + P], qst[:, j, g, 0:P],
                              kT[:, bass.ds(h, 1), 0:P].rearrange("p a t -> p (a t)"), start=True, stop=True)
                for g in range(NG):
                    last = pe.matmul(ps[:, 3 * j + 1 + g // 2, (g % 2) * T:(g % 2) * T + T], qst[:, j, g, P:T],
                                     kT[:, bass.ds(h, 1), :].rearrange("p a t -> p (a t)"), start=True, stop=True)
                last.then_inc(at_sc, 1)

            def at_turn(h, j):
                pe.wait_ge(at_w, h + 1)
                pe.wait_ge(at_wt, h + 1)
                for n in range(3):
                    last = pe.transpose(ps[:, 6, n * P:n * P + P], wsum[:, j, n * P:n * P + P], ident[:])
                last.then_inc(at_pt, 1)

            def at_values(h, j):
                pe.wait_ge(at_wt, h + 2)
                pe.wait_ge(at_vs, h + 1)
                pe.wait_ge(at_o, h + 1)
                o = ps[:, 7, 0:T]
                pe.matmul(o, vst[:, j, 0, :], wT[:, 0:T], start=True, stop=False)
                pe.matmul(o[:, P:T], vst[:, j, 1, :], wT[:, T:T + P], start=False, stop=True).then_inc(at_pv, 1)

            in_turn(pe, [(2, at_scores), (-1, at_values), (0, at_turn)])
            pe.wait_ge(at_o, HEADS + 1)
            panels(G["o"])
            ffn(1, T_FFN1)

            for l in range(NLAYER2):
                g = G[f"in{l}"]

                def in_panel(q, steps={}):
                    pe.wait_ge(evac_done, g.evacuated(q) - 2)
                    for k in range(g.chunks):
                        chunk(g, q, q % 2, k, xh, xl)
                        if k in steps:
                            steps[k]()

                def turn_cols(bank, cols, width, done):
                    for f, col in enumerate(cols):
                        for b in range(TB):
                            last = pe.transpose(ps[0:width, bank, f * T + b * P:f * T + b * P + P],
                                                proj[:, b, col:col + width], ident[:])
                    last.then_inc(done, 1)

                def lru_inputs(units):
                    for u in units:
                        turn_cols(4 + u, [C_LX + LBW * (2 * u + f) for f in range(2)], LBW, l_xt)

                def lru_params():
                    pe.wait_ge(lru_in, 16 * 7 * (l + 1))
                    pe.transpose(ps[0:LBW, 7, 0:64], lru_rows[:], ident[0:64, 0:64]).then_inc(l_row, 1)
                    pe.wait_ge(evac_done, g.evacuated(1))
                    lru_inputs(range(3))

                def lru_last_inputs():
                    pe.wait_ge(l_par, l + 1)
                    lru_inputs([3])

                def lru_gate(n):
                    def step():
                        if n == 0:
                            pe.wait_ge(l_conv, l + 1)
                            pe.wait_ge(l_x, 4 * (l + 1))
                        if n >= 4:
                            pe.wait_ge(l_sig, LB * l + n - 3)
                        bank = ps[0:LBW, 4 + n % 4]
                        pe.matmul(bank[:, 0:T], lru_wa[:, n, :], lru_c[:, n, :], start=True, stop=True)
                        pe.matmul(bank[:, T:2 * T], lru_wx[:, n, :], lru_c[:, n, :], start=True, stop=True).then_inc(l_g, 1)
                    return step

                def lru_outputs():
                    pe.wait_ge(l_h, l + 1)
                    for u in range(4):
                        b, half = u // 2, u % 2
                        for f in range(4):
                            last = pe.transpose(ps[:, 4 + u, f * LBW:f * LBW + LBW],
                                                lru_y[:, 4 * half + f, b * P:b * P + P], ident[0:LBW, 0:LBW])
                        last.then_inc(l_ht, 1)

                def ret_turns(units):
                    if 0 in units:
                        pe.wait_ge(rope_done, 2 * l + 1)
                        pe.wait_ge(mix_lru, 4 * (l + 1))
                    else:
                        pe.wait_ge(a_ev, 10 * l + 4)
                    for u in units:
                        turn_cols(4 + u % 4, [C_RQ + P * (2 * u + f) for f in range(2)], P, a_tr)

                def dif_turns():
                    pe.wait_ge(rope_done, 2 * l + 2)
                    pe.wait_ge(r_ev, RH * (l + 1))
                    for u in range(4):
                        turn_cols(4 + u, [C_DQ + P * (2 * u + f) for f in range(2)], P, a_tr)

                def r_scores(h):
                    if h == 0:
                        pe.wait_ge(a_ev, 10 * l + 6)
                    if h >= 2:
                        pe.wait_ge(r_a, RH * l + h - 1)
                    (q_at, q_n), (k_at, k_n) = ret_tile(h), ret_tile(RH + h)
                    q, k = q_at[:, q_n, :], k_at[:, k_n, :]
                    pe.matmul(ps[:, 4 + h % 2, 0:T], k[:, 0:P], q, start=True, stop=True)
                    pe.matmul(ps[:, 4 + h % 2, T:T + P], k[:, P:T], q[:, P:T], start=True, stop=True).then_inc(r_s, 1)

                def r_values(h):
                    pe.wait_ge(r_a, RH * l + h + 1)
                    if h >= 2:
                        pe.wait_ge(r_ev, RH * l + h - 1)
                    v = proj[:, :, C_RV + DH * h:C_RV + DH * h + DH]
                    o, a = ps[:, 6 + h % 2, :], ra[:, h % 2, :]
                    pe.matmul(o[:, 0:DH], a[:, 0:P], v[:, 0, :], start=True, stop=True)
                    pe.matmul(o[:, DH:2 * DH], a[:, P:T], v[:, 0, :], start=True, stop=False)
                    pe.matmul(o[:, DH:2 * DH], a[:, T:T + P], v[:, 1, :], start=False, stop=True).then_inc(r_o, 1)

                def retention(k):
                    def step():
                        if k < RH:
                            r_scores(k)
                        if k >= 2:
                            r_values(k - 2)
                    return step

                def d_scores(h):
                    if h == 0:
                        pe.wait_ge(a_ev, 10 * l + 10)
                    if h >= 2:
                        pe.wait_ge(d_m, DIFH * l + h - 1)
                    for m in range(2):
                        rows = slice(64 * m, 64 * m + 64)
                        s = ps[:, 4 + 2 * (h % 2) + m, :]
                        q, k = dif_T[0][rows, h, :], dif_T[1][rows, h, :]
                        pe.matmul(s[:, 0:P], q[:, 0:P], k[:, 0:P], start=True, stop=True)
                        last = pe.matmul(s[:, P:P + T], q[:, P:T], k, start=True, stop=True)
                    last.then_inc(d_s, 1)

                def d_turn(h):
                    pe.wait_ge(d_w, DIFH * l + h + 1)
                    pe.wait_ge(evac_done, g.evacuated(11))
                    if h:
                        pe.wait_ge(d_wt, DIFH * l + h)
                    for n in range(3):
                        last = pe.transpose(ps[:, 2, n * P:n * P + P], dw[:, n * P:n * P + P], ident[:])
                    last.then_inc(d_pt, 1)

                def d_values(h):
                    pe.wait_ge(d_wt, DIFH * l + h + 1)
                    if h:
                        pe.wait_ge(d_ev, DIFH * l + h)
                    v = proj[:, :, C_DV + DH * h:C_DV + DH * h + DH]
                    o = ps[:, 3, :]
                    pe.matmul(o[:, 0:DH], dwT[:, 0:P], v[:, 0, :], start=True, stop=True)
                    pe.matmul(o[:, DH:2 * DH], dwT[:, P:T], v[:, 0, :], start=True, stop=False)
                    pe.matmul(o[:, DH:2 * DH], dwT[:, T:T + P], v[:, 1, :], start=False, stop=True).then_inc(d_o, 1)

                turned(T_PRE[l])(g, 0, 0, xh, xl)
                in_panel(1)
                in_panel(2, {4: lru_params, 6: lru_last_inputs})
                in_panel(3)
                in_panel(4, {n: lru_gate(n) for n in range(LB)})
                in_panel(5)
                in_panel(6)
                in_panel(7, {2: lru_outputs})
                in_panel(8, {7: lambda: ret_turns(range(4))})
                in_panel(9, {4: lambda: ret_turns(range(4, 6))})
                in_panel(10, {k: retention(k) for k in range(8)})
                in_panel(11, {7: dif_turns})
                in_panel(12, {2: lambda: d_scores(0), 3: lambda: d_scores(1), 5: lambda: d_scores(2),
                              7: lambda: d_scores(3)})
                for h in range(DIFH):
                    d_turn(h)
                    d_values(h)
                panels(G[f"out{l}"], first=turned(T_OUT[l]))

        @block.vector
        def _(dve):
            dl = Links(dve, dve_link)
            link = dl.link
            dve.nop().then_inc(lo_done, AHEAD)
            for start, n in ((evac_done, 2), (x_done, 2), (head_norm, 1), (s5_rot, 1), (s5_q, 2), (s5_z, 1),
                             (at_bias, 2), (at_o, 1)):
                dve.nop().then_inc(start, n)

            def split(g, q, ks):
                for k in ks:
                    dve.wait_ge(hi_done, g.chunk(q, k) + 1)
                    dve.wait_ge(chunk_used, g.chunk(q, k) + 1)
                    dve.tensor_tensor(wlo[:, k % SPLIT], raw[:, k % RAW], whi[:, k % SPLIT].bitcast(F32),
                                      ALU.subtract).then_inc(lo_done, 1)

            def product(g, q, j, scaled=True):
                dve.wait_ge(chunk_used, g.done(q))
                dve.wait_ge(evac_done, g.evacuated(q) - 1)
                for b in range(TB):
                    last = dve.scalar_tensor_tensor(hbuf[:, b], ps[:, 2 * j + b, :], rstd[:, b:b + 1] if scaled else 1.0,
                                                    gbuf[:, b], ALU.mult, ALU.mult)
                last.then_inc(evac_done, 1)

            def residual(g, q, j):
                dve.wait_ge(chunk_used, g.done(q))
                cols = x[:, :, bass.ds(q * PANEL, PANEL)]
                dve.tensor_tensor(cols, panel_ps(j), cols, ALU.add).then_inc(evac_done, 1)

            def hidden_lo(fi, i):
                for u in range(2):
                    dve.wait_ge(x_hi_done, fi * 2 + (u + 1))
                    tiles = bass.ds(i * 4 + 2 * u, 2)
                    dve.tensor_tensor(hl[:, tiles, :], ps[:, 4 + u, :].rearrange("p (a t) -> p a t", a=2),
                                      hh[:, tiles, :].bitcast(F32), ALU.subtract).then_inc(x_done, 1)

            def mean(v):
                dve.wait_ge(nrm_ssq, 2 * v + 2)
                dve.tensor_scalar(msq[:], ssq[:], 1.0 / D, EPS, ALU.mult, ALU.add).then_inc(nrm_ms, 1)

            def inverse(v):
                dve.wait_ge(nrm_sd, v + 1)
                if v == N_MIX0:
                    link(dve.reciprocal(rstd[:], sdev[:]))
                else:
                    dve.reciprocal(rstd[:], sdev[:]).then_inc(rstd_ready, 1)
                    dve.wait_ge(rstd_ready, v)

            def turn_lo(v, u):
                gain = TURNS[v]
                dve.wait_ge(tr_hi, 8 * v + u + 1)
                for kk in range(2):
                    kt = 2 * u + kk
                    scale = 1.0 if gain is None else gains[:, GAINS.index(gain), kt:kt + 1]
                    last = dve.scalar_tensor_tensor(xl[:, kt, :], ps[:, 4 + u % 4, kk * T:(kk + 1) * T], scale,
                                                    xh[:, kt, :].bitcast(F32), ALU.mult, ALU.subtract)
                last.then_inc(tr_lo, 1)

            def first_panel(g, pending=None, late=None, v=None, pending_mid=None):
                split(g, 0, [0])
                if pending:
                    pending()
                for k in range(g.chunks):
                    if v is not None:
                        turn_lo(v, k)
                    if k:
                        split(g, 0, [k])
                    if k == 4 and pending_mid:
                        pending_mid()
                    if k == 6 and v in NORM_OF:
                        mean(NORM_OF[v])
                    if k == 7 and v in NORM_OF:
                        inverse(NORM_OF[v])
                    if k == 7 and late:
                        late()

            def panels(g, evac, pending=None, late=None, v=None, mid=None, pending_mid=None):
                def one(q, j):
                    split(g, q, range(2))
                    evac(q - 1, 1 - j)
                    split(g, q, range(2, 5))
                    if mid:
                        mid(q - 1, 1 - j)
                    split(g, q, range(5, g.chunks))
                first_panel(g, pending, late, v, pending_mid)
                one(1, 1)
                pairs = g.panels // 2
                if pairs > 2:
                    with dve.Fori(1, pairs) as i:
                        for j in range(2):
                            one(i * 2 + j, j)
                elif pairs == 2:
                    for j in range(2):
                        one(2 + j, j)
                last = 2 * pairs - 1
                if g.panels % 2:
                    one(g.panels - 1, 0)
                    last = g.panels - 1
                return lambda: evac(last, last % 2)

            def exp_to(dst, src, n, r, e, bits):
                link(dve.tensor_scalar(n, src, 1.0 / math.log(2.0), MAGIC, ALU.mult, ALU.add))
                link(dve.tensor_scalar(n, n, MAGIC, -127.0, ALU.subtract, ALU.max))
                link(dve.scalar_tensor_tensor(r, n, -0.693359375, src, ALU.mult, ALU.add))
                link(dve.scalar_tensor_tensor(r, n, 2.12194440054690583e-4, r, ALU.mult, ALU.add))
                link(dve.tensor_scalar(e, r, 1.0 / math.factorial(8), None, ALU.mult))
                for k in range(7, 0, -1):
                    link(dve.scalar_tensor_tensor(e, e, 1.0 / math.factorial(k), r, ALU.add, ALU.mult))
                link(dve.tensor_scalar(bits, n, 127.0, float(2**23), ALU.add, ALU.mult))
                link(dve.scalar_tensor_tensor(dst, e, 1.0, bits.bitcast(F32), ALU.add, ALU.mult))

            def turns_of(phi, ang, n):
                link(dve.tensor_scalar(n, ang, 1.0 / (2 * math.pi), MAGIC, ALU.mult, ALU.add))
                link(dve.tensor_scalar(n, n, MAGIC, None, ALU.subtract))
                for part in (C1, C2, C3):
                    link(dve.scalar_tensor_tensor(ang, n, -part, ang, ALU.mult, ALU.add))
                link(dve.tensor_scalar(phi, ang, 1.0 / (2 * math.pi), 0.5, ALU.mult, ALU.min))
                return dve.tensor_scalar(phi, phi, -0.5, None, ALU.max)

            V = lambda n: par[:, n, :]
            dve.wait_ge(s5_in, 16 * 4)
            dve.tensor_copy(dt_wide[:], dt_rows[:].unsqueeze(2).to_broadcast([64, 2, 64])).then_inc(s5_dt_wide, 1)
            dve.wait_ge(s5_a_tr, 1)
            dve.tensor_scalar(V(0), ps[:, 1, 0:64], -1e-4, None, ALU.min)
            link(dve.tensor_copy(V(1), ps[:, 1, 64:128]))
            dve.wait_ge(s5_dt_tr, 1)
            link(dve.tensor_copy(V(19), ps[:, 2, 0:64]))
            exp_to(V(2), V(19), V(6), V(7), V(17), V(18).bitcast(I32))
            link(dve.tensor_tensor(V(3), V(0), V(2), ALU.mult))
            exp_to(V(4), V(3), V(6), V(7), V(17), V(18).bitcast(I32))
            link(dve.tensor_tensor(V(5), V(1), V(2), ALU.mult))
            turns_of(V(8), V(5), V(6)).then_inc(s5_par, 1)
            mean(N_MIX0)
            inverse(N_MIX0)
            for b in range(TB):
                dve.tensor_scalar(tok[:, b, :], x[:, b, :], rstd[:, b:b + 1], None, ALU.mult).then_inc(xn_ready, 1)
            dve.wait_ge(s5_exp, 2)
            link(dve.tensor_tensor(V(12), V(4), V(11), ALU.mult))
            link(dve.tensor_tensor(V(13), V(4), V(10), ALU.mult))
            link(dve.tensor_tensor(V(14), V(0), V(0), ALU.mult))
            link(dve.tensor_tensor(V(17), V(1), V(1), ALU.mult))
            link(dve.tensor_tensor(V(14), V(14), V(17), ALU.add))
            link(dve.reciprocal(V(14), V(14)))
            link(dve.tensor_scalar(V(12), V(12), -1.0, None, ALU.add))
            for dst, (a, b), op in ((15, (0, 1), ALU.add), (16, (1, 0), ALU.subtract)):
                x_, y_ = (12, 13) if dst == 15 else (13, 12)
                link(dve.tensor_tensor(V(17), V(x_), V(0), ALU.mult))
                link(dve.tensor_tensor(V(18), V(y_), V(1), ALU.mult))
                link(dve.tensor_tensor(V(17), V(17), V(18), op))
                link(dve.tensor_tensor(V(dst), V(17), V(14), ALU.mult))
            dve.wait_ge(s5_bc_in, 16 * 5)
            wide = lambda n: V(n).unsqueeze(2).to_broadcast([P, 64, 16])
            tmp = whole[:].rearrange("p a t -> p (a t)").rearrange("p (j h) -> p j h", h=16)
            for dst, (m, n), op in ((bb_re, (b_re, b_im), ALU.subtract), (bb_im, (b_im, b_re), ALU.add)):
                link(dve.tensor_tensor(dst[:], m[:], wide(15), ALU.mult))
                link(dve.tensor_tensor(tmp, n[:], wide(16), ALU.mult))
                last = dve.tensor_tensor(dst[:], dst[:], tmp, op)
                if dst is bb_re:
                    link(last)
            last.then_inc(s5_par, 1)

            def s5_round(i, j):
                dve.wait_ge(s5_turn, i + 1)
                dve.wait_ge(s5_frac, i + 1)
                dve.tensor_scalar(whole[:], turn[:, j], MAGIC, MAGIC, ALU.add, ALU.subtract).then_inc(s5_whole, 1)

            def s5_rotate(i, j):
                cos, sin = cs[:, j, 0], cs[:, j, 1]
                dve.wait_ge(s5_cs, i + 2)
                dve.wait_ge(s5_b, i + 3)
                dve.wait_ge(s5_add, i + 1)
                in_re, in_im = ps[:, 0:4, 0:T], ps[:, 0:4, T:2 * T]
                dve.tensor_tensor(p4[:, 2], in_im, cos, ALU.mult)
                dve.tensor_tensor(p4[:, 3], in_re, sin, ALU.mult)
                dve.tensor_tensor(p4[:, 0], in_re, cos, ALU.mult)
                dve.tensor_tensor(p4[:, 1], in_im, sin, ALU.mult).then_inc(s5_rot, 1)

            def s5_scan(i, j, part, dst):
                for s in range(4):
                    mag = par[:, 4, bass.ds(i * 4 + s, 1)].to_broadcast([P, T])
                    last = dve.tensor_tensor_scan(dst[:, s, :], mag, p4[:, part, s, :], 0.0, ALU.mult, ALU.add)
                return last

            def s5_states(i, j):
                dve.wait_ge(s5_rot, i + 2)
                dve.tensor_tensor(p4[:, 0], p4[:, 0], p4[:, 1], ALU.add).then_inc(s5_link, 1)
                dve.wait_ge(s5_link, i * 2 + 1)
                dve.wait_ge(s5_qp, i + 2)
                s5_scan(i, j, 0, r_re).then_inc(s5_re, 1)
                dve.wait_ge(s5_add, i + 2)
                s5_scan(i, j, 2, r_im).then_inc(s5_link, 1)
                dve.wait_ge(s5_link, i * 2 + 2)
                dve.wait_ge(s5_y, i + 2)
                dve.tensor_tensor(q4[:, 1], r_im[:], cs[:, j, 1], ALU.mult)
                dve.tensor_tensor(q4[:, 3], r_im[:], cs[:, j, 0], ALU.mult).then_inc(s5_q, 1)

            def s5_skip(i, j):
                dve.wait_ge(s5_y, i + 3)
                u = uT[:, bass.ds(i, 1), :].rearrange("p a t -> p (a t)")
                dve.scalar_tensor_tensor(u, u, gains[:, GAINS.index("skip"), bass.ds(i, 1)], ps[:, 5, 0:T],
                                         ALU.mult, ALU.add).then_inc(s5_z, 1)

            dve.wait_ge(s5_par, 2)
            in_turn(dve, [(0, s5_rotate), (0, s5_states), (2, s5_round), (-1, s5_skip)], KT)
            for n in range(4):
                dve.wait_ge(s5_gh, n + 1)
                dve.tensor_tensor(xl[:, 4 * n:4 * n + 4, :], uT[:, 4 * n:4 * n + 4, :],
                                  xh[:, 4 * n:4 * n + 4, :].bitcast(F32), ALU.subtract).then_inc(s5_gl, 1)

            def glu(q, j):
                if j == 0:
                    return
                g = G["glu"]
                product(g, q, j, False)
                dve.wait_ge(evac_done, g.evacuated(q))
                cols = x[:, :, bass.ds((q - 1) * (PANEL // 2), PANEL)]
                dve.tensor_tensor(cols, cols, hbuf[:], ALU.add).then_inc(glu_added, 1)

            last_glu = panels(G["glu"], glu)

            def ffn(layer, v, pending):
                g, x0, n = G[f"gu{layer}"], (0, 27)[layer], G[f"gu{layer}"].panels // 2
                def last_product(i):
                    dve.wait_ge(x_tr, i * 2 + (2 * x0))
                    product(g, i * 2 - 1, 1)
                def one(i, j):
                    split(g, i * 2 + j, range(2))
                    if j == 0:
                        last_product(i)
                    split(g, i * 2 + j, range(2, g.chunks))
                    if j == 0:
                        hidden_lo(i + (11 * layer - 1), i - 1)
                first_panel(g, pending, None, v)
                one(0, 1)
                with dve.Fori(1, n) as i:
                    for j in range(2):
                        one(i, j)
                return panels(G[f"dn{layer}"], lambda q, j: residual(G[f"dn{layer}"], q, j),
                              pending=lambda: last_product(n), late=lambda: hidden_lo(11 * layer + n - 1, n - 1))

            last_dn = ffn(0, T_FFN0, last_glu)

            by_head = lambda t: t[:].rearrange("p b (h e) -> p b h e", e=DH)

            def head_squares(g, q, n, xi):
                dve.wait_ge(evac_done, g.evacuated(q))
                dve.wait_ge(x_tr, xi * 2 + 2)
                dve.tensor_tensor(hbuf[:], gbuf[:], gbuf[:], ALU.mult).then_inc(head_link, 1)
                dve.wait_ge(head_link, n * 3 + 1)
                dve.tensor_reduce(hssq[:, 0], by_head(hbuf), AX.X, ALU.add).then_inc(head_link, 1)
                dve.wait_ge(head_link, n * 3 + 2)
                dve.tensor_scalar(hssq[:, 0], hssq[:, 0], 1.0 / DH, EPS, ALU.mult, ALU.add).then_inc(hd_ms, 1)

            def head_rms(n):
                dve.wait_ge(hd_sd, n + 1)
                dve.reciprocal(hssq[:, 2], hssq[:, 1]).then_inc(head_link, 1)
                dve.wait_ge(head_link, n * 3 + 3)
                dve.tensor_tensor(by_head(hbuf), by_head(gbuf), hssq[:, 2].unsqueeze(3).to_broadcast([P, TB, 4, DH]),
                                  ALU.mult).then_inc(head_norm, 1)

            last_k = panels(G["k"], lambda q, j: head_squares(G["k"], q, q, q + 11), pending=last_dn, v=T_KV,
                            mid=lambda q, j: head_rms(q))
            panels(G["v"], lambda q, j: None, pending=last_k, pending_mid=lambda: head_rms(3))
            last_q = panels(G["q"], lambda q, j: head_squares(G["q"], q, q + 4, q + 15), v=T_MIX1,
                            mid=lambda q, j: head_rms(q + 4))
            last_q()
            head_rms(15)
            dve.wait_ge(at_in, 64)
            dve.tensor_scalar(gqk[:], qkg[:, 0:NG], qkg[:, NG:NG + 1], DH ** -0.5, ALU.mult, ALU.mult).then_inc(gqk_ready, 1)

            def at_a(h, j):
                dve.wait_ge(at_sc, h + 3)
                dve.wait_ge(at_sum, h * 2 + 1)
                for g in range(NG):
                    for lo, width, src in ((g * P, P, ps[:, 3 * j, g * P:g * P + P]),
                                           (3 * P + g * T, T, ps[:, 3 * j + 1 + g // 2, (g % 2) * T:(g % 2) * T + T])):
                        last = dve.scalar_tensor_tensor(score[:, j, lo:lo + width], dist[:, lo:lo + width],
                                                        slope[:, bass.ds(h, 1), g:g + 1].rearrange("p a b -> p (a b)"),
                                                        src, ALU.mult, ALU.add)
                last.then_inc(at_bias, 1)

            def at_top(h, j):
                dve.wait_ge(at_bias, h + 3)
                dve.tensor_reduce(negm[:, 2 * j:2 * j + 1], score[:, j, 0:384], AX.X, ALU.max, negate=True)
                dve.tensor_reduce(negm[:, 2 * j + 1:2 * j + 2], score[:, j, 384:1152], AX.X, ALU.max,
                                  negate=True).then_inc(at_max, 1)

            def at_inverse(h, j):
                dve.wait_ge(at_exp, h + 1)
                dve.reciprocal(rden[:, 2 * j:2 * j + 2], den[:, 2 * j:2 * j + 2]).then_inc(at_inv, 1)

            def at_c(h, j):
                dve.wait_ge(at_oh, h + 1)
                flat = lambda t: t[:, bass.ds(h, 1), :].rearrange("p a t -> p (a t)")
                dve.tensor_tensor(flat(xl), ps[:, 7, 0:T], flat(xh).bitcast(F32), ALU.subtract).then_inc(at_o, 1)

            in_turn(dve, [(1, at_a), (0, at_inverse), (1, at_top), (-2, at_c)])
            last_o = panels(G["o"], lambda q, j: residual(G["o"], q, j))
            last_x = ffn(1, T_FFN1, last_o)

            def angles():
                dve.wait_ge(b2_in, 64)
                link(dve.tensor_copy(pos_f, pos_i[:]))
                for b in range(TB):
                    link(dve.tensor_scalar(rope_t[:, 2, b], inv[:], pos_f[:, b:b + 1], None, ALU.mult))
                turns_of(rope_t[:, 0], rope_t[:, 2], rope_t[:, 3]).then_inc(rope_ang, 1)

            def lam_of(l, lam_init):
                dve.wait_ge(b2l_in, 16 * 5 * (l + 1))
                link(dve.tensor_tensor(lam_p[:], lam_v[:, 0:4:2, :], lam_v[:, 1:4:2, :], ALU.mult))
                dve.tensor_reduce(lam_e, lam_p[:], AX.X, ALU.add).then_inc(lam_dot, 1)
                dve.wait_ge(lam_exp, l + 1)
                link(dve.tensor_tensor(lam_col, lam_e[:, 0:1], lam_e[:, 1:2], ALU.subtract))
                link(dve.tensor_scalar(lam_col, lam_col, lam_init, None, ALU.add))
                dve.tensor_scalar(sub_g[:], sub_g[:], 1.0 - lam_init, None, ALU.mult).then_inc(sub_ready, 1)

            for l in range(NLAYER2):
                def small(l=l):
                    if l == 0:
                        angles()
                    lam_of(l, 0.8 - 0.6 * math.exp(-0.3 * l))

                g = G[f"in{l}"]

                def in_panel(q, steps={}):
                    for k in range(g.chunks):
                        split(g, q, [k])
                        if k in steps:
                            steps[k]()

                z = lru_p[:, 7, :]
                tt = lambda n: lru_t[:, n, :]

                def lru_abs():
                    dve.wait_ge(l_par, l + 1)
                    dve.scalar_tensor_tensor(tt(0), z, -1.0, z, ALU.mult, ALU.max).then_inc(l_e, 1)
                    link(dve.memset(lru_x[:, :, 0:3], 0.0))

                def lru_log_start():
                    dve.wait_ge(l_e2, l + 1)
                    link(dve.tensor_scalar(tt(2), tt(1), 2.0, None, ALU.add))
                    link(dve.reciprocal(tt(2), tt(2)))
                    link(dve.tensor_tensor(tt(2), tt(2), tt(1), ALU.mult))
                    link(dve.tensor_tensor(tt(3), tt(2), tt(2), ALU.mult))
                    link(dve.tensor_scalar(tt(4), tt(3), 1.0 / 19, None, ALU.mult))
                    link(dve.tensor_scalar(tt(5), z, 0.0, 8.0, ALU.min, ALU.mult))

                def lru_log_rest():
                    for k in range(17, 1, -2):
                        link(dve.scalar_tensor_tensor(tt(4), tt(4), 1.0 / k, tt(3), ALU.add, ALU.mult))
                    link(dve.scalar_tensor_tensor(tt(4), tt(4), 1.0, tt(2), ALU.add, ALU.mult))
                    link(dve.scalar_tensor_tensor(tt(5), tt(4), -16.0, tt(5), ALU.mult, ALU.add))

                def lru_conv(k):
                    def step():
                        dve.wait_ge(l_x, 4 * (l + 1))
                        for n in range(LB):
                            src = lru_x[:, n, k:k + T]
                            if k == 0:
                                last = dve.tensor_scalar(lru_c[:, n, :], src, lru_p[:, 0, n:n + 1], lru_p[:, 4, n:n + 1],
                                                         ALU.mult, ALU.add)
                            else:
                                last = dve.scalar_tensor_tensor(lru_c[:, n, :], src, lru_p[:, k, n:n + 1],
                                                                lru_c[:, n, :], ALU.mult, ALU.add)
                        if k < CONV - 1:
                            link(last)
                        else:
                            last.then_inc(l_conv, 1)
                    return step

                def lru_log_a():
                    dve.wait_ge(l_sig, LB * (l + 1))
                    dve.tensor_tensor(lru_r[:], lru_r[:], tt(5).unsqueeze(2).to_broadcast([LBW, LB, T]),
                                      ALU.mult).then_inc(l_la, 1)

                def lru_input_gate():
                    dve.wait_ge(l_conv, l + 1)
                    link(dve.tensor_tensor(lru_i[:], lru_i[:], lru_c[:], ALU.mult))

                def lru_mult():
                    dve.wait_ge(l_a, 3 * l + 3)
                    dve.scalar_tensor_tensor(lru_r[:], lru_r[:], 1.0, lru_y[:], ALU.add, ALU.mult).then_inc(l_m, 1)

                def lru_gated():
                    dve.wait_ge(l_mq, l + 1)
                    link(dve.tensor_tensor(lru_i[:], lru_i[:], lru_y[:], ALU.mult))

                def lru_scan():
                    for n in range(LB):
                        last = dve.tensor_tensor_scan(lru_y[:, n, :], lru_x[:, n, 0:T], lru_i[:, n, :], 0.0, ALU.mult, ALU.add)
                    last.then_inc(l_h, 1)

                def lru_mix():
                    dve.wait_ge(gates_done, 3 * l + 1)
                    for u in range(4):
                        b, half = u // 2, u % 2
                        dve.wait_ge(l_ht, 4 * l + u + 1)
                        c0 = half * 4 * LBW
                        dve.tensor_tensor(tok[:, b, RW + DW + c0:RW + DW + c0 + 384], ps[:, 4 + u, 0:384],
                                          proj[:, b, C_LG + c0:C_LG + c0 + 384], ALU.mult).then_inc(mix_lru, 1)

                def rope(q, b, col, n, half, first, done=False):
                    def step():
                        dve.wait_ge(evac_done, g.evacuated(q))
                        dve.wait_ge(rope_ready, 1)
                        v = proj[:, b, col:col + n * 2 * half].rearrange("p (h s e) -> p h s e", s=2, e=half)
                        x1, x2 = v[:, :, 0, :], v[:, :, 1, :]
                        t = [rope_a[:, k, 0:n * half].rearrange("p (h e) -> p h e", e=half) for k in range(4)]
                        cos, sin = (rope_cs[:, k, b, first:first + half].unsqueeze(1).to_broadcast([P, n, half])
                                    for k in range(2))
                        dve.tensor_tensor(t[0], x1, cos, ALU.mult)
                        dve.tensor_tensor(t[1], x2, sin, ALU.mult)
                        dve.tensor_tensor(t[2], x2, cos, ALU.mult)
                        link(dve.tensor_tensor(t[3], x1, sin, ALU.mult))
                        dve.tensor_tensor(x1, t[0], t[1], ALU.subtract)
                        last = dve.tensor_tensor(x2, t[2], t[3], ALU.add)
                        if done:
                            last.then_inc(rope_done, 1)
                        else:
                            link(last)
                    return step

                rope_ret = lambda b, col, done=False: rope(5, b, col, RH, DH // 2, 0, done)
                rope_dif = lambda b, done=False: rope(10, b, C_DQ, 4 * DIFH, DH // 4, 64, done)

                def ret_decay(h):
                    def step():
                        dve.wait_ge(r_s, RH * l + h + 1)
                        if h >= 2:
                            dve.wait_ge(r_o, RH * l + h - 1)
                        dve.tensor_tensor(ra[:, h % 2, :], ps[:, 4 + h % 2, 0:384], decay[:, h, :], ALU.mult).then_inc(r_a, 1)
                    return step

                def squares(col, heads, sums):
                    t = tok[:, :, col:col + heads * DH]
                    sq = sq2[:, :, 0:heads * DH]
                    link(dve.tensor_tensor(sq, t, t, ALU.mult))
                    link(dve.tensor_reduce(sums.rearrange("p (b h) -> p b h", b=TB),
                                           sq.rearrange("p b (h e) -> p b h e", e=DH), AX.X, ALU.add))
                    dve.tensor_scalar(sums, sums, 1.0 / DH, EPS, ALU.mult, ALU.add).then_inc(h_ms, 1)

                def normalise(col, heads, sums, sds):
                    link(dve.reciprocal(sums, sds))
                    for b in range(TB):
                        t = tok[:, b, col:col + heads * DH].rearrange("p (h e) -> p h e", e=DH)
                        last = dve.tensor_tensor(t, t, sums.rearrange("p (b h) -> p b h", b=TB)[:, b].unsqueeze(2)
                                                 .to_broadcast([P, heads, DH]), ALU.mult)
                    link(last)

                def ret_squares():
                    dve.wait_ge(r_ev, RH * (l + 1))
                    dve.wait_ge(rope_done, 2 * l + 2)
                    squares(0, RH, hs_ret)

                def ret_norm():
                    dve.wait_ge(h_sd, 2 * l + 1)
                    normalise(0, RH, hs_ret, hs_ret_sd)

                def ret_mix():
                    dve.wait_ge(gates_done, 3 * l + 2)
                    dve.tensor_tensor(tok[:, :, 0:RW], tok[:, :, 0:RW], proj[:, :, C_RG:C_RG + RW],
                                      ALU.mult).then_inc(mix_ret, 1)

                def d_a(h):
                    dve.wait_ge(d_s, DIFH * l + h + 1)
                    if h >= 2:
                        dve.wait_ge(d_w, DIFH * l + h - 1)
                    for m in range(2):
                        last = dve.scalar_tensor_tensor(ds[:, h % 2, m, :], ps[:, 4 + 2 * (h % 2) + m, 0:384],
                                                        (DH // 2) ** -0.5, causal[:], ALU.mult, ALU.add)
                    last.then_inc(d_m, 1)
                    dve.wait_ge(d_m, DIFH * l + h + 1)
                    for m in range(2):
                        for b, (lo, hi) in enumerate(((0, 128), (128, 384))):
                            last = dve.tensor_reduce(dnegm[:, h % 2, 2 * m + b:2 * m + b + 1], ds[:, h % 2, m, lo:hi],
                                                     AX.X, ALU.max, negate=True)
                    last.then_inc(d_max, 1)

                def d_inverse(h):
                    dve.wait_ge(d_exp, DIFH * l + h + 1)
                    dve.reciprocal(drden[:, h % 2], dden[:, h % 2]).then_inc(d_den, 1)
                    dve.wait_ge(d_den, DIFH * l + h + 1)
                    dve.tensor_scalar(dlr[:, h % 2, 0:2], drden[:, h % 2, 2:4], lam_col, None, ALU.mult)
                    for b, (lo, hi) in enumerate(((0, 128), (128, 384))):
                        last = dve.tensor_scalar(ds[:, h % 2, 0, lo:hi], ds[:, h % 2, 0, lo:hi], drden[:, h % 2, b:b + 1],
                                                 None, ALU.mult)
                    link(last)
                    for b, (lo, hi) in enumerate(((0, 128), (128, 384))):
                        last = dve.tensor_scalar(ds[:, h % 2, 1, lo:hi], ds[:, h % 2, 1, lo:hi], dlr[:, h % 2, b:b + 1],
                                                 None, ALU.mult)
                    link(last)
                    if h:
                        dve.wait_ge(d_pt, DIFH * l + h)
                    dve.tensor_tensor(dw[:], ds[:, h % 2, 0, :], ds[:, h % 2, 1, :], ALU.subtract).then_inc(d_w, 1)

                first_panel(g, last_x, small, T_PRE[l])
                in_panel(1)
                in_panel(2, {6: lru_abs})
                in_panel(3, {1: lru_conv(0), 3: lru_conv(1), 5: lru_conv(2), 7: lru_conv(3)})
                in_panel(4, {1: lru_log_start, 4: lru_log_rest})
                in_panel(5, {3: lru_log_a, 4: lru_input_gate})
                in_panel(6, {1: lru_mult, 5: lru_gated, 6: lru_scan})
                in_panel(7, {4: lru_mix, 6: rope_ret(0, C_RQ)})
                in_panel(8, {0: rope_ret(0, C_RK), 2: rope_ret(1, C_RQ), 4: rope_ret(1, C_RK, True)})
                in_panel(9)
                in_panel(10, {h + 2: ret_decay(h) for h in range(RH)})
                in_panel(11, {3: rope_dif(0), 5: rope_dif(1, True), 6: ret_squares})
                in_panel(12, {0: ret_norm, 2: ret_mix, 4: lambda: d_a(0), 5: lambda: d_a(1),
                              6: lambda: d_inverse(0), 7: lambda: d_a(2)})
                d_inverse(1)
                d_a(3)
                d_inverse(2)
                d_inverse(3)
                dve.wait_ge(d_ev, DIFH * (l + 1))
                squares(RW, DIFH, hs_dif)
                dve.wait_ge(h_sd, 2 * l + 2)
                normalise(RW, DIFH, hs_dif, hs_dif_sd)
                dve.wait_ge(dg_ready, l + 1)
                dve.tensor_tensor(tok[:, :, RW:RW + DW], tok[:, :, RW:RW + DW], proj[:, :, C_DG:C_DG + DW],
                                  ALU.mult).then_inc(mix_dif, 1)
                g = G[f"out{l}"]

                def out_panel(q, j, g=g):
                    dve.wait_ge(evac_done, g.evacuated(q))
                    cols = bass.ds(q * PANEL, PANEL)
                    dve.tensor_tensor(yg[:, :, cols], tok[:, :, cols],
                                      post_g[:, cols].unsqueeze(1).to_broadcast([P, TB, PANEL]), ALU.mult).then_inc(yg_done, 1)

                last_panel = panels(g, out_panel, v=T_OUT[l], late=lambda: dve.wait_ge(pg_in, 16 * (l + 1)))

                def last_x(l=l, last_panel=last_panel):
                    last_panel()
                    dve.wait_ge(y_ssq, 8 * (l + 1))
                    link(dve.tensor_reduce(ssq[:], y_sums[:], AX.X, ALU.add))
                    dve.tensor_scalar(msq[:], ssq[:], 1.0 / D, EPS, ALU.mult, ALU.add).then_inc(y_ms, 1)
                    dve.wait_ge(y_sd, l + 1)
                    link(dve.reciprocal(rstd[:], sdev[:]))
                    dve.wait_ge(yg_done, 4 * (l + 1))
                    for n in range(D // PANEL):
                        cols = slice(n * PANEL, n * PANEL + PANEL)
                        for b in range(TB):
                            last = dve.scalar_tensor_tensor(x[:, b, cols], yg[:, b, cols], rstd[:, b:b + 1],
                                                            x[:, b, cols], ALU.mult, ALU.add)
                        last.then_inc(res_added, 1)
            last_x()


def tables():
    t = np.arange(T)
    c = {"ident": np.eye(P, dtype=np.float32)}
    c["tval"] = np.broadcast_to(t - P, (P, T)).astype(np.float32)
    rows = np.arange(P)[:, None]
    c["parity"] = np.concatenate([(rows // 16) % 2 == np.arange(2), rows // 64 == np.arange(2)], axis=1).astype(np.float32)
    d = t[:, None] - t[None, :]
    keep = [(d >= 0) & (d % dil == 0) & (d <= win) for win, dil in ((128, 1), (512, 4), (2048, 16))]
    far = [np.where(k, d, BIG).astype(np.float32) for k in keep]
    c["dist"] = np.concatenate([f[0:P, 0:P] for f in far] + [f[P:T, :] for f in far], axis=1)
    s = np.exp2(-8.0 * np.arange(1, NG * HEADS + 1) / (NG * HEADS)).reshape(HEADS, NG)
    c["slope"] = np.broadcast_to(-s, (P, HEADS, NG)).astype(np.float32)
    mask = np.where(d >= 0, 0.0, -BIG)
    c["causal"] = np.concatenate([mask[0:P, 0:P], mask[P:T, :]], axis=1).astype(np.float32)
    log_g = np.log1p(-np.exp2(-5.0 - np.arange(RH)))
    full = np.where(d >= 0, np.exp(np.maximum(d, 0)[None] * log_g[:, None, None]), 0.0) * DH ** -0.5
    full = full.transpose(2, 0, 1)
    c["decay"] = np.concatenate([full[0:P], full[P:T, :, P:T]], axis=2).astype(np.float32)
    inv_r = 1.0 / (10000.0 ** np.linspace(0.0, 1.0, DH // 2))
    inv_d = 1.0 / (10000.0 ** (np.arange(0, DH // 2, 2) / (DH // 2)))
    c["inv"] = np.broadcast_to(np.concatenate([inv_r, inv_d]), (P, 96)).astype(np.float32)
    return {k: np.ascontiguousarray(v) for k, v in c.items()}


def kernel(**inputs):
    import concourse.bacc as bacc
    from concourse.bass_utils import run_bass_kernel_spmd

    nc = bacc.Bacc("TRN2", target_bir_lowering=False, num_devices=1)
    arrays, w, c = {}, {}, {}
    for group, source, prefix in ((w, inputs, "in"), (c, tables(), "const")):
        for name, a in source.items():
            a = np.ascontiguousarray(a)
            key = f"{prefix}_{name}"
            arrays[key] = a
            group[name] = nc.dram_tensor(key, a.shape, mybir.dt.from_np(a.dtype), kind="ExternalInput").ap()
    out = nc.dram_tensor("out_x", (1, T, D), F32, kind="ExternalOutput").ap()
    with nc.allow_non_contiguous_dma(reason="a few small parameter vectors and tables go to columns"):
        program(nc, w, c, out)
    r = run_bass_kernel_spmd(nc, [arrays], core_ids=[0])
    return r.results[0]["out_x"]
```
